# Optimizing a Trainium2 kernel written in Bass

```python
import jax, jax.numpy as jnp
from jax import lax
import numpy as np

D_MODEL = 1024
BATCH = 1
SEQ = 256
DEPTH = 1
DEC_BATCH = 8
DEC_SEQ = 16
PAST_LEN = 128

CHUNK = 64
D_RNN = D_MODEL
N_LRU_BLOCKS = 16
LRU_BLOCK = D_RNN // N_LRU_BLOCKS
CONV_WIDTH = 4
LRU_C = 8.0
MLP_CHUNK = 128
N_MLP_GROUPS = 4
MLP_GROUP_DIM = D_MODEL // 8
D_MLP = N_MLP_GROUPS * MLP_GROUP_DIM
SPLITS = (D_RNN, 2 * D_RNN, 2 * D_RNN + D_MLP, 2 * D_RNN + 2 * D_MLP, 2 * D_RNN + 2 * D_MLP + D_MODEL)
N_IN = 2 * D_RNN + 2 * D_MLP + 2 * D_MODEL
N_EXPERTS = 32
TOP_K = 4
D_EXPERT = D_MODEL
SWIGLU_LIMIT = 7.0
SWIGLU_ALPHA = 1.702
MOE_BLOCK = 128
RMS_EPS = 1e-6
LN_EPS = 1e-5

kernel_name = "hawk_gmlp_moe_streaming_step"

def rms_norm(x, g):
    xf = x.astype(jnp.float32)
    y = xf * lax.rsqrt(jnp.mean(xf * xf, axis=-1, keepdims=True) + RMS_EPS)
    return (y * g.astype(jnp.float32)).astype(x.dtype)

def layer_norm(x, g, b):
    xf = x.astype(jnp.float32)
    mu = jnp.mean(xf, axis=-1, keepdims=True)
    xc = xf - mu
    y = xc * lax.rsqrt(jnp.mean(xc * xc, axis=-1, keepdims=True) + LN_EPS)
    return (y * g.astype(jnp.float32) + b.astype(jnp.float32)).astype(x.dtype)

def causal_conv(xb, buf, conv_w, conv_b):
    S = xb.shape[1]
    xp = jnp.concatenate([buf.astype(xb.dtype), xb], axis=1)
    y = conv_b
    for k in range(CONV_WIDTH):
        y = y + xp[:, k:k + S] * conv_w[k]
    return y, xp[:, -(CONV_WIDTH - 1):]

def rg_lru(xc, h0, start, w_rg, b_rg, w_ig, b_ig, lru_lambda):
    B, S, _ = xc.shape
    xblk = xc.reshape(B, S, N_LRU_BLOCKS, LRU_BLOCK)
    r = jax.nn.sigmoid((jnp.einsum('bshi,hij->bshj', xblk, w_rg).reshape(B, S, D_RNN) + b_rg).astype(jnp.float32))
    i = jax.nn.sigmoid((jnp.einsum('bshi,hij->bshj', xblk, w_ig).reshape(B, S, D_RNN) + b_ig).astype(jnp.float32))
    log_a = -LRU_C * r * jax.nn.softplus(-lru_lambda.astype(jnp.float32))
    a = jnp.exp(log_a)
    mult = jnp.sqrt(jnp.maximum(1.0 - jnp.exp(2.0 * log_a), 0.0))
    pos = start + jnp.arange(S)
    mult = jnp.where((pos == 0)[None, :, None], 1.0, mult)
    bterm = mult * i * xc.astype(jnp.float32)
    bterm = bterm.at[:, 0].add(a[:, 0] * h0.astype(jnp.float32))

    def combine(left, right):
        a1, b1 = left
        a2, b2 = right
        return a1 * a2, a2 * b1 + b2

    _, h = lax.associative_scan(combine, (a, bterm), axis=1)
    return h, h[:, -1]

def chunk_spatial_mix(v, w_s, b_s):
    B, S = v.shape[0], v.shape[1]
    n_chunks = -(-S // MLP_CHUNK)
    pad = n_chunks * MLP_CHUNK - S
    vp = jnp.pad(v, ((0, 0), (0, pad), (0, 0), (0, 0)))
    vp = vp.reshape(B, n_chunks, MLP_CHUNK, N_MLP_GROUPS, MLP_GROUP_DIM)
    mask = jnp.tril(jnp.ones((MLP_CHUNK, MLP_CHUNK), dtype=bool))
    ws = jnp.where(mask[None], w_s, 0)
    out = jnp.einsum('gts,bcsgd->bctgd', ws, vp) + b_s.T[None, None, :, :, None]
    return out.reshape(B, n_chunks * MLP_CHUNK, N_MLP_GROUPS, MLP_GROUP_DIM)[:, :S]

def mixer(xn, conv_buf, h0, start, w_in, conv_w, conv_b, w_rg, b_rg, w_ig, b_ig, lru_lambda,
          ln_v_g, ln_v_b, w_s, b_s, w_proj_a, w_proj_b, w_out):
    B, S, _ = xn.shape
    z = xn @ w_in
    xa, ga, u, v, gate_a, gate_b = jnp.split(z, SPLITS, axis=-1)
    xc, new_buf = causal_conv(xa, conv_buf, conv_w, conv_b)
    h, h_last = rg_lru(xc, h0, start, w_rg, b_rg, w_ig, b_ig, lru_lambda)
    ya = (h * jax.nn.gelu(ga.astype(jnp.float32))).astype(xn.dtype) @ w_proj_a
    u = jax.nn.gelu(u)
    v = layer_norm(jax.nn.gelu(v), ln_v_g, ln_v_b)
    vmix = chunk_spatial_mix(v.reshape(B, S, N_MLP_GROUPS, MLP_GROUP_DIM), w_s, b_s).reshape(B, S, D_MLP)
    yb = (u * vmix) @ w_proj_b
    merged = jax.nn.sigmoid(gate_a) * ya + jax.nn.sigmoid(gate_b) * yb
    return merged @ w_out, new_buf, h_last, v

def moe(x2d, w_router, b_router, w_gate_up, b_gate_up, w_down, b_down):
    T, D = x2d.shape
    n_assign = T * TOP_K
    n_blocks = -(-(n_assign + N_EXPERTS * (MOE_BLOCK - 1)) // MOE_BLOCK)
    n_rows = n_blocks * MOE_BLOCK
    logits = (x2d @ w_router + b_router).astype(jnp.float32)
    top_logits, top_idx = lax.top_k(logits, TOP_K)
    gates = jax.nn.softmax(top_logits, axis=-1)
    flat_e = top_idx.reshape(-1).astype(jnp.int32)
    order = jnp.argsort(flat_e)
    sorted_e = flat_e[order]
    counts = jnp.bincount(flat_e, length=N_EXPERTS)
    padded = (counts + MOE_BLOCK - 1) // MOE_BLOCK * MOE_BLOCK
    grp_start = jnp.cumsum(counts) - counts
    pad_end = jnp.cumsum(padded)
    pad_start = pad_end - padded
    dest = pad_start[sorted_e] + jnp.arange(n_assign) - grp_start[sorted_e]
    row_tok = jnp.full((n_rows,), T, jnp.int32).at[dest].set((order // TOP_K).astype(jnp.int32))
    row_gate = jnp.zeros((n_rows,), jnp.float32).at[dest].set(gates.reshape(-1)[order])
    blk_exp = jnp.minimum(jnp.searchsorted(pad_end, jnp.arange(n_blocks) * MOE_BLOCK, side='right'), N_EXPERTS - 1)
    x_pad = jnp.concatenate([x2d, jnp.zeros((1, D), x2d.dtype)], axis=0)

    def expert_block(args):
        tok, e = args
        hb = x_pad[tok]
        gu = (hb @ w_gate_up[e] + b_gate_up[e]).astype(jnp.float32)
        gate, up = gu[:, :D_EXPERT], gu[:, D_EXPERT:]
        gate = jnp.minimum(gate, SWIGLU_LIMIT)
        up = jnp.clip(up, -SWIGLU_LIMIT, SWIGLU_LIMIT)
        act = (up + 1.0) * (gate * jax.nn.sigmoid(SWIGLU_ALPHA * gate))
        return (act.astype(x2d.dtype) @ w_down[e] + b_down[e]).astype(jnp.float32)

    outs = lax.map(expert_block, (row_tok.reshape(n_blocks, MOE_BLOCK), blk_exp))
    y = jnp.zeros((T + 1, D), jnp.float32).at[row_tok].add(outs.reshape(n_rows, D) * row_gate[:, None])
    return y[:T].astype(x2d.dtype)

def layer(x, conv_buf, h0, start, norm1_g, w_in, conv_w, conv_b, w_rg, b_rg, w_ig, b_ig, lru_lambda,
          ln_v_g, ln_v_b, w_s, b_s, w_proj_a, w_proj_b, w_out, norm2_g, w_router, b_router,
          w_gate_up, b_gate_up, w_down, b_down):
    B, S, D = x.shape
    mix, new_buf, h_last, v_rows = mixer(rms_norm(x, norm1_g), conv_buf, h0, start, w_in, conv_w, conv_b,
                                         w_rg, b_rg, w_ig, b_ig, lru_lambda, ln_v_g, ln_v_b, w_s, b_s,
                                         w_proj_a, w_proj_b, w_out)
    x = x + mix
    x = x + moe(rms_norm(x, norm2_g).reshape(B * S, D), w_router, b_router,
                w_gate_up, b_gate_up, w_down, b_down).reshape(B, S, D)
    return x, new_buf, h_last, v_rows

def setup_inputs(seed: int = 0) -> dict:
    key = jax.random.key(seed)
    ks = iter(jax.random.split(key, 40))

    def nrm(shape, scale):
        return jax.random.normal(next(ks), shape, jnp.float32) * scale

    u_a = jax.random.uniform(next(ks), (DEPTH, D_RNN), jnp.float32, minval=0.9, maxval=0.999)
    return {
        "x_prompt": nrm((BATCH, SEQ, D_MODEL), 1.0),
        "x_sample": nrm((DEC_BATCH, DEC_SEQ, D_MODEL), 1.0),
        "state_conv": nrm((DEPTH, DEC_BATCH, CONV_WIDTH - 1, D_RNN), 1.0),
        "state_h": nrm((DEPTH, DEC_BATCH, D_RNN), 0.5),
        "norm1_g": 1.0 + nrm((DEPTH, D_MODEL), 0.02),
        "w_in": nrm((DEPTH, D_MODEL, N_IN), D_MODEL ** -0.5),
        "conv_w": nrm((DEPTH, CONV_WIDTH, D_RNN), CONV_WIDTH ** -0.5),
        "conv_b": nrm((DEPTH, D_RNN), 0.01),
        "w_rg": nrm((DEPTH, N_LRU_BLOCKS, LRU_BLOCK, LRU_BLOCK), LRU_BLOCK ** -0.5),
        "b_rg": nrm((DEPTH, D_RNN), 0.01),
        "w_ig": nrm((DEPTH, N_LRU_BLOCKS, LRU_BLOCK, LRU_BLOCK), LRU_BLOCK ** -0.5),
        "b_ig": nrm((DEPTH, D_RNN), 0.01),
        "lru_lambda": jnp.log(u_a) - jnp.log1p(-u_a),
        "ln_v_g": 1.0 + nrm((DEPTH, D_MLP), 0.02),
        "ln_v_b": nrm((DEPTH, D_MLP), 0.01),
        "w_s": nrm((DEPTH, N_MLP_GROUPS, MLP_CHUNK, MLP_CHUNK), MLP_CHUNK ** -0.5),
        "b_s": 1.0 + nrm((DEPTH, N_MLP_GROUPS, MLP_CHUNK), 0.1),
        "w_proj_a": nrm((DEPTH, D_RNN, D_MODEL), D_RNN ** -0.5),
        "w_proj_b": nrm((DEPTH, D_MLP, D_MODEL), D_MLP ** -0.5),
        "w_out": nrm((DEPTH, D_MODEL, D_MODEL), D_MODEL ** -0.5),
        "norm2_g": 1.0 + nrm((DEPTH, D_MODEL), 0.02),
        "w_router": nrm((DEPTH, D_MODEL, N_EXPERTS), D_MODEL ** -0.5),
        "b_router": nrm((DEPTH, N_EXPERTS), 0.01),
        "w_gate_up": nrm((DEPTH, N_EXPERTS, D_MODEL, 2 * D_EXPERT), D_MODEL ** -0.5),
        "b_gate_up": nrm((DEPTH, N_EXPERTS, 2 * D_EXPERT), 0.01),
        "w_down": nrm((DEPTH, N_EXPERTS, D_EXPERT, D_MODEL), D_EXPERT ** -0.5),
        "b_down": nrm((DEPTH, N_EXPERTS, D_MODEL), 0.01),
        "final_norm_g": 1.0 + nrm((D_MODEL,), 0.02),
    }

def reference(x_prompt, x_sample, state_conv, state_h, norm1_g, w_in, conv_w, conv_b, w_rg, b_rg,
              w_ig, b_ig, lru_lambda, ln_v_g, ln_v_b, w_s, b_s, w_proj_a, w_proj_b, w_out, norm2_g,
              w_router, b_router, w_gate_up, b_gate_up, w_down, b_down, final_norm_g):
    yp, ys = x_prompt, x_sample
    conv_p, h_p, conv_s, h_s, v_s = [], [], [], [], []
    for l in range(DEPTH):
        lp = (norm1_g[l], w_in[l], conv_w[l], conv_b[l], w_rg[l], b_rg[l], w_ig[l], b_ig[l], lru_lambda[l],
              ln_v_g[l], ln_v_b[l], w_s[l], b_s[l], w_proj_a[l], w_proj_b[l], w_out[l], norm2_g[l],
              w_router[l], b_router[l], w_gate_up[l], b_gate_up[l], w_down[l], b_down[l])
        nb = yp.shape[0]
        yp, buf_p, hl_p, _ = layer(yp, jnp.zeros((nb, CONV_WIDTH - 1, D_RNN), yp.dtype),
                                   jnp.zeros((nb, D_RNN), jnp.float32), 0, *lp)
        conv_p.append(buf_p)
        h_p.append(hl_p)
        ys, buf_s, hl_s, v_rows = layer(ys, state_conv[l], state_h[l], PAST_LEN, *lp)
        conv_s.append(buf_s)
        h_s.append(hl_s)
        v_s.append(v_rows)
    y_prompt = rms_norm(yp, final_norm_g)
    y_sample = rms_norm(ys, final_norm_g)
    return (y_prompt, y_sample, jnp.stack(conv_p), jnp.stack(h_p), jnp.stack(conv_s), jnp.stack(h_s), jnp.stack(v_s))


_drawn_inputs = setup_inputs


def setup_inputs(seed=0):
    import zlib

    import numpy as np

    out = dict(_drawn_inputs(seed))
    spreads = {}
    factors = {'b_rg': 23.801,
     'b_ig': 15.854,
     'ln_v_g': 2.831,
     'ln_v_b': 4.607,
     'b_gate_up': 8.0,
     'b_down': 8.0,
     'final_norm_g': 9.685}
    for name, (base, spread) in spreads.items():
        noise = np.random.default_rng([zlib.crc32(name.encode()), seed]).standard_normal(out[name].shape)
        drawn = base * np.exp(spread * noise) if base else spread * noise
        out[name] = __import__('jax').numpy.asarray(drawn.astype(out[name].dtype))
    for name, factor in factors.items():
        out[name] = (out[name] * factor).astype(out[name].dtype)
    return out
```

```python
from contextlib import ExitStack

import concourse.bass as bass
from concourse import mybir

ALU = mybir.AluOpType
ACT = mybir.ActivationFunctionType
F32 = mybir.dt.float32
F32R = mybir.dt.float32r
BF16 = mybir.dt.bfloat16
I32 = mybir.dt.int32
U32 = mybir.dt.uint32
AX_X = mybir.AxisListType.X

P = 128
D = 1024
CB = D // P
SEQ = 256
ST, SF = 8, 16
T = SEQ + ST * SF
TT = T // P
CW = 4
PADP = CW - 1 + SEQ
PADS = CW - 1 + SF
DM = 512
MG = DM // P
NE = 32
TOPK = 4
LIMIT, ALPHA = 7.0, 1.702
RMS_EPS, LN_EPS = 1e-6, 1e-5

KB = 4
UC = 512
MIX_RING = 2
RAW_RING = 6
SPLIT_RING = 3
Z_CHUNKS = [0, 1, 2, 3, 4, 6, 7, 8, 9, 5]
NZ = len(Z_CHUNKS) - 1
V_U = 2 * NZ
PB_U = V_U + 2
PA_U = PB_U + 2
WO_U = PA_U + 4
MIX_U = WO_U + 4
EXP_U = 12
FAR = 1000.0

G1_R, CBIAS_R, BRG_R, BIG_R, LAM_R, CONVW_R = 0, 8, 16, 24, 32, 40
ROWS = CONVW_R + CW * CB


def hawk_gmlp_moe_streaming_step(
    nc, x_prompt, x_sample, state_conv, state_h, norm1_g, w_in, conv_w, conv_b, w_rg, b_rg, w_ig, b_ig,
    lru_lambda, ln_v_g, ln_v_b, w_s, b_s, w_proj_a, w_proj_b, w_out, norm2_g, w_router, b_router,
    w_gate_up, b_gate_up, w_down, b_down, final_norm_g,
    y_prompt, y_sample, new_conv_prompt, new_h_prompt, new_conv_sample, new_h_sample, new_v_sample,
):
    base = (nc.sbuf_base + 31) // 32 * 32
    with ExitStack() as ctx:
        def at(name, offset, shape, dt=F32):
            return nc.alloc_sbuf_tensor_at(name, shape, dt, offset=base + offset)

        def sem(name):
            return ctx.enter_context(nc.semaphore(name))

        split_h = at("split_h", 0, [P, SPLIT_RING, KB, UC], F32R)
        split_l = at("split_l", 24576, [P, SPLIT_RING, KB, UC], F32R)
        raw = at("raw", 49152, [P, RAW_RING, KB, UC])
        x_in = at("x_in", 65536, [P, TT, D])
        lru_r = at("lru_r", 65536, [P, CB // 2, T])
        lru_i = at("lru_i", 71680, [P, CB // 2, T])
        lru_a = at("lru_a", 77824, [P, CB // 2, T])
        wst = at("wst", 83968, [P, 2, MG, P])
        lng = at("lng", 88064, [P, DM])
        lnb = at("lnb", 90112, [P, DM])
        bsb = at("bsb", 92160, [P, MG, P])
        tmp = at("tmp", 94208, [P, CB // 2, T])
        state_out = at("state_out", 94208, [36, D])
        act_h = at("act_h", 102400, [P, CB, T], F32R)
        act_l = at("act_l", 114688, [P, CB, T], F32R)
        xn_h = at("xn_h", 102400, [P, TT, D], F32R)
        xn_l = at("xn_l", 114688, [P, TT, D], F32R)
        ga = at("ga", 126976, [P, CB, T])
        mrg_h = at("mrg_h", 126976, [P, CB, T], F32R)
        xc = at("xc", 139264, [P, CB, T])
        mrg_l = at("mrg_l", 139264, [P, CB, T], F32R)
        at_h = at("at_h", 126976, [P, CB, P], F32R)
        at_l = at("at_l", 131072, [P, CB, P], F32R)
        out_h = at("out_h", 135168, [P, D], F32R)
        out_l = at("out_l", 139264, [P, D], F32R)
        xt_h = at("xt_h", 143360, [P, CB, P], F32R)
        xt_l = at("xt_l", 147456, [P, CB, P], F32R)
        gate_a = at("gate_a", 151552, [P, CB, T])
        xs = at("xs", 151552, [P, TT, D])
        bias_hl = at("bias_hl", 151552, [2 * NE, 2 * D], F32R)
        actv = at("actv", 159744, [P, D])
        bdn = at("bdn", 159744, [NE, D])
        gate_b = at("gate_b", 163840, [P, CB, T])
        ws_raw = at("ws_raw", 163840, [P, 2, MG, P])
        state_in = at("state_in", 172032, [32, D])
        g1 = at("g1", 163840, [P, UC])
        u1 = at("u1", 165888, [P, UC])
        sil = at("sil", 167936, [P, UC])
        pick = at("pick", 169984, [P, TT, P], F32R)
        pick_t = at("pick_t", 171520, [P, T], F32R)
        wr = at("wr", 173056, [P, CB, NE])
        sel = at("sel", 174080, [2 * NE, P], F32R)
        post = at("post", 174592, [NE, T], F32R)
        xpad = at("xpad", 176128, [P, CB, PADP + ST * PADS])
        yb_h = at("yb_h", 176128, [P, MG, T], F32R)
        yb_l = at("yb_l", 182272, [P, MG, T], F32R)
        bias_raw = at("bias_raw", 176128, [2 * NE, 2 * D])
        xnt = at("xnt", 176128, [P, CB, T])
        u = at("u", 189440, [P, MG, T])
        v = at("v", 195584, [P, TT, DM])
        y = at("y", 189440, [P, TT, D])
        lruw = at("lruw", 201728, [P, 2, CB, P])
        n2b = at("n2b", 201728, [P, D])
        fnb = at("fnb", 205824, [P, D])
        rows = at("rows", 209920, [ROWS, P])
        ident = at("ident", 210432, [P, P])
        iota_s = at("iota_s", 209920, [P, P])
        cols = at("cols", 210944, [P, ROWS])
        tri = at("tri", 211232, [P, P], BF16)
        small = at("small", 211488, [P, 320])
        pos = at("pos", 100352, [P, TT, NE])
        gat = at("gat", 100736, [P, TT, NE])
        h0 = small[:, 0:64].rearrange("p (c b) -> p c b", b=ST)
        st8 = small[:, 64:128]
        pack = at("pack", 100352, [P, CB, 36])
        ones_b = at("ones_b", 101504, [P, P], BF16)
        onehot = at("onehot", 101760, [2 * NE, NE])
        cnt_i = at("cnt_i", 101888, [1, 1], I32)
        slot_p = at("slot_p", 101920, [P, 1])
        pos_e = at("pos_e", 102112, [P, TT])
        gslot = at("gslot", 101952, [P, 1])
        brb = at("brb", 101984, [P, NE])
        lg = at("lg", 126976, [P, TT, NE])
        mx = at("mx", 127360, [P, TT, 8])
        ix = at("ix", 127456, [P, TT, 8], U32)
        ixf = at("ixf", 127552, [P, TT, 8])
        ex = at("ex", 127648, [P, TT, 8])
        oh = at("oh", 127744, [P, TT, TOPK, NE])
        mask = at("mask", 129280, [P, TT, NE], BF16)
        maskf = at("maskf", 129472, [P, TT, NE])
        gat_t = at("gat_t", 129856, [NE, T])
        cnt = at("cnt", 131392, [1, 8])
        xn2 = at("xn2", 139264, [P, TT, D])
        squares = at("squares", 184320, [P, D])
        squares3 = at("squares3", 143360, [P, D])
        lam8 = small[:, 128:152]
        bn = small[:, 152:170].rearrange("p (t k) -> p t k", k=6)
        bnm = small[:, 170:176].rearrange("p (t k) -> p t k", k=2)
        rt = small[:, 192:256]
        ps = ctx.enter_context(nc.psum_tensor("ps", [P, 8, 512], F32))

        x_loaded, rows_loaded = sem("x_loaded"), sem("rows_loaded")
        lruw_loaded, ws_loaded, ln_loaded = sem("lruw_loaded"), sem("ws_loaded"), sem("ln_loaded")
        late_loaded, y_loaded, bias_loaded = sem("late_loaded"), sem("y_loaded"), sem("bias_loaded")
        mix_landed = [sem(f"mix_landed{i}") for i in range(MIX_RING)]
        exp_landed = [sem(f"exp_landed{i}") for i in range(RAW_RING)]
        high_done, low_done, unit_used = sem("high_done"), sem("low_done"), sem("unit_used")
        const_ready, pool_step, dve_step, act_step = sem("const_ready"), sem("pool_step"), sem("dve_step"), sem("act_step")
        zeroed = sem("zeroed")
        squared, rstd_in, rstd_out, xs_ready = sem("squared"), sem("rstd_in"), sem("rstd_out"), sem("xs_ready")
        rows_turned, rows_copied, xs_turned, xn_high, xn_ready = (
            sem("rows_turned"), sem("rows_copied"), sem("xs_turned"), sem("xn_high"), sem("xn_ready"))
        lam_in, lam_exp, lam_ln_in, lam_ln, lam_ready = (
            sem("lam_in"), sem("lam_exp"), sem("lam_ln_in"), sem("lam_ln"), sem("lam_ready"))
        z_ready, z_evac, conv_done = sem("z_ready"), sem("z_evac"), sem("conv_done")
        gates_mm, gates_read, decay_ready, mult_in, mult_ready, lru_ready, scanned = (
            sem("gates_mm"), sem("gates_read"), sem("decay_ready"), sem("mult_in"), sem("mult_ready"),
            sem("lru_ready"), sem("scanned"))
        v_mm, v_read, ln_in, ln_out, v_ready = sem("v_mm"), sem("v_read"), sem("ln_in"), sem("ln_out"), sem("v_ready")
        ws_turned, ws_ready, vmix_mm, yb_ready = sem("ws_turned"), sem("ws_ready"), sem("vmix_mm"), sem("yb_ready")
        pb_mm, pb_read, pa_mm, mrg_ready, wo_mm, y_ready = (
            sem("pb_mm"), sem("pb_read"), sem("pa_mm"), sem("mrg_ready"), sem("wo_mm"), sem("y_ready"))
        st_packed, st_turned, st_ready = sem("st_packed"), sem("st_turned"), sem("st_ready")
        sq2, r2_in, r2_out, xn2_ready, xn2_turned, xnt_ready, xn2_high = (
            sem("sq2"), sem("r2_in"), sem("r2_out"), sem("xn2_ready"), sem("xn2_turned"), sem("xnt_ready"),
            sem("xn2_high"))
        logits_mm, top_ready, top_exp, mask_ready, pos_mm, pos_ready, post_mm, route_ready = (
            sem("logits_mm"), sem("top_ready"), sem("top_exp"), sem("mask_ready"), sem("pos_mm"),
            sem("pos_ready"), sem("post_mm"), sem("route_ready"))
        gat_mm, gat_ready, bd_mm = sem("gat_mm"), sem("gat_ready"), sem("bd_mm")
        ranks_ready, column_ready = sem("ranks_ready"), sem("column_ready")
        ranks_seen, column_seen = sem("ranks_seen"), sem("column_seen")
        pick_ready, pick_used, sel_ready, sel_used = (
            sem("pick_ready"), sem("pick_used"), sem("sel_ready"), sem("sel_used"))
        gathered, xt_ready, out_high, out_ready, pick_t_ready, combined, y_added = (
            sem("gathered"), sem("xt_ready"), sem("out_high"), sem("out_ready"), sem("pick_t_ready"),
            sem("combined"), sem("y_added"))
        clipped, silu_done, act_ready, act_turned, at_high, at_ready, gslot_ready = (
            sem("clipped"), sem("silu_done"), sem("act_ready"), sem("act_turned"), sem("at_high"),
            sem("at_ready"), sem("gslot_ready"))
        xn2_low, r3_mean = sem("xn2_low"), sem("r3_mean")
        sq3, r3_in, r3_out, out_final, stored = sem("sq3"), sem("r3_in"), sem("r3_out"), sem("out_final"), sem("stored")

        def halves(w):
            return w.rearrange("o (h j p) n -> (o h) p j n", j=KB, p=P)

        win, wpa, wpb, wout = halves(w_in), halves(w_proj_a), halves(w_proj_b), halves(w_out)
        wgu = w_gate_up.rearrange("o e (h j p) n -> (o e) h p j n", j=KB, p=P)
        wdn = w_down.rearrange("o e (h j p) n -> (o e) h p j n", j=KB, p=P)

        def mix_unit(n):
            if n < PB_U:
                c = Z_CHUNKS[n // 2]
                return win[n % 2][:, :, c * UC:(c + 1) * UC]
            if n < PA_U:
                c = n - PB_U
                return wpb[0][:, :, c * UC:(c + 1) * UC]
            w, m = (wpa, n - PA_U) if n < WO_U else (wout, n - WO_U)
            return w[m % 2][:, :, m // 2 * UC:(m // 2 + 1) * UC]

        def exp_unit(e, m):
            if m < 8:
                c = (0, 2, 1, 3)[m // 2]
                w, half = wgu, m % 2
            else:
                c, half, w = m % 2, (m - 8) // 2, wdn
            return w[bass.ds(e, 1), half, :, :, c * UC:(c + 1) * UC].rearrange("o p j n -> (o p) j n")

        def wait_part(eng, ready, parts, k, i, unit):
            if i < parts - 1:
                eng.wait_ge(ready, (parts - 1) * k + i + 1)
            else:
                eng.wait_ge(unit_used, unit + 1)

        samp_pad = xpad[:, :, PADP:].rearrange("p c (b j) -> p c b j", j=PADS)
        block = ctx.enter_context(nc.Block())

        @block.sync
        def _(sp):
            sp.dma_start(x_in[:, 0:2, :], x_prompt.rearrange("o (t p) d -> p (o t) d", p=P)).then_inc(x_loaded, 16)
            sp.dma_start(x_in[:, 2, :], x_sample.rearrange("b s d -> (b s) d")).then_inc(x_loaded, 16)
            for r, a in ((G1_R, norm1_g), (CBIAS_R, conv_b), (BRG_R, b_rg), (BIG_R, b_ig), (LAM_R, lru_lambda)):
                sp.dma_start(rows[r:r + CB, :], a.rearrange("o (c p) -> (o c) p", p=P)).then_inc(rows_loaded, 16)
            sp.dma_start(rows[CONVW_R:ROWS, :], conv_w.rearrange("o k (c p) -> (o k c) p", p=P)).then_inc(rows_loaded, 16)
            sp.dma_start(state_in[0:24, :], state_conv.rearrange("o b k d -> (o b k) d")).then_inc(rows_loaded, 16)
            sp.dma_start(state_in[24:32, :], state_h.rearrange("o b d -> (o b) d")).then_inc(rows_loaded, 16)
            for n in range(MIX_U):
                if n >= MIX_RING:
                    sp.wait_ge(low_done, n - MIX_RING + 1)
                sp.dma_start(raw[:, n % MIX_RING], mix_unit(n)).then_inc(mix_landed[n % MIX_RING], 16)
                if n == PA_U:
                    sp.wait_ge(v_ready, 1)
                    sp.dma_start(new_v_sample.rearrange("o b s d -> (o b s) d"), v[:, 2, :]).then_inc(stored, 16)
            sp.wait_ge(st_ready, 1)
            sp.dma_start(new_conv_prompt.rearrange("o b k d -> (o b k) d"), state_out[0:3, :]).then_inc(stored, 16)
            sp.dma_start(new_conv_sample.rearrange("o b k d -> (o b k) d"), state_out[3:27, :]).then_inc(stored, 16)
            sp.dma_start(new_h_prompt.rearrange("o b d -> (o b) d"), state_out[27:28, :]).then_inc(stored, 16)
            sp.dma_start(new_h_sample.rearrange("o b d -> (o b) d"), state_out[28:36, :]).then_inc(stored, 16)
            sp.wait_ge(yb_ready, MG)
            sp.wait_ge(stored, 5 * 16)
            sp.dma_start(y[:, 0:2, :], x_prompt.rearrange("o (t p) d -> p (o t) d", p=P)).then_inc(y_loaded, 16)
            sp.dma_start(y[:, 2, :], x_sample.rearrange("b s d -> (b s) d")).then_inc(y_loaded, 16)
            sp.wait_ge(low_done, MIX_U)

            def expert(it, e):
                for m in range(EXP_U):
                    sp.wait_ge(low_done, it * EXP_U + (MIX_U + m - RAW_RING + 1))
                    sp.dma_start(raw[:, m % RAW_RING], exp_unit(e, m)).then_inc(exp_landed[m % RAW_RING], 16)

            with sp.Fori(0, NE) as e:
                expert(e, e)
            sp.wait_ge(route_ready, 1)
            rounds = sp.value_load(cnt_i[0:1, 0:1], min_val=1, max_val=TT)
            with sp.Fori(1, TT) as r:
                with sp.If(r < rounds):
                    with sp.Fori(0, NE) as e:
                        expert(r * NE + e, e)
                sp.nop()
            sp.wait_ge(out_final, TT)
            sp.dma_start(y_prompt.rearrange("o (t p) d -> p (o t) d", p=P), y[:, 0:2, :]).then_inc(stored, 16)
            sp.dma_start(y_sample.rearrange("b s d -> (b s) d"), y[:, 2, :]).then_inc(stored, 16)
            sp.wait_ge(stored, 7 * 16)

        @block.gpsimd
        def _(pool):
            step = [0]

            def link(ins):
                step[0] += 1
                ins.then_inc(pool_step, 1)
                pool.wait_ge(pool_step, step[0])

            link(pool.memset(ident[:], 0.0))
            pool.affine_select(out=ident[:], in_=ident[:], compare_op=ALU.not_equal, fill=1.0, base=0,
                               pattern=[[-1, P]], channel_multiplier=1).then_inc(const_ready, 1)
            pool.memset(lruw[:], 0.0).then_inc(zeroed, 1)
            pool.memset(ws_raw[:, 1], 0.0).then_inc(zeroed, 1)
            pool.memset(xpad[:, :, 0:CW - 1], 0.0).then_inc(const_ready, 1)
            pool.wait_ge(zeroed, 2)
            pool.dma_start(ws_raw[:, 0], w_s.rearrange("o g t s -> t (o g) s")).then_inc(ws_loaded, 16)
            for b in range(ST):
                pool.dma_start(ws_raw[b * SF:(b + 1) * SF, 1, :, b * SF:(b + 1) * SF],
                               w_s[:, :, 0:SF, 0:SF].rearrange("o g t s -> t (o g) s")).then_inc(ws_loaded, 16)
            for k, w in enumerate((w_rg, w_ig)):
                for q in range(2):
                    pool.dma_start(lruw[64 * q:64 * q + 64, k, :, 64 * q:64 * q + 64],
                                   w.rearrange("o (c q) i j -> q i (o c) j", q=2)[q]).then_inc(lruw_loaded, 16)
            pool.dma_start(lng[:], ln_v_g.broadcast_to([P, DM])).then_inc(ln_loaded, 16)
            pool.dma_start(lnb[:], ln_v_b.broadcast_to([P, DM])).then_inc(ln_loaded, 16)
            pool.dma_start(bsb[:], b_s.broadcast_to([P, MG, P])).then_inc(ln_loaded, 16)
            link(pool.memset(tri[:], 1.0))
            link(pool.affine_select(out=tri[:], in_=tri[:], compare_op=ALU.is_gt, fill=0.0, base=0,
                                    pattern=[[1, P]], channel_multiplier=-1))
            link(pool.memset(ones_b[:], 1.0))
            for k in range(2):
                pool.wait_ge(ws_ready, k + 1)
                pool.affine_select(out=wst[:, k], in_=wst[:, k], compare_op=ALU.is_ge, fill=0.0, base=0,
                                   pattern=[[0, MG], [1, P]], channel_multiplier=-1).then_inc(const_ready, 1)
            pool.wait_ge(rows_copied, 1)
            link(pool.iota(iota_s[:], pattern=[[1, P]], base=0, channel_multiplier=0, allow_small_or_imprecise_dtypes=True))
            link(pool.iota(slot_p[:], pattern=[[0, 1]], base=0, channel_multiplier=1, allow_small_or_imprecise_dtypes=True))
            link(pool.memset(onehot[:], 0.0))
            link(pool.affine_select(out=onehot[:], in_=onehot[:], compare_op=ALU.not_equal, fill=1.0, base=0,
                                    pattern=[[-1, NE]], channel_multiplier=1))
            pool.affine_select(out=onehot[:], in_=onehot[:], compare_op=ALU.not_equal, fill=1.0, base=-NE,
                               pattern=[[-1, NE]], channel_multiplier=1).then_inc(const_ready, 1)
            pool.dma_start(brb[:], b_router.broadcast_to([P, NE])).then_inc(late_loaded, 16)
            pool.wait_ge(gates_mm, 4)
            pool.dma_start(n2b[:], norm2_g.broadcast_to([P, D])).then_inc(late_loaded, 16)
            pool.dma_start(fnb[:], final_norm_g.rearrange("(o d) -> o d", o=1).broadcast_to([P, D])).then_inc(late_loaded, 16)
            pool.wait_ge(unit_used, PA_U)
            for k in range(2):
                pool.dma_start(bias_raw[k * NE:(k + 1) * NE, :], b_gate_up.rearrange("o e n -> (o e) n")).then_inc(bias_loaded, 16)
            pool.wait_ge(mrg_ready, CB)
            pool.dma_start(wr[:], w_router.rearrange("o (c p) e -> p (o c) e", p=P)).then_inc(late_loaded, 16)
            pool.dma_start(bdn[:], b_down.rearrange("o e n -> (o e) n")).then_inc(late_loaded, 16)

            pool.wait_ge(route_ready, 1)
            pool.wait_ge(const_ready, 5)

            def next_ranks(r):
                pool.wait_ge(sel_used, r * NE + 1)
                pool.sem_inc(ranks_seen, 1)
                pool.tensor_scalar(pos[:], pos[:], -float(P), None, ALU.add)
                pool.tensor_scalar(post[:], post[:].bitcast(F32), -float(P), None, ALU.add).then_inc(ranks_ready, 1)
                pool.wait_ge(ranks_ready, r + 1)
                pool.sem_inc(ranks_seen, 1)

            def expert(it, e):
                pool.wait_ge(pick_used, it + 1)
                pool.tensor_copy(pos_e[:], pos[:, :, bass.ds(e, 1)].rearrange("p t o -> p (t o)")).then_inc(column_ready, 1)
                pool.wait_ge(column_ready, it + 1)
                pool.sem_inc(column_seen, 1)
                for t in range(TT):
                    i_ = pool.tensor_scalar(pick[:, t, :], iota_s[:], pos_e[:, t:t + 1], None, ALU.is_equal)
                i_.then_inc(pick_ready, 1)
                pool.wait_ge(sel_used, it + 1)
                pool.tensor_copy(sel[:], onehot[:, bass.ds(e, 1)].broadcast_to([2 * NE, P])).then_inc(sel_ready, 1)

            next_ranks(0)
            with pool.Fori(0, NE) as e:
                expert(e, e)
            rounds = pool.value_load(cnt_i[0:1, 0:1], min_val=1, max_val=TT)
            with pool.Fori(1, TT) as r:
                with pool.If(r < rounds):
                    next_ranks(r)
                    with pool.Fori(0, NE) as e:
                        expert(r * NE + e, e)
                pool.nop()

        @block.scalar
        def _(act):
            def high(n):
                act.wait_ge(mix_landed[n % MIX_RING], 16 * (n // MIX_RING + 1))
                if n >= SPLIT_RING:
                    act.wait_ge(unit_used, n - SPLIT_RING + 1)
                act.activation(split_h[:, n % SPLIT_RING], raw[:, n % MIX_RING], ACT.Copy).then_inc(high_done, 1)

            act.wait_ge(x_loaded, 32)
            for t in range(TT):
                act.activation(xs[:, t, :], x_in[:, t, :], ACT.Square, accum_out=st8[:, t:t + 1]).then_inc(squared, 1)
            act.wait_ge(rstd_in, 1)
            act.activation(st8[:, 8:8 + TT], st8[:, 4:4 + TT], ACT.Sqrt).then_inc(rstd_out, 1)
            high(0)
            high(1)
            act.wait_ge(lam_in, 1)
            act.activation(st8[:, 24:32], st8[:, 16:24], ACT.Exp).then_inc(lam_exp, 1)
            act.wait_ge(lam_ln_in, 1)
            act.activation(st8[:, 40:48], st8[:, 32:40], ACT.Ln).then_inc(lam_ln, 1)
            act.wait_ge(rows_copied, 1)
            for c in range(CB):
                act.wait_ge(xs_turned, c + 1)
                act.activation(act_h[:, c, :], ps[:, c, 0:T], ACT.Identity, scale=cols[:, G1_R + c:G1_R + c + 1]).then_inc(xn_high, 1)
            high(2)

            def evacuate(c):
                for b in range(4):
                    wait_part(act, z_ready, 4, c, b, 2 * c + 1)
                    src = ps[:, 4 * (c % 3 % 2) + b, 0:T]
                    if c < 2:
                        act.activation(xpad[:, 4 * c + b, CW - 1:PADP], src[:, 0:SEQ], ACT.Identity)
                        act.activation(samp_pad[:, 4 * c + b, :, CW - 1:],
                                       src[:, SEQ:T].rearrange("p (b s) -> p b s", s=SF), ACT.Identity).then_inc(z_evac, 1)
                        continue
                    dst, func = {2: (ga[:, b], 0), 3: (ga[:, 4 + b], 0), 4: (u[:, b], 0), 5: (gate_a[:, b], 1),
                                 6: (gate_a[:, 4 + b], 1), 7: (gate_b[:, b], 1), 8: (gate_b[:, 4 + b], 1)}[c]
                    act.activation(dst, src, ACT.Sigmoid if func else ACT.Gelu_apprx_tanh).then_inc(z_evac, 1)

            for c in range(NZ):
                high(2 * c + 3)
                evacuate(c)
                high(2 * c + 4)

            def sigmoids(hf):
                for k, (dst, r) in enumerate(((lru_r, BRG_R), (lru_i, BIG_R))):
                    act.wait_ge(gates_mm, 2 * hf + k + 1)
                    for b in range(4):
                        bank = (4 * (k if hf == 0 else 1 - k)) + b
                        col = r + 4 * hf + b
                        if k == 0 and hf == 1 and b == 0:
                            act.wait_ge(st_packed, 1)
                        i_ = act.activation(dst[:, b], ps[:, bank, 0:T], ACT.Sigmoid, bias=cols[:, col:col + 1])
                    i_.then_inc(gates_read, 1)

            def decays(hf):
                act.wait_ge(lam_ready, 1)
                act.wait_ge(gates_read, 2 * hf + 1)
                for b in range(4):
                    act.activation(lru_a[:, b], lru_r[:, b], ACT.Exp, scale=st8[:, 48 + 4 * hf + b:49 + 4 * hf + b])
                for b in range(4):
                    i_ = act.activation(lru_r[:, b], lru_r[:, b], ACT.Tanh, scale=st8[:, 56 + 4 * hf + b:57 + 4 * hf + b])
                i_.then_inc(decay_ready, 1)

            def roots(hf):
                act.wait_ge(mult_in, hf + 1)
                act.activation(lru_r[:], lru_r[:], ACT.Sqrt).then_inc(mult_ready, 1)

            sigmoids(0)
            decays(0)
            roots(0)
            high(V_U + 3)
            for t in range(TT):
                wait_part(act, v_mm, TT, 0, t, V_U + 1)
                act.activation(v[:, t, :], ps[:, t, :], ACT.Gelu_apprx_tanh).then_inc(v_read, 1)
            high(V_U + 4)
            act.wait_ge(ln_in, 1)
            act.activation(st8[:, 12:15], st8[:, 8:11], ACT.Sqrt).then_inc(ln_out, 1)
            sigmoids(1)
            decays(1)
            roots(1)
            for n in range(V_U + 5, MIX_U):
                high(n)

            for t in range(TT):
                act.wait_ge(y_ready, TT + t + 1)
                if t:
                    act.wait_ge(sq2, t)
                act.activation(squares[:], y[:, t, :], ACT.Square, accum_out=rt[:, t:t + 1]).then_inc(sq2, 1)
            act.wait_ge(r2_in, 1)
            act.activation(rt[:, 8:8 + TT], rt[:, 4:4 + TT], ACT.Sqrt).then_inc(r2_out, 1)
            for t in range(TT):
                act.wait_ge(xn2_ready, t + 1)
                act.activation(xn_h[:, t, :], xn2[:, t, :], ACT.Copy).then_inc(xn2_high, 1)
            for t in range(TT):
                for half in range(2):
                    act.wait_ge(xn2_turned, 2 * t + half + 1)
                    act.activation(xnt[:, 4 * half:4 * half + 4, t * P:(t + 1) * P],
                                   ps[:, 2 * t + half, :].rearrange("p (c t) -> p c t", t=P), ACT.Copy).then_inc(xnt_ready, 1)
            act.wait_ge(top_ready, 1)
            for t in range(TT):
                i_ = act.activation(ex[:, t, 0:TOPK], mx[:, t, 0:TOPK], ACT.Exp, bias=rt[:, 16 + t:17 + t], accum_out=rt[:, 20 + t:21 + t])
            i_.then_inc(top_exp, 1)
            act.wait_ge(route_ready, 1)
            act.wait_ge(sel_used, 1)
            act.activation(gslot[:], slot_p[:], ACT.Copy, scale=0.0).then_inc(gslot_ready, 1)

            def out_high_part(it):
                act.wait_ge(unit_used, it * EXP_U + MIX_U)
                act.wait_ge(gslot_ready, it + 1)
                act.activation(out_h[:], ps[:, 4:6, :].rearrange("p a b -> p (a b)"), ACT.Copy, scale=gslot[:, 0:1]).then_inc(out_high, 1)

            def expert(it):
                def high(m):
                    act.wait_ge(exp_landed[m % RAW_RING], it * (16 * EXP_U // RAW_RING) + 16 * (m // RAW_RING + 1))
                    act.wait_ge(unit_used, it * EXP_U + (MIX_U + m - SPLIT_RING + 1))
                    act.activation(split_h[:, m % SPLIT_RING], raw[:, m % RAW_RING], ACT.Copy).then_inc(high_done, 1)

                def silu(j):
                    act.wait_ge(clipped, it * 2 + (j + 1))
                    act.activation(sil[:], g1[:], ACT.Silu, scale=ALPHA).then_inc(silu_done, 1)

                def turned_high(j):
                    act.wait_ge(act_turned, it * 2 + (j + 1))
                    act.activation(at_h[:, 4 * j:4 * j + 4, :].rearrange("p c s -> p (c s)"), ps[:, 6 + j, :], ACT.Copy).then_inc(at_high, 1)

                high(0)
                high(1)
                out_high_part(it)
                high(2)
                for k, xt in enumerate((xt_h, xt_l)):
                    act.wait_ge(gathered, it * 2 + (k + 1))
                    act.activation(xt[:].rearrange("p c s -> p (c s)"), ps[:, 2 * k:2 * k + 2, :].rearrange("p a b -> p (a b)"),
                                   ACT.Copy).then_inc(xt_ready, 1)
                for m in range(3, 7):
                    high(m)
                silu(0)
                high(7)
                high(8)
                turned_high(0)
                high(9)
                high(10)
                silu(1)
                high(11)
                turned_high(1)
                act.wait_ge(pick_used, it + 2)
                act.activation(gslot[:], ps[:, 3, 0:1], ACT.Copy, scale=1.0 / ALPHA).then_inc(gslot_ready, 1)

            with act.Fori(0, NE) as e:
                expert(e)
            rounds = act.value_load(cnt_i[0:1, 0:1], min_val=1, max_val=TT)
            with act.Fori(1, TT) as r:
                with act.If(r < rounds):
                    with act.Fori(0, NE) as e:
                        expert(r * NE + e)
                act.nop()
            out_high_part(rounds * NE)
            for t in range(TT):
                act.wait_ge(y_added, rounds * (NE * TT) + (t + 1))
                if t:
                    act.wait_ge(sq3, t)
                act.activation(squares3[:], y[:, t, :], ACT.Square, accum_out=rt[:, 32 + t:33 + t]).then_inc(sq3, 1)
            act.wait_ge(r3_in, 1)
            act.activation(rt[:, 40:40 + TT], rt[:, 36:36 + TT], ACT.Sqrt).then_inc(r3_out, 1)

        @block.vector
        def _(dve):
            step = [0]

            def link(ins):
                step[0] += 1
                ins.then_inc(dve_step, 1)
                dve.wait_ge(dve_step, step[0])

            def low(n):
                dve.wait_ge(high_done, n + 1)
                dve.tensor_tensor(split_l[:, n % SPLIT_RING], raw[:, n % MIX_RING],
                                  split_h[:, n % SPLIT_RING].bitcast(F32), ALU.subtract).then_inc(low_done, 1)

            dve.wait_ge(squared, TT)
            link(dve.tensor_scalar(st8[:, 4:4 + TT], st8[:, 0:TT], 1.0 / D, RMS_EPS, ALU.mult, ALU.add))
            dve.reciprocal(st8[:, 4:4 + TT], st8[:, 4:4 + TT]).then_inc(rstd_in, 1)
            dve.wait_ge(rstd_out, 1)
            for t in range(TT):
                dve.tensor_scalar(xs[:, t, :], x_in[:, t, :], st8[:, 8 + t:9 + t], None, ALU.mult).then_inc(xs_ready, 1)
            dve.wait_ge(rows_turned, 1)
            link(dve.tensor_copy(cols[:], ps[:, 0, 0:ROWS]))
            turned = ps[:, 1, 0:CB * 32].rearrange("p (c r) -> p c r", r=32)
            dve.tensor_copy(samp_pad[:, :, :, 0:CW - 1], turned[:, :, 0:24].rearrange("p c (b k) -> p c b k", k=CW - 1))
            dve.tensor_copy(h0, turned[:, :, 24:32]).then_inc(rows_copied, 1)
            lam, neg, pos_, one, dif = cols[:, LAM_R:LAM_R + CB], st8[:, 16:24], lam8[:, 0:8], st8[:, 32:40], lam8[:, 8:16]
            link(dve.tensor_scalar(neg, lam, -1.0, None, ALU.mult))
            link(dve.tensor_scalar(pos_, neg, 0.0, None, ALU.max))
            dve.tensor_tensor(neg, neg, lam, ALU.min).then_inc(lam_in, 1)
            dve.wait_ge(lam_exp, 1)
            dve.tensor_scalar(one, st8[:, 24:32], 1.0, None, ALU.add).then_inc(lam_ln_in, 1)
            dve.wait_ge(lam_ln_in, 1)
            link(dve.tensor_scalar(dif, one, -1.0, None, ALU.add))
            link(dve.scalar_tensor_tensor(out=lam8[:, 16:24], in0=dif, scalar=0.0, in1=st8[:, 24:32], op0=ALU.is_equal, op1=ALU.mult))
            link(dve.tensor_scalar(dif, dif, 1e-30, None, ALU.max))
            link(dve.reciprocal(dif, dif))
            link(dve.tensor_tensor(dif, dif, st8[:, 24:32], ALU.mult))
            dve.wait_ge(lam_ln, 1)
            link(dve.tensor_tensor(dif, dif, st8[:, 40:48], ALU.mult))
            link(dve.tensor_tensor(dif, dif, lam8[:, 16:24], ALU.add))
            link(dve.tensor_tensor(dif, dif, pos_, ALU.add))
            dve.tensor_scalar(st8[:, 48:56], dif, -8.0, None, ALU.mult)
            dve.tensor_scalar(st8[:, 56:64], dif, 8.0, None, ALU.mult).then_inc(lam_ready, 1)
            for k in range(2):
                dve.wait_ge(ws_turned, k + 1)
                dve.tensor_copy(wst[:, k].rearrange("p g t -> p (g t)"), ps[:, 2 + k, :]).then_inc(ws_ready, 1)
            low(0)
            low(1)
            for c in range(CB):
                dve.wait_ge(xn_high, c + 1)
                i_ = dve.scalar_tensor_tensor(out=act_l[:, c, :], in0=ps[:, c, 0:T], scalar=cols[:, G1_R + c:G1_R + c + 1],
                                              in1=act_h[:, c, :].bitcast(F32), op0=ALU.mult, op1=ALU.subtract)
                i_.then_inc(xn_ready, 1)
            dve.wait_ge(xn_ready, CB)
            dve.nop().then_inc(z_evac, 4)
            low(2)

            def conv(k):
                for c in range(CB):
                    wk = cols[:, CONVW_R + CB * k + c:CONVW_R + CB * k + c + 1]
                    for src, dst in ((xpad[:, c, k:k + SEQ], xc[:, c, 0:SEQ]),
                                     (samp_pad[:, c, :, k:k + SF], xc[:, c, SEQ:T].rearrange("p (b s) -> p b s", s=SF))):
                        if k == 0:
                            i_ = dve.tensor_scalar(dst, src, wk, cols[:, CBIAS_R + c:CBIAS_R + c + 1], ALU.mult, ALU.add)
                        else:
                            i_ = dve.scalar_tensor_tensor(out=dst, in0=src, scalar=wk, in1=dst, op0=ALU.mult, op1=ALU.add)
                link(i_)

            for c in range(NZ):
                low(2 * c + 3)
                if c == 2:
                    dve.wait_ge(z_evac, 4 + 8)
                    dve.wait_ge(const_ready, 2)
                    conv(0)
                if c in (3, 4, 5):
                    conv(c - 2)
                if c == 5:
                    dve.nop().then_inc(conv_done, 1)
                    dve.tensor_copy(pack[:, :, 0:3], xpad[:, :, SEQ:PADP])
                    dve.tensor_copy(pack[:, :, 3:27].rearrange("p c (b k) -> p c b k", k=CW - 1), samp_pad[:, :, :, SF:])
                low(2 * c + 4)

            def lru(hf):
                cs = slice(4 * hf, 4 * hf + 4)
                dve.wait_ge(gates_read, 2 * hf + 2)
                link(dve.tensor_tensor(lru_i[:], lru_i[:], xc[:, cs], ALU.mult))
                dve.wait_ge(decay_ready, hf + 1)
                link(dve.tensor_tensor(tmp[:], lru_a[:], lru_a[:], ALU.mult))
                link(dve.scalar_tensor_tensor(out=lru_r[:], in0=tmp[:], scalar=1.0, in1=lru_r[:], op0=ALU.add, op1=ALU.mult))
                dve.tensor_scalar(lru_r[:], lru_r[:], 0.0, None, ALU.max).then_inc(mult_in, 1)
                dve.wait_ge(mult_ready, hf + 1)
                link(dve.memset(lru_r[:, :, 0:1], 1.0))
                link(dve.tensor_tensor(lru_i[:], lru_i[:], lru_r[:], ALU.mult))
                first_a = lru_a[:, :, SEQ:T].rearrange("p c (b s) -> p c b s", s=SF)[:, :, :, 0]
                first_i = lru_i[:, :, SEQ:T].rearrange("p c (b s) -> p c b s", s=SF)[:, :, :, 0]
                link(dve.tensor_tensor(tmp[:, :, 0:ST], first_a, h0[:, cs, :], ALU.mult))
                link(dve.tensor_tensor(first_i, first_i, tmp[:, :, 0:ST], ALU.add))
                dve.memset(first_a, 0.0)
                link(dve.memset(lru_a[:, :, 0:1], 0.0))
                link(dve.tensor_tensor_scan(xc[:, cs].rearrange("p c t -> p (c t)"), lru_a[:].rearrange("p c t -> p (c t)"),
                                            lru_i[:].rearrange("p c t -> p (c t)"), 0.0, ALU.mult, ALU.add))
                dve.tensor_copy(pack[:, cs, 27:28], xc[:, cs, SEQ - 1:SEQ])
                dve.tensor_copy(pack[:, cs, 28:36], xc[:, cs, SEQ:T].rearrange("p c (b s) -> p c b s", s=SF)[:, :, :, SF - 1]).then_inc(st_packed, 1)
                link(dve.tensor_tensor(tmp[:], xc[:, cs], ga[:, cs], ALU.mult))

            def lru_split(hf):
                cs = slice(4 * hf, 4 * hf + 4)
                dve.wait_ge(unit_used, PB_U)
                link(dve.tensor_copy(act_h[:, cs], tmp[:]))
                dve.tensor_tensor(act_l[:, cs], tmp[:], act_h[:, cs].bitcast(F32), ALU.subtract).then_inc(lru_ready, 1)
                dve.wait_ge(lru_ready, hf + 1)

            lru(0)
            low(V_U + 3)
            for t in range(TT):
                dve.wait_ge(v_read, t + 1)
                i_ = dve.bn_stats(bn[:, t, :], v[:, t, :])
            link(i_)
            for t in range(TT):
                i_ = dve.bn_aggr(bnm[:, t, :], bn[:, t, :])
            link(i_)
            link(dve.tensor_scalar(st8[:, 8:8 + TT], bnm[:, :, 1], LN_EPS, None, ALU.add))
            dve.reciprocal(st8[:, 8:8 + TT], st8[:, 8:8 + TT]).then_inc(ln_in, 1)
            dve.wait_ge(ln_out, 1)
            for t in range(TT):
                i_ = dve.tensor_scalar(v[:, t, :], v[:, t, :], bnm[:, t, 0:1], st8[:, 12 + t:13 + t], ALU.subtract, ALU.mult)
            link(i_)
            dve.wait_ge(ln_loaded, 48)
            link(dve.tensor_tensor(v[:], v[:], lng[:].unsqueeze(1).broadcast_to([P, TT, DM]), ALU.mult))
            dve.tensor_tensor(v[:], v[:], lnb[:].unsqueeze(1).broadcast_to([P, TT, DM]), ALU.add).then_inc(v_ready, 1)
            lru_split(0)
            low(V_U + 4)
            for g in range(MG):
                dve.wait_ge(vmix_mm, g + 1)
                s_p = tmp[:, g % 2, :]
                dve.tensor_tensor(s_p[:, 0:SEQ].rearrange("p (n t) -> p n t", t=P), ps[:, g, 0:SEQ].rearrange("p (n t) -> p n t", t=P),
                                  bsb[:, g, :].unsqueeze(1).broadcast_to([P, 2, P]), ALU.add)
                link(dve.tensor_tensor(s_p[:, SEQ:T].rearrange("p (b s) -> p b s", s=SF), ps[:, g, SEQ:T].rearrange("p (b s) -> p b s", s=SF),
                                       bsb[:, g, 0:SF].unsqueeze(1).broadcast_to([P, ST, SF]), ALU.add))
                link(dve.tensor_tensor(s_p, s_p, u[:, g, :], ALU.mult))
                link(dve.tensor_copy(yb_h[:, g, :], s_p))
                dve.tensor_tensor(yb_l[:, g, :], s_p, yb_h[:, g, :].bitcast(F32), ALU.subtract).then_inc(yb_ready, 1)
            lru(1)
            lru_split(1)
            low(V_U + 5)
            for k in range(2):
                for b in range(4):
                    wait_part(dve, pb_mm, 4, k, b, PB_U + k)
                    i_ = dve.tensor_tensor(gate_b[:, 4 * k + b, :], gate_b[:, 4 * k + b, :], ps[:, 4 * (1 - k) + b, 0:T], ALU.mult)
                    i_.then_inc(pb_read, 1)
                low(V_U + 6 + k)
            for k in range(2):
                for b in range(4):
                    c = 4 * k + b
                    wait_part(dve, pa_mm, 4, k, b, PA_U + 2 * k + 1)
                    link(dve.tensor_tensor(gate_a[:, c, :], gate_a[:, c, :], ps[:, 4 * (1 - k) + b, 0:T], ALU.mult))
                    if c == 0:
                        dve.wait_ge(pb_read, CB)
                    link(dve.tensor_tensor(gate_a[:, c, :], gate_a[:, c, :], gate_b[:, c, :], ALU.add))
                    link(dve.tensor_copy(mrg_h[:, c, :], gate_a[:, c, :]))
                    dve.tensor_tensor(mrg_l[:, c, :], gate_a[:, c, :], mrg_h[:, c, :].bitcast(F32), ALU.subtract).then_inc(mrg_ready, 1)
                low(V_U + 8 + 2 * k)
                low(V_U + 9 + 2 * k)
            for k in range(2):
                dve.wait_ge(st_turned, k + 1)
                i_ = dve.tensor_copy(state_out[:, 512 * k:512 * k + 512], ps[0:36, 4 * k + 3, :])
            i_.then_inc(st_ready, 1)
            dve.wait_ge(y_loaded, 32)
            for k in range(2):
                for t in range(TT):
                    wait_part(dve, wo_mm, TT, k, t, WO_U + 2 * k + 1)
                    dve.tensor_tensor(y[:, t, UC * k:UC * k + UC], y[:, t, UC * k:UC * k + UC], ps[:, 4 * (1 - k) + t, :],
                                      ALU.add).then_inc(y_ready, 1)
            dve.wait_ge(bias_loaded, 32)
            link(dve.tensor_copy(bias_hl[:], bias_raw[:]))
            dve.tensor_tensor(bias_hl[NE:2 * NE, :], bias_raw[NE:2 * NE, :], bias_hl[NE:2 * NE, :].bitcast(F32), ALU.subtract)
            dve.wait_ge(sq2, TT)
            link(dve.tensor_scalar(rt[:, 4:4 + TT], rt[:, 0:TT], 1.0 / D, RMS_EPS, ALU.mult, ALU.add))
            dve.reciprocal(rt[:, 4:4 + TT], rt[:, 4:4 + TT]).then_inc(r2_in, 1)
            dve.wait_ge(r2_out, 1)
            dve.wait_ge(late_loaded, 5 * 16)
            for t in range(TT):
                dve.scalar_tensor_tensor(out=xn2[:, t, :], in0=y[:, t, :], scalar=rt[:, 8 + t:9 + t], in1=n2b[:],
                                         op0=ALU.mult, op1=ALU.mult).then_inc(xn2_ready, 1)
            for t in range(TT):
                dve.wait_ge(xn2_high, t + 1)
                i_ = dve.tensor_tensor(xn_l[:, t, :], xn2[:, t, :], xn_h[:, t, :].bitcast(F32), ALU.subtract)
            i_.then_inc(xn2_low, 1)
            dve.wait_ge(logits_mm, 1)
            link(dve.tensor_tensor(lg[:], ps[:, 6, 0:TT * NE].rearrange("p (t e) -> p t e", e=NE),
                                   brb[:].unsqueeze(1).broadcast_to([P, TT, NE]), ALU.add))
            for t in range(TT):
                i_ = dve.max(mx[:, t, :], lg[:, t, :])
            link(i_)
            dve.tensor_scalar(rt[:, 16:16 + TT], mx[:, :, 0], -1.0, None, ALU.mult).then_inc(top_ready, 1)
            for t in range(TT):
                i_ = dve.max_index(ix[:, t, :], mx[:, t, :], lg[:, t, :])
            link(i_)
            link(dve.tensor_copy(ixf[:], ix[:]))
            dve.wait_ge(top_exp, 1)
            link(dve.reciprocal(rt[:, 24:24 + TT], rt[:, 20:20 + TT]))
            for t in range(TT):
                i_ = dve.tensor_scalar(ex[:, t, 0:TOPK], ex[:, t, 0:TOPK], rt[:, 24 + t:25 + t], None, ALU.mult)
            link(i_)
            for t in range(TT):
                for k in range(TOPK):
                    i_ = dve.tensor_scalar(oh[:, t, k, :], iota_s[:, 0:NE], ixf[:, t, k:k + 1], ex[:, t, k:k + 1], ALU.is_equal, ALU.mult)
            link(i_)
            link(dve.tensor_reduce(gat[:], oh[:].rearrange("p t k e -> p t e k"), AX_X, ALU.add))
            link(dve.tensor_scalar(maskf[:], gat[:], 0.0, None, ALU.is_gt))
            dve.tensor_copy(mask[:], maskf[:]).then_inc(mask_ready, 1)
            link(dve.tensor_scalar(maskf[:], maskf[:], FAR, P - FAR, ALU.mult, ALU.add))
            dve.wait_ge(pos_mm, 1)
            link(dve.tensor_tensor(pos[:], maskf[:], ps[:, 7, 0:TT * NE].rearrange("p (t e) -> p t e", e=NE), ALU.add))
            link(dve.tensor_reduce(cnt[0:1, 0:1], ps[0:1, 7, TT * NE:(TT + 1) * NE], AX_X, ALU.max))
            link(dve.tensor_scalar(cnt[0:1, 1:2], cnt[0:1, 0:1], float(P), 1.0, ALU.is_gt, ALU.add))
            link(dve.tensor_scalar(cnt[0:1, 2:3], cnt[0:1, 0:1], 2.0 * P, None, ALU.is_gt))
            link(dve.tensor_tensor(cnt[0:1, 3:4], cnt[0:1, 1:2], cnt[0:1, 2:3], ALU.add))
            dve.tensor_copy(cnt_i[0:1, 0:1], cnt[0:1, 3:4]).then_inc(pos_ready, 1)
            dve.wait_ge(post_mm, 1)
            dve.tensor_copy(post[:], ps[0:NE, 5, 0:T])
            dve.tensor_copy(gat_t[:], ps[0:NE, 4, 0:T]).then_inc(gat_ready, 1)
            dve.memset(pick_t[:].bitcast(F32), 0.0).then_inc(pick_t_ready, 1)
            dve.wait_ge(gat_ready, 1)
            dve.wait_ge(pos_ready, 1)
            for t in range(TT):
                dve.wait_ge(bd_mm, t + 1)
                i_ = dve.tensor_tensor(y[:, t, :], y[:, t, :], ps[:, 2 * t:2 * t + 2, :].rearrange("p a b -> p (a b)"), ALU.add)
            i_.then_inc(route_ready, 1)
            dve.wait_ge(route_ready, 1)

            def out_low_part(it):
                dve.wait_ge(out_high, it + 1)
                dve.scalar_tensor_tensor(out=out_l[:], in0=ps[:, 4:6, :].rearrange("p a b -> p (a b)"), scalar=gslot[:, 0:1],
                                         in1=out_h[:].bitcast(F32), op0=ALU.mult, op1=ALU.subtract).then_inc(out_ready, 1)

            def add_to_tokens(it):
                for t, bank in enumerate((6, 4, 0)):
                    dve.wait_ge(combined, it * TT + (t + 1))
                    dve.tensor_tensor(y[:, t, :], y[:, t, :], ps[:, bank:bank + 2, :].rearrange("p a b -> p (a b)"),
                                      ALU.add).then_inc(y_added, 1)

            def expert(it):
                def low(m):
                    dve.wait_ge(high_done, it * EXP_U + (MIX_U + m + 1))
                    dve.tensor_tensor(split_l[:, m % SPLIT_RING], raw[:, m % RAW_RING],
                                      split_h[:, m % SPLIT_RING].bitcast(F32), ALU.subtract).then_inc(low_done, 1)

                def clip(j):
                    gate_bank = (2, 0)[j]
                    dve.wait_ge(unit_used, it * EXP_U + (MIX_U + 4 * (j + 1)))
                    dve.tensor_scalar(u1[:], ps[:, gate_bank + 1, :], LIMIT, -LIMIT, ALU.min, ALU.max)
                    dve.tensor_scalar(g1[:], ps[:, gate_bank, :], LIMIT, None, ALU.min).then_inc(clipped, 1)
                    dve.wait_ge(silu_done, it * 2 + (j + 1))
                    dve.scalar_tensor_tensor(out=actv[:, UC * j:UC * j + UC], in0=u1[:], scalar=1.0, in1=sil[:],
                                             op0=ALU.add, op1=ALU.mult).then_inc(act_ready, 1)

                def turned_low(j):
                    dve.wait_ge(at_high, it * 2 + (j + 1))
                    dve.tensor_tensor(at_l[:, 4 * j:4 * j + 4, :].rearrange("p c s -> p (c s)"), ps[:, 6 + j, :],
                                      at_h[:, 4 * j:4 * j + 4, :].rearrange("p c s -> p (c s)").bitcast(F32),
                                      ALU.subtract).then_inc(at_ready, 1)

                low(0)
                low(1)
                out_low_part(it)
                low(2)
                add_to_tokens(it)
                for m in range(3, 7):
                    low(m)
                clip(0)
                low(7)
                low(8)
                turned_low(0)
                low(9)
                low(10)
                clip(1)
                low(11)
                turned_low(1)
                dve.wait_ge(sel_used, it + 2)
                dve.tensor_scalar(pick_t[:], ps[:, 2, 0:T], slot_p[:, 0:1], None, ALU.is_equal).then_inc(pick_t_ready, 1)

            with dve.Fori(0, NE) as e:
                expert(e)
            rounds = dve.value_load(cnt_i[0:1, 0:1], min_val=1, max_val=TT)
            with dve.Fori(1, TT) as r:
                with dve.If(r < rounds):
                    with dve.Fori(0, NE) as e:
                        expert(r * NE + e)
                dve.nop()
            out_low_part(rounds * NE)
            add_to_tokens(rounds * NE)
            dve.wait_ge(sq3, TT)
            dve.tensor_scalar(rt[:, 36:36 + TT], rt[:, 32:32 + TT], 1.0 / D, RMS_EPS, ALU.mult, ALU.add).then_inc(r3_mean, 1)
            dve.wait_ge(r3_mean, 1)
            dve.reciprocal(rt[:, 36:36 + TT], rt[:, 36:36 + TT]).then_inc(r3_in, 1)
            dve.wait_ge(r3_out, 1)
            for t in range(TT):
                dve.scalar_tensor_tensor(out=y[:, t, :], in0=y[:, t, :], scalar=rt[:, 40 + t:41 + t], in1=fnb[:],
                                         op0=ALU.mult, op1=ALU.mult).then_inc(out_final, 1)

        @block.tensor
        def _(pe):
            def three(out, a_h, a_l, b_h, b_l, start, stop):
                pe.matmul(out, a_h, b_h, start=start, stop=False)
                pe.matmul(out, a_h, b_l, start=False, stop=False)
                return pe.matmul(out, a_l, b_h, start=False, stop=stop)

            pe.wait_ge(const_ready, 1)
            pe.wait_ge(rows_loaded, 8 * 16)
            pe.transpose(ps[:, 0, 0:ROWS], rows[:], ident[0:ROWS, 0:ROWS])
            for c in range(CB):
                i_ = pe.transpose(ps[:, 1, 32 * c:32 * c + 32], state_in[:, c * P:(c + 1) * P], ident[0:32, 0:32])
            i_.then_inc(rows_turned, 1)
            pe.wait_ge(ws_loaded, 16 * (1 + ST))
            for k in range(2):
                for g in range(MG):
                    i_ = pe.transpose(ps[:, 2 + k, g * P:(g + 1) * P], ws_raw[:, k, g, :], ident[:])
                i_.then_inc(ws_turned, 1)
            for c in range(CB):
                if c == 0:
                    pe.wait_ge(rows_copied, 1)
                    pe.wait_ge(xs_ready, TT)
                if c == 2:
                    pe.wait_ge(ws_ready, 2)
                for t in range(TT):
                    i_ = pe.transpose(ps[:, c, t * P:(t + 1) * P], xs[:, t, c * P:(c + 1) * P], ident[:])
                i_.then_inc(xs_turned, 1)
            pe.wait_ge(xn_ready, CB)

            def channel_unit(slot, k_blocks, bank, act_hl, start, stop, ready=None, before=None):
                x_h, x_l = act_hl
                for b in range(4):
                    if before:
                        before(b)
                    for j in range(KB):
                        cols_ = slice(b * P, (b + 1) * P)
                        i_ = three(ps[:, bank + b, 0:T], split_h[:, slot, j, cols_], split_l[:, slot, j, cols_],
                                   x_h[:, k_blocks + j, :], x_l[:, k_blocks + j, :], start and j == 0, stop and j == KB - 1)
                    if b == 3:
                        i_.then_inc(unit_used, 1)
                    elif ready:
                        i_.then_inc(ready, 1)

            with pe.Fori(0, NZ // 3) as g:
                for c in range(3):
                    for h in range(2):
                        pe.wait_ge(low_done, g * 6 + (2 * c + h + 1))

                        def bank_free(b):
                            if h == 0 and c != 1:
                                pe.wait_ge(z_evac, g * 12 + (b + 1 + (4 if c == 2 else 0)))
                        channel_unit((2 * c + h) % SPLIT_RING, KB * h, 4 * (c % 2), (act_h, act_l), h == 0, h == 1,
                                     z_ready if h else None, bank_free)

            def lru_gates(hf):
                for k in range(2):
                    bank = 4 * (k if hf == 0 else 1 - k)
                    if hf == 0:
                        pe.wait_ge(z_evac, 4 * (NZ + 1))
                    else:
                        pe.wait_ge(gates_read, 2)
                        pe.wait_ge(v_read, TT)
                    for b in range(4):
                        i_ = pe.matmul(ps[:, bank + b, 0:T], lruw[:, k, 4 * hf + b, :], xc_view[:, 4 * hf + b, :], start=True, stop=True)
                    i_.then_inc(gates_mm, 1)

            xc_view = xc
            pe.wait_ge(conv_done, 1)
            pe.wait_ge(lruw_loaded, 64)
            lru_gates(0)
            pe.wait_ge(gates_read, 1)
            for h in range(2):
                n = V_U + h
                pe.wait_ge(low_done, n + 1)
                for t in range(TT):
                    for j in range(KB):
                        ts_ = slice(t * P, (t + 1) * P)
                        i_ = three(ps[:, t, :], act_h[:, KB * h + j, ts_], act_l[:, KB * h + j, ts_],
                                   split_h[:, n % SPLIT_RING, j, :], split_l[:, n % SPLIT_RING, j, :],
                                   h == 0 and j == 0, h == 1 and j == KB - 1)
                    if t == TT - 1:
                        i_.then_inc(unit_used, 1)
                    elif h:
                        i_.then_inc(v_mm, 1)
            lru_gates(1)
            pe.wait_ge(v_ready, 1)
            pe.wait_ge(const_ready, 4)
            pe.wait_ge(gates_read, 4)
            for g in range(MG):
                for t in range(TT):
                    i_ = pe.matmul(ps[:, g, t * P:(t + 1) * P], v[:, t, g * P:(g + 1) * P], wst[:, t // 2, g, :], start=True, stop=True)
                i_.then_inc(vmix_mm, 1)
            pe.wait_ge(yb_ready, MG)
            for k in range(2):
                pe.wait_ge(low_done, PB_U + k + 1)
                channel_unit((PB_U + k) % SPLIT_RING, 0, 4 * (1 - k), (yb_h, yb_l), True, True, pb_mm)
            pe.wait_ge(lru_ready, 2)
            for k in range(2):
                for h in range(2):
                    n = PA_U + 2 * k + h
                    pe.wait_ge(low_done, n + 1)
                    channel_unit(n % SPLIT_RING, KB * h, 4 * (1 - k), (act_h, act_l), h == 0, h == 1, pa_mm if h else None,
                                 (lambda b: pe.wait_ge(pb_read, 4 * k + b + 1)) if h == 0 else None)
            pe.wait_ge(mrg_ready, CB)
            pe.wait_ge(st_packed, 2)
            for c in range(CB):
                i_ = pe.transpose(ps[0:36, 4 * (c // 4) + 3, (c % 4) * P:(c % 4 + 1) * P], pack[:, c, :], ident[:])
                if c % 4 == 3:
                    i_.then_inc(st_turned, 1)
            for k in range(2):
                for h in range(2):
                    n = WO_U + 2 * k + h
                    pe.wait_ge(low_done, n + 1)
                    for t in range(TT):
                        for j in range(KB):
                            ts_ = slice(t * P, (t + 1) * P)
                            i_ = three(ps[:, 4 * (1 - k) + t, :], mrg_h[:, KB * h + j, ts_], mrg_l[:, KB * h + j, ts_],
                                       split_h[:, n % SPLIT_RING, j, :], split_l[:, n % SPLIT_RING, j, :],
                                       h == 0 and j == 0, h == 1 and j == KB - 1)
                        if t == TT - 1:
                            i_.then_inc(unit_used, 1)
                        elif h:
                            i_.then_inc(wo_mm, 1)
            pe.wait_ge(y_ready, 2 * TT)
            for t in range(TT):
                pe.wait_ge(xn2_ready, t + 1)
                for c in range(CB):
                    i_ = pe.transpose(ps[:, 2 * t + c // 4, (c % 4) * P:(c % 4 + 1) * P], xn2[:, t, c * P:(c + 1) * P], ident[:])
                    if c % 4 == 3:
                        i_.then_inc(xn2_turned, 1)
            for t in range(TT):
                pe.wait_ge(xnt_ready, 2 * (t + 1))
                for c in range(CB):
                    i_ = pe.matmul(ps[:, 6, t * NE:(t + 1) * NE], xnt[:, c, t * P:(t + 1) * P], wr[:, c, :], start=c == 0, stop=c == CB - 1)
            i_.then_inc(logits_mm, 1)
            pe.wait_ge(mask_ready, 1)
            pe.wait_ge(st_ready, 1)
            for t in range(TT):
                for s_ in range(t + 1):
                    pe.matmul(ps[:, 7, t * NE:(t + 1) * NE], tri[:] if s_ == t else ones_b[:], mask[:, s_, :], start=s_ == 0, stop=s_ == t)
            for t in range(TT):
                i_ = pe.matmul(ps[:, 7, TT * NE:(TT + 1) * NE], ones_b[:], mask[:, t, :], start=t == 0, stop=t == TT - 1)
            i_.then_inc(pos_mm, 1)
            pe.wait_ge(pos_ready, 1)
            for t in range(TT):
                pe.transpose(ps[0:NE, 5, t * P:(t + 1) * P], pos[:, t, :], ident[:])
                i_ = pe.transpose(ps[0:NE, 4, t * P:(t + 1) * P], gat[:, t, :], ident[:])
            i_.then_inc(post_mm, 1)
            pe.wait_ge(gat_ready, 1)
            for t in range(TT):
                for k in range(2):
                    i_ = pe.matmul(ps[:, 2 * t + k, :], gat_t[:, t * P:(t + 1) * P], bdn[:, UC * k:UC * k + UC], start=True, stop=True)
                i_.then_inc(bd_mm, 1)
            pe.wait_ge(route_ready, 1)
            pe.wait_ge(pick_t_ready, 1)
            pe.wait_ge(xn2_high, TT)
            pe.wait_ge(xn2_low, 1)
            pe.matmul(ps[:, 4, :], pick_t[:, 0:P], xn_h[:, 0, 0:UC], start=True, stop=True).then_inc(pick_used, 1)
            pe.matmul(ps[:, 5, :], pick_t[:, 0:P], xn_h[:, 0, 0:UC], start=True, stop=True).then_inc(sel_used, 1)

            def combine(it, last):
                pe.wait_ge(out_ready, it + 1)
                pe.wait_ge(pick_t_ready, it + 1)
                for t, bank in enumerate((6, 4, 0)):
                    if t == 2 and not last:
                        pe.wait_ge(xt_ready, it * 2 + 1)
                    for k in range(2):
                        pe.matmul(ps[:, bank + k, :], pick_t[:, t * P:(t + 1) * P], out_h[:, UC * k:UC * k + UC], start=True, stop=False)
                        i_ = pe.matmul(ps[:, bank + k, :], pick_t[:, t * P:(t + 1) * P], out_l[:, UC * k:UC * k + UC], start=False, stop=True)
                    i_.then_inc(combined, 1)

            def expert(it, e):
                def unit(m, bank, x_h, x_l, first, last):
                    pe.wait_ge(low_done, it * EXP_U + (MIX_U + m + 1))
                    k0 = KB * (m % 2 if m < 8 else (m - 8) // 2)
                    for j in range(KB):
                        i_ = three(ps[:, bank, :], x_h[:, k0 + j, :], x_l[:, k0 + j, :], split_h[:, m % SPLIT_RING, j, :],
                                   split_l[:, m % SPLIT_RING, j, :], first and j == 0, last and j == KB - 1)
                    i_.then_inc(unit_used, 1)

                def linear(m, bank, bias_col):
                    pe.matmul(ps[:, bank, :], sel[:], bias_hl[:, bias_col:bias_col + UC], start=True, stop=False)
                    unit(m, bank, xt_h, xt_l, False, False)
                    unit(m + 1, bank, xt_h, xt_l, False, True)

                def turn(j):
                    pe.wait_ge(act_ready, it * 2 + (j + 1))
                    for c in range(4):
                        i_ = pe.transpose(ps[:, 6 + j, c * P:(c + 1) * P], actv[:, UC * j + c * P:UC * j + (c + 1) * P], ident[:])
                    i_.then_inc(act_turned, 1)

                pe.wait_ge(pick_ready, it + 1)
                for k, xn in enumerate((xn_h, xn_l)):
                    if k == 1:
                        pe.wait_ge(pick_t_ready, it + 1)
                        pe.wait_ge(gslot_ready, it + 1)
                    for c in range(CB):
                        for t in range(TT):
                            i_ = pe.matmul(ps[:, 2 * k + c // 4, (c % 4) * P:(c % 4 + 1) * P], xn[:, t, c * P:(c + 1) * P],
                                           pick[:, t, :], start=t == 0, stop=t == TT - 1)
                    i_.then_inc(gathered, 1)
                combine(it, False)
                pe.wait_ge(xt_ready, it * 2 + 2)
                pe.wait_ge(sel_ready, it + 1)
                linear(0, 2, 0)
                linear(2, 3, D)
                pe.wait_ge(y_added, it * TT + TT)
                linear(4, 0, UC)
                turn(0)
                linear(6, 1, D + UC)
                pe.matmul(ps[:, 2, 0:T], sel[0:NE, :], post[:], start=True, stop=True).then_inc(sel_used, 1)
                for t in range(TT):
                    i_ = pe.matmul(ps[:, 3, 0:1], pick[:, t, :].bitcast(F32), gat[:, t, bass.ds(e, 1)], start=t == 0, stop=t == TT - 1)
                i_.then_inc(pick_used, 1)
                pe.wait_ge(at_ready, it * 2 + 1)
                unit(8, 4, at_h, at_l, True, False)
                unit(9, 5, at_h, at_l, True, False)
                turn(1)
                pe.wait_ge(at_ready, it * 2 + 2)
                unit(10, 4, at_h, at_l, False, True)
                unit(11, 5, at_h, at_l, False, True)

            with pe.Fori(0, NE) as e:
                expert(e, e)
            rounds = pe.value_load(cnt_i[0:1, 0:1], min_val=1, max_val=TT)
            with pe.Fori(1, TT) as r:
                with pe.If(r < rounds):
                    with pe.Fori(0, NE) as e:
                        expert(r * NE + e, e)
                pe.nop()
            combine(rounds * NE, True)


_INS = ['x_prompt', 'x_sample', 'state_conv', 'state_h', 'norm1_g', 'w_in', 'conv_w', 'conv_b', 'w_rg', 'b_rg',
        'w_ig', 'b_ig', 'lru_lambda', 'ln_v_g', 'ln_v_b', 'w_s', 'b_s', 'w_proj_a', 'w_proj_b', 'w_out', 'norm2_g',
        'w_router', 'b_router', 'w_gate_up', 'b_gate_up', 'w_down', 'b_down', 'final_norm_g']
_OUTS = [((1, SEQ, D), 'float32'), ((ST, SF, D), 'float32'), ((1, 1, CW - 1, D), 'float32'), ((1, 1, D), 'float32'),
         ((1, ST, CW - 1, D), 'float32'), ((1, ST, D), 'float32'), ((1, ST, SF, DM), 'float32')]


def kernel(**inputs):
    import numpy as _np
    import concourse.bacc as _bacc
    from concourse import mybir as _mybir
    from concourse.bass_utils import run_bass_kernel_spmd as _run

    nc = _bacc.Bacc("TRN2", target_bir_lowering=False, num_devices=1)
    arrays, args = {}, []
    for name in _INS:
        a = _np.ascontiguousarray(inputs[name])
        arrays[f"in_{name}_dram"] = a
        args.append(nc.dram_tensor(f"in_{name}_dram", a.shape, _mybir.dt.from_np(a.dtype), kind="ExternalInput").ap())
    for i, (shape, dtype) in enumerate(_OUTS):
        dt = _mybir.dt.from_np(_np.dtype(dtype))
        args.append(nc.dram_tensor(f"out_{i}_dram", shape, dt, kind="ExternalOutput").ap())
    hawk_gmlp_moe_streaming_step(nc, *args)
    r = _run(nc, [arrays], core_ids=[0])
    return tuple(r.results[0][f"out_{i}_dram"] for i in range(len(_OUTS)))
```

```python
from contextlib import ExitStack

import concourse.bass as bass
from concourse import mybir

ALU = mybir.AluOpType
ACT = mybir.ActivationFunctionType
F32 = mybir.dt.float32
F32R = mybir.dt.float32r
BF16 = mybir.dt.bfloat16
I32 = mybir.dt.int32
U32 = mybir.dt.uint32
AX_X = mybir.AxisListType.X

P = 128
D = 1024
CB = D // P
SEQ = 256
ST, SF = 8, 16
T = SEQ + ST * SF
TT = T // P
CW = 4
PADP = CW - 1 + SEQ
PADS = CW - 1 + SF
DM = 512
MG = DM // P
NE = 32
TOPK = 4
LIMIT, ALPHA = 7.0, 1.702
RMS_EPS, LN_EPS = 1e-6, 1e-5

KB = 4
UC = 512
MIX_RING = 2
RAW_RING = 4
MIX_SPLIT = 3
SPLIT_RING = 4
Z_CHUNKS = [0, 1, 2, 3, 4, 6, 7, 8, 9, 5]
NZ = len(Z_CHUNKS) - 1
V_U = 2 * NZ
PB_U = V_U + 2
PA_U = PB_U + 2
WO_U = PA_U + 4
MIX_U = WO_U + 4
EXP_U = 12
COMBINE_BANKS = ((2, 2), (1, 0), (0, 6))
FAR = 1000.0

G1_R, CBIAS_R, BRG_R, BIG_R, LAM_R, CONVW_R = 0, 8, 16, 24, 32, 40
ROWS = CONVW_R + CW * CB


def hawk_gmlp_moe_streaming_step(
    nc, x_prompt, x_sample, state_conv, state_h, norm1_g, w_in, conv_w, conv_b, w_rg, b_rg, w_ig, b_ig,
    lru_lambda, ln_v_g, ln_v_b, w_s, b_s, w_proj_a, w_proj_b, w_out, norm2_g, w_router, b_router,
    w_gate_up, b_gate_up, w_down, b_down, final_norm_g,
    y_prompt, y_sample, new_conv_prompt, new_h_prompt, new_conv_sample, new_h_sample, new_v_sample,
):
    base = (nc.sbuf_base + 31) // 32 * 32
    with ExitStack() as ctx:
        def at(name, offset, shape, dt=F32):
            return nc.alloc_sbuf_tensor_at(name, shape, dt, offset=base + offset)

        def sem(name):
            return ctx.enter_context(nc.semaphore(name))

        split_h = at("split_h", 0, [P, SPLIT_RING, KB, UC], F32R)
        split_l = at("split_l", 32768, [P, SPLIT_RING, KB, UC], F32R)
        raw = at("raw", 65536, [P, RAW_RING, KB, UC])
        x_in = at("x_in", 126976, [P, TT, D])
        lru_r = at("lru_r", 24576, [P, CB // 2, T])
        lru_i = at("lru_i", 57344, [P, CB // 2, T])
        lru_a = at("lru_a", 81920, [P, CB // 2, T])
        wst = at("wst", 88064, [P, 2, MG, P])
        lng = at("lng", 92160, [P, DM])
        lnb = at("lnb", 63488, [P, DM])
        bsb = at("bsb", 30720, [P, MG, P])
        tmp = at("tmp", 94208, [P, CB // 2, T])
        state_out = at("state_out", 94208, [36, D])
        act_h = at("act_h", 102400, [P, CB, T], F32R)
        act_l = at("act_l", 114688, [P, CB, T], F32R)
        xn_h = at("xn_h", 102400, [P, TT, D], F32R)
        xn_l = at("xn_l", 114688, [P, TT, D], F32R)
        ga = at("ga", 126976, [P, CB, T])
        mrg_h = at("mrg_h", 126976, [P, CB, T], F32R)
        xc = at("xc", 139264, [P, CB, T])
        mrg_l = at("mrg_l", 139264, [P, CB, T], F32R)
        at_h = at("at_h", 126976, [P, CB, P], F32R)
        at_l = at("at_l", 131072, [P, CB, P], F32R)
        out_h = [at("out_h0", 135168, [P, D], F32R), at("out_h1", 201728, [P, D], F32R)]
        out_l = [at("out_l0", 139264, [P, D], F32R), at("out_l1", 205824, [P, D], F32R)]
        xt_h = at("xt_h", 143360, [P, CB, 2, P], F32R)
        xt_l = at("xt_l", 176128, [P, CB, 2, P], F32R)
        gate_a = at("gate_a", 151552, [P, CB, T])
        xs = at("xs", 151552, [P, TT, D])
        bias_hl = at("bias_hl", 151552, [2 * NE, 2 * D], F32R)
        actv = at("actv", 159744, [P, D])
        bdn = at("bdn", 159744, [NE, D])
        gate_b = at("gate_b", 163840, [P, CB, T])
        ws_raw = at("ws_raw", 163840, [P, 2, MG, P])
        state_in = at("state_in", 172032, [32, D])
        g1 = at("g1", 163840, [P, UC])
        u1 = at("u1", 165888, [P, UC])
        sil = at("sil", 167936, [P, UC])
        pick = at("pick", 184320, [P, TT, 2, P], F32R)
        pick_t = at("pick_t", 169984, [P, 2, T], F32R)
        wr = at("wr", 173056, [P, CB, NE])
        sel = at("sel", 174080, [2 * NE, P], F32R)
        post = at("post", 174592, [NE, T], F32R)
        xpad = at("xpad", 176128, [P, CB, PADP + ST * PADS])
        yb_h = at("yb_h", 176128, [P, MG, T], F32R)
        yb_l = at("yb_l", 182272, [P, MG, T], F32R)
        bias_raw = at("bias_raw", 176128, [2 * NE, 2 * D])
        xnt = at("xnt", 176128, [P, CB, T])
        u = at("u", 189440, [P, MG, T])
        v = at("v", 195584, [P, TT, DM])
        y = at("y", 189440, [P, TT, D])
        lruw = at("lruw", 201728, [P, 2, CB, P])
        n2b = at("n2b", 201728, [P, D])
        fnb = at("fnb", 65536, [P, D])
        rows = at("rows", 209920, [ROWS, P])
        ident = at("ident", 210432, [P, P])
        iota_s = at("iota_s", 209920, [P, P])
        cols = at("cols", 210944, [P, ROWS])
        tri = at("tri", 211232, [P, P], BF16)
        small = at("small", 211488, [P, 320])
        pos = at("pos", 100352, [P, TT, NE])
        gat = at("gat", 100736, [P, TT, NE])
        h0 = small[:, 0:64].rearrange("p (c b) -> p c b", b=ST)
        st8 = small[:, 64:128]
        pack = at("pack", 100352, [P, CB, 36])
        ones_b = at("ones_b", 101504, [P, P], BF16)
        onehot = at("onehot", 101760, [2 * NE, NE])
        cnt_i = at("cnt_i", 101888, [1, 1], I32)
        slot_p = at("slot_p", 101920, [P, 1])
        pos_e = at("pos_e", 102112, [P, TT, 2])
        gslot = at("gslot", 101952, [P, 1])
        brb = at("brb", 101984, [P, NE])
        lg = at("lg", 126976, [P, TT, NE])
        mx = at("mx", 127360, [P, TT, 8])
        ix = at("ix", 127456, [P, TT, 8], U32)
        ixf = at("ixf", 127552, [P, TT, 8])
        ex = at("ex", 127648, [P, TT, 8])
        oh = at("oh", 127744, [P, TT, TOPK, NE])
        mask = at("mask", 129280, [P, TT, NE], BF16)
        maskf = at("maskf", 129472, [P, TT, NE])
        gat_t = at("gat_t", 129856, [NE, T])
        cnt = at("cnt", 131392, [1, 8])
        xn2 = at("xn2", 139264, [P, TT, D])
        squares = at("squares", 184320, [P, D])
        squares3 = at("squares3", 143360, [P, D])
        lam8 = small[:, 128:152]
        bn = small[:, 152:170].rearrange("p (t k) -> p t k", k=6)
        bnm = small[:, 170:176].rearrange("p (t k) -> p t k", k=2)
        rt = small[:, 192:256]
        ps = ctx.enter_context(nc.psum_tensor("ps", [P, 8, 512], F32))

        x_loaded, rows_loaded = sem("x_loaded"), sem("rows_loaded")
        lruw_loaded, ws_loaded, ln_loaded = sem("lruw_loaded"), sem("ws_loaded"), sem("ln_loaded")
        late_loaded, y_loaded, bias_loaded = sem("late_loaded"), sem("y_loaded"), sem("bias_loaded")
        fnb_loaded = sem("fnb_loaded")
        mix_landed = [sem(f"mix_landed{i}") for i in range(MIX_RING)]
        exp_landed = [sem(f"exp_landed{i}") for i in range(RAW_RING)]
        high_done, low_done, unit_used = sem("high_done"), sem("low_done"), sem("unit_used")
        const_ready, pool_step, dve_step, act_step = sem("const_ready"), sem("pool_step"), sem("dve_step"), sem("act_step")
        zeroed = sem("zeroed")
        squared, rstd_in, rstd_out, xs_ready = sem("squared"), sem("rstd_in"), sem("rstd_out"), sem("xs_ready")
        rows_turned, rows_copied, xs_turned, xn_high, xn_ready = (
            sem("rows_turned"), sem("rows_copied"), sem("xs_turned"), sem("xn_high"), sem("xn_ready"))
        lam_in, lam_exp, lam_ln_in, lam_ln, lam_ready = (
            sem("lam_in"), sem("lam_exp"), sem("lam_ln_in"), sem("lam_ln"), sem("lam_ready"))
        z_ready, z_evac, conv_done = sem("z_ready"), sem("z_evac"), sem("conv_done")
        gates_mm, gates_read, decay_ready, mult_in, mult_ready, lru_ready, scanned = (
            sem("gates_mm"), sem("gates_read"), sem("decay_ready"), sem("mult_in"), sem("mult_ready"),
            sem("lru_ready"), sem("scanned"))
        v_mm, v_read, ln_in, ln_out, v_ready = sem("v_mm"), sem("v_read"), sem("ln_in"), sem("ln_out"), sem("v_ready")
        ws_turned, ws_ready, vmix_mm, yb_ready = sem("ws_turned"), sem("ws_ready"), sem("vmix_mm"), sem("yb_ready")
        pb_mm, pb_read, pa_mm, mrg_ready, wo_mm, y_ready = (
            sem("pb_mm"), sem("pb_read"), sem("pa_mm"), sem("mrg_ready"), sem("wo_mm"), sem("y_ready"))
        st_packed, st_turned, st_ready = sem("st_packed"), sem("st_turned"), sem("st_ready")
        sq2, r2_in, r2_out, xn2_ready, xn2_turned, xnt_ready, xn2_high = (
            sem("sq2"), sem("r2_in"), sem("r2_out"), sem("xn2_ready"), sem("xn2_turned"), sem("xnt_ready"),
            sem("xn2_high"))
        logits_mm, top_ready, top_exp, mask_ready, pos_mm, pos_ready, post_mm, route_ready = (
            sem("logits_mm"), sem("top_ready"), sem("top_exp"), sem("mask_ready"), sem("pos_mm"),
            sem("pos_ready"), sem("post_mm"), sem("route_ready"))
        gat_mm, gat_ready, bd_mm = sem("gat_mm"), sem("gat_ready"), sem("bd_mm")
        ranks_ready, column_ready = sem("ranks_ready"), sem("column_ready")
        ranks_seen, column_seen = sem("ranks_seen"), sem("column_seen")
        pick_ready, pick_used, sel_ready, sel_used = (
            sem("pick_ready"), sem("pick_used"), sem("sel_ready"), sem("sel_used"))
        gathered, xt_ready, xt_low_ready, out_high, out_ready, pick_t_ready, combined, y_added = (
            sem("gathered"), sem("xt_ready"), sem("xt_low_ready"), sem("out_high"), sem("out_ready"), sem("pick_t_ready"),
            sem("combined"), sem("y_added"))
        clipped, up_clipped, silu_done, act_ready, act_turned, at_high, at_ready, gslot_ready = (
            sem("clipped"), sem("up_clipped"), sem("silu_done"), sem("act_ready"), sem("act_turned"), sem("at_high"),
            sem("at_ready"), sem("gslot_ready"))
        xn2_low, r3_mean = sem("xn2_low"), sem("r3_mean")
        sq3, r3_in, r3_out, out_final, stored = sem("sq3"), sem("r3_in"), sem("r3_out"), sem("out_final"), sem("stored")

        def halves(w):
            return w.rearrange("o (h j p) n -> (o h) p j n", j=KB, p=P)

        win, wpa, wpb, wout = halves(w_in), halves(w_proj_a), halves(w_proj_b), halves(w_out)
        wgu = w_gate_up.rearrange("o e (h j p) n -> (o e) h p j n", j=KB, p=P)
        wdn = w_down.rearrange("o e (h j p) n -> (o e) h p j n", j=KB, p=P)

        def mix_unit(n):
            if n < PB_U:
                c = Z_CHUNKS[n // 2]
                return win[n % 2][:, :, c * UC:(c + 1) * UC]
            if n < PA_U:
                c = n - PB_U
                return wpb[0][:, :, c * UC:(c + 1) * UC]
            w, m = (wpa, n - PA_U) if n < WO_U else (wout, n - WO_U)
            return w[m % 2][:, :, m // 2 * UC:(m // 2 + 1) * UC]

        def exp_unit(e, m):
            if m < 8:
                c = (0, 2, 1, 3)[m // 2]
                w, half = wgu, m % 2
            else:
                c, half, w = m % 2, (m - 8) // 2, wdn
            return w[bass.ds(e, 1), half, :, :, c * UC:(c + 1) * UC].rearrange("o p j n -> (o p) j n")

        def wait_part(eng, ready, parts, k, i, unit):
            if i < parts - 1:
                eng.wait_ge(ready, (parts - 1) * k + i + 1)
            else:
                eng.wait_ge(unit_used, unit + 1)

        samp_pad = xpad[:, :, PADP:].rearrange("p c (b j) -> p c b j", j=PADS)
        block = ctx.enter_context(nc.Block())

        @block.sync
        def _(sp):
            sp.dma_start(x_in[:, 0:2, :], x_prompt.rearrange("o (t p) d -> p (o t) d", p=P)).then_inc(x_loaded, 16)
            sp.dma_start(x_in[:, 2, :], x_sample.rearrange("b s d -> (b s) d")).then_inc(x_loaded, 16)
            for r, a in ((G1_R, norm1_g), (CBIAS_R, conv_b), (BRG_R, b_rg), (BIG_R, b_ig), (LAM_R, lru_lambda)):
                sp.dma_start(rows[r:r + CB, :], a.rearrange("o (c p) -> (o c) p", p=P)).then_inc(rows_loaded, 16)
            sp.dma_start(rows[CONVW_R:ROWS, :], conv_w.rearrange("o k (c p) -> (o k c) p", p=P)).then_inc(rows_loaded, 16)
            sp.dma_start(state_in[0:24, :], state_conv.rearrange("o b k d -> (o b k) d")).then_inc(rows_loaded, 16)
            sp.dma_start(state_in[24:32, :], state_h.rearrange("o b d -> (o b) d")).then_inc(rows_loaded, 16)
            for n in range(MIX_U):
                if n >= MIX_RING:
                    sp.wait_ge(low_done, n - MIX_RING + 1)
                sp.dma_start(raw[:, n % MIX_RING], mix_unit(n)).then_inc(mix_landed[n % MIX_RING], 16)
                if n == PA_U:
                    sp.wait_ge(v_ready, 1)
                    sp.dma_start(new_v_sample.rearrange("o b s d -> (o b s) d"), v[:, 2, :]).then_inc(stored, 16)
            sp.wait_ge(st_ready, 1)
            sp.dma_start(new_conv_prompt.rearrange("o b k d -> (o b k) d"), state_out[0:3, :]).then_inc(stored, 16)
            sp.dma_start(new_conv_sample.rearrange("o b k d -> (o b k) d"), state_out[3:27, :]).then_inc(stored, 16)
            sp.dma_start(new_h_prompt.rearrange("o b d -> (o b) d"), state_out[27:28, :]).then_inc(stored, 16)
            sp.dma_start(new_h_sample.rearrange("o b d -> (o b) d"), state_out[28:36, :]).then_inc(stored, 16)
            sp.wait_ge(yb_ready, MG)
            sp.wait_ge(stored, 5 * 16)
            sp.dma_start(y[:, 0:2, :], x_prompt.rearrange("o (t p) d -> p (o t) d", p=P)).then_inc(y_loaded, 16)
            sp.dma_start(y[:, 2, :], x_sample.rearrange("b s d -> (b s) d")).then_inc(y_loaded, 16)
            sp.wait_ge(low_done, MIX_U)

            def expert(it, e):
                for m in range(EXP_U):
                    sp.wait_ge(low_done, it * EXP_U + (MIX_U + m - RAW_RING + 1))
                    sp.dma_start(raw[:, m % RAW_RING], exp_unit(e, m)).then_inc(exp_landed[m % RAW_RING], 16)

            with sp.Fori(0, NE // 2) as g:
                for x in range(2):
                    expert(g * 2 + x, g * 2 + x)
            sp.wait_ge(route_ready, 1)
            rounds = sp.value_load(cnt_i[0:1, 0:1], min_val=1, max_val=TT)
            with sp.Fori(1, TT) as r:
                with sp.If(r < rounds):
                    with sp.Fori(0, NE // 2) as g:
                        for x in range(2):
                            expert(r * NE + (g * 2 + x), g * 2 + x)
                sp.nop()
            sp.wait_ge(low_done, rounds * (NE * EXP_U) + MIX_U)
            sp.dma_start(fnb[:], final_norm_g.rearrange("(o d) -> o d", o=1).broadcast_to([P, D])).then_inc(fnb_loaded, 16)
            sp.wait_ge(out_final, TT)
            sp.dma_start(y_prompt.rearrange("o (t p) d -> p (o t) d", p=P), y[:, 0:2, :]).then_inc(stored, 16)
            sp.dma_start(y_sample.rearrange("b s d -> (b s) d"), y[:, 2, :]).then_inc(stored, 16)
            sp.wait_ge(stored, 7 * 16)

        @block.gpsimd
        def _(pool):
            step = [0]

            def link(ins):
                step[0] += 1
                ins.then_inc(pool_step, 1)
                pool.wait_ge(pool_step, step[0])

            link(pool.memset(ident[:], 0.0))
            pool.affine_select(out=ident[:], in_=ident[:], compare_op=ALU.not_equal, fill=1.0, base=0,
                               pattern=[[-1, P]], channel_multiplier=1).then_inc(const_ready, 1)
            pool.memset(lruw[:], 0.0).then_inc(zeroed, 1)
            pool.memset(ws_raw[:, 1], 0.0).then_inc(zeroed, 1)
            pool.memset(xpad[:, :, 0:CW - 1], 0.0).then_inc(const_ready, 1)
            pool.wait_ge(zeroed, 2)
            pool.dma_start(ws_raw[:, 0], w_s.rearrange("o g t s -> t (o g) s")).then_inc(ws_loaded, 16)
            for b in range(ST):
                pool.dma_start(ws_raw[b * SF:(b + 1) * SF, 1, :, b * SF:(b + 1) * SF],
                               w_s[:, :, 0:SF, 0:SF].rearrange("o g t s -> t (o g) s")).then_inc(ws_loaded, 16)
            for k, w in enumerate((w_rg, w_ig)):
                for q in range(2):
                    pool.dma_start(lruw[64 * q:64 * q + 64, k, :, 64 * q:64 * q + 64],
                                   w.rearrange("o (c q) i j -> q i (o c) j", q=2)[q]).then_inc(lruw_loaded, 16)
            pool.dma_start(lng[:], ln_v_g.broadcast_to([P, DM])).then_inc(ln_loaded, 16)
            pool.dma_start(lnb[:], ln_v_b.broadcast_to([P, DM])).then_inc(ln_loaded, 16)
            pool.dma_start(bsb[:], b_s.broadcast_to([P, MG, P])).then_inc(ln_loaded, 16)
            link(pool.memset(tri[:], 1.0))
            link(pool.affine_select(out=tri[:], in_=tri[:], compare_op=ALU.is_gt, fill=0.0, base=0,
                                    pattern=[[1, P]], channel_multiplier=-1))
            link(pool.memset(ones_b[:], 1.0))
            for k in range(2):
                pool.wait_ge(ws_ready, k + 1)
                pool.affine_select(out=wst[:, k], in_=wst[:, k], compare_op=ALU.is_ge, fill=0.0, base=0,
                                   pattern=[[0, MG], [1, P]], channel_multiplier=-1).then_inc(const_ready, 1)
            pool.wait_ge(rows_copied, 1)
            link(pool.iota(iota_s[:], pattern=[[1, P]], base=0, channel_multiplier=0, allow_small_or_imprecise_dtypes=True))
            link(pool.iota(slot_p[:], pattern=[[0, 1]], base=0, channel_multiplier=1, allow_small_or_imprecise_dtypes=True))
            link(pool.memset(onehot[:], 0.0))
            link(pool.affine_select(out=onehot[:], in_=onehot[:], compare_op=ALU.not_equal, fill=1.0, base=0,
                                    pattern=[[-1, NE]], channel_multiplier=1))
            pool.affine_select(out=onehot[:], in_=onehot[:], compare_op=ALU.not_equal, fill=1.0, base=-NE,
                               pattern=[[-1, NE]], channel_multiplier=1).then_inc(const_ready, 1)
            pool.dma_start(brb[:], b_router.broadcast_to([P, NE])).then_inc(late_loaded, 16)
            pool.wait_ge(gates_mm, 4)
            pool.dma_start(n2b[:], norm2_g.broadcast_to([P, D])).then_inc(late_loaded, 16)
            pool.wait_ge(unit_used, PA_U)
            for k in range(2):
                pool.dma_start(bias_raw[k * NE:(k + 1) * NE, :], b_gate_up.rearrange("o e n -> (o e) n")).then_inc(bias_loaded, 16)
            pool.wait_ge(mrg_ready, CB)
            pool.dma_start(wr[:], w_router.rearrange("o (c p) e -> p (o c) e", p=P)).then_inc(late_loaded, 16)
            pool.dma_start(bdn[:], b_down.rearrange("o e n -> (o e) n")).then_inc(late_loaded, 16)

            pool.wait_ge(route_ready, 1)
            pool.wait_ge(const_ready, 5)

            def next_ranks(r):
                pool.wait_ge(sel_used, r * NE + 1)
                pool.sem_inc(ranks_seen, 1)
                pool.tensor_scalar(pos[:], pos[:], -float(P), None, ALU.add)
                pool.tensor_scalar(post[:], post[:].bitcast(F32), -float(P), None, ALU.add).then_inc(ranks_ready, 1)
                pool.wait_ge(ranks_ready, r + 1)
                pool.sem_inc(ranks_seen, 1)

            def pair(p_, g):
                pool.wait_ge(pick_used, p_ * 2 + 1)
                pool.tensor_copy(pos_e[:], pos[:, :, bass.ds(g * 2, 2)]).then_inc(column_ready, 1)
                pool.wait_ge(column_ready, p_ + 1)
                pool.sem_inc(column_seen, 1)
                for t in range(TT):
                    for x in range(2):
                        i_ = pool.tensor_scalar(pick[:, t, x, :], iota_s[:], pos_e[:, t, x:x + 1], None, ALU.is_equal)
                i_.then_inc(pick_ready, 1)
                for x in range(2):
                    pool.wait_ge(sel_used, p_ * 2 + (x + 1))
                    pool.tensor_copy(sel[:], onehot[:, bass.ds(g * 2 + x, 1)].broadcast_to([2 * NE, P])).then_inc(sel_ready, 1)

            next_ranks(0)
            with pool.Fori(0, NE // 2) as g:
                pair(g, g)
            rounds = pool.value_load(cnt_i[0:1, 0:1], min_val=1, max_val=TT)
            with pool.Fori(1, TT) as r:
                with pool.If(r < rounds):
                    next_ranks(r)
                    with pool.Fori(0, NE // 2) as g:
                        pair(r * (NE // 2) + g, g)
                pool.nop()

        @block.scalar
        def _(act):
            def high(n):
                act.wait_ge(mix_landed[n % MIX_RING], 16 * (n // MIX_RING + 1))
                if n >= MIX_SPLIT:
                    act.wait_ge(unit_used, n - MIX_SPLIT + 1)
                act.activation(split_h[:, n % MIX_SPLIT], raw[:, n % MIX_RING], ACT.Copy).then_inc(high_done, 1)

            act.wait_ge(x_loaded, 32)
            for t in range(TT):
                act.activation(xs[:, t, :], x_in[:, t, :], ACT.Square, accum_out=st8[:, t:t + 1]).then_inc(squared, 1)
            act.wait_ge(rstd_in, 1)
            act.activation(st8[:, 8:8 + TT], st8[:, 4:4 + TT], ACT.Sqrt).then_inc(rstd_out, 1)
            high(0)
            high(1)
            act.wait_ge(lam_in, 1)
            act.activation(st8[:, 24:32], st8[:, 16:24], ACT.Exp).then_inc(lam_exp, 1)
            act.wait_ge(lam_ln_in, 1)
            act.activation(st8[:, 40:48], st8[:, 32:40], ACT.Ln).then_inc(lam_ln, 1)
            act.wait_ge(rows_copied, 1)
            for c in range(CB):
                act.wait_ge(xs_turned, c + 1)
                act.activation(act_h[:, c, :], ps[:, c, 0:T], ACT.Identity, scale=cols[:, G1_R + c:G1_R + c + 1]).then_inc(xn_high, 1)
            high(2)

            def evacuate(c):
                for b in range(4):
                    wait_part(act, z_ready, 4, c, b, 2 * c + 1)
                    src = ps[:, 4 * (c % 3 % 2) + b, 0:T]
                    if c < 2:
                        act.activation(xpad[:, 4 * c + b, CW - 1:PADP], src[:, 0:SEQ], ACT.Identity)
                        act.activation(samp_pad[:, 4 * c + b, :, CW - 1:],
                                       src[:, SEQ:T].rearrange("p (b s) -> p b s", s=SF), ACT.Identity).then_inc(z_evac, 1)
                        continue
                    dst, func = {2: (ga[:, b], 0), 3: (ga[:, 4 + b], 0), 4: (u[:, b], 0), 5: (gate_a[:, b], 1),
                                 6: (gate_a[:, 4 + b], 1), 7: (gate_b[:, b], 1), 8: (gate_b[:, 4 + b], 1)}[c]
                    act.activation(dst, src, ACT.Sigmoid if func else ACT.Gelu_apprx_tanh).then_inc(z_evac, 1)

            for c in range(NZ):
                high(2 * c + 3)
                evacuate(c)
                high(2 * c + 4)

            def sigmoids(hf):
                for k, (dst, r) in enumerate(((lru_r, BRG_R), (lru_i, BIG_R))):
                    act.wait_ge(gates_mm, 2 * hf + k + 1)
                    for b in range(4):
                        bank = (4 * (k if hf == 0 else 1 - k)) + b
                        col = r + 4 * hf + b
                        if k == 0 and hf == 1 and b == 0:
                            act.wait_ge(st_packed, 1)
                        i_ = act.activation(dst[:, b], ps[:, bank, 0:T], ACT.Sigmoid, bias=cols[:, col:col + 1])
                    i_.then_inc(gates_read, 1)

            def decays(hf):
                act.wait_ge(lam_ready, 1)
                act.wait_ge(gates_read, 2 * hf + 1)
                for b in range(4):
                    act.activation(lru_a[:, b], lru_r[:, b], ACT.Exp, scale=st8[:, 48 + 4 * hf + b:49 + 4 * hf + b])
                for b in range(4):
                    i_ = act.activation(lru_r[:, b], lru_r[:, b], ACT.Tanh, scale=st8[:, 56 + 4 * hf + b:57 + 4 * hf + b])
                i_.then_inc(decay_ready, 1)

            def roots(hf):
                act.wait_ge(mult_in, hf + 1)
                act.activation(lru_r[:], lru_r[:], ACT.Sqrt).then_inc(mult_ready, 1)

            sigmoids(0)
            decays(0)
            roots(0)
            high(V_U + 3)
            for t in range(TT):
                wait_part(act, v_mm, TT, 0, t, V_U + 1)
                act.activation(v[:, t, :], ps[:, t, :], ACT.Gelu_apprx_tanh).then_inc(v_read, 1)
            high(V_U + 4)
            act.wait_ge(ln_in, 1)
            act.activation(st8[:, 12:15], st8[:, 8:11], ACT.Sqrt).then_inc(ln_out, 1)
            sigmoids(1)
            decays(1)
            roots(1)
            for n in range(V_U + 5, MIX_U):
                high(n)

            for t in range(TT):
                act.wait_ge(y_ready, TT + t + 1)
                if t:
                    act.wait_ge(sq2, t)
                act.activation(squares[:], y[:, t, :], ACT.Square, accum_out=rt[:, t:t + 1]).then_inc(sq2, 1)
            act.wait_ge(r2_in, 1)
            act.activation(rt[:, 8:8 + TT], rt[:, 4:4 + TT], ACT.Sqrt).then_inc(r2_out, 1)
            for t in range(TT):
                act.wait_ge(xn2_ready, t + 1)
                act.activation(xn_h[:, t, :], xn2[:, t, :], ACT.Copy).then_inc(xn2_high, 1)
            for t in range(TT):
                for half in range(2):
                    act.wait_ge(xn2_turned, 2 * t + half + 1)
                    act.activation(xnt[:, 4 * half:4 * half + 4, t * P:(t + 1) * P],
                                   ps[:, 2 * t + half, :].rearrange("p (c t) -> p c t", t=P), ACT.Copy).then_inc(xnt_ready, 1)
            act.wait_ge(top_ready, 1)
            for t in range(TT):
                i_ = act.activation(ex[:, t, 0:TOPK], mx[:, t, 0:TOPK], ACT.Exp, bias=rt[:, 16 + t:17 + t], accum_out=rt[:, 20 + t:21 + t])
            i_.then_inc(top_exp, 1)
            act.wait_ge(route_ready, 1)
            act.wait_ge(sel_used, 1)
            act.preload_act_table(ACT.Silu)
            act.activation(gslot[:], slot_p[:], ACT.Copy, scale=0.0).then_inc(gslot_ready, 1)

            def out_high_part(it, x):
                act.wait_ge(unit_used, it * EXP_U + MIX_U)
                act.wait_ge(gslot_ready, it + 1)
                act.activation(out_h[x][:], ps[:, 4:6, :].rearrange("p a b -> p (a b)"), ACT.Copy, scale=gslot[:, 0:1]).then_inc(out_high, 1)

            def expert(p_, x):
                it = p_ * 2 + x

                def high(m):
                    act.wait_ge(exp_landed[m % RAW_RING], it * (16 * EXP_U // RAW_RING) + 16 * (m // RAW_RING + 1))
                    act.wait_ge(unit_used, it * EXP_U + (MIX_U + m - SPLIT_RING + 1))
                    act.activation(split_h[:, m % SPLIT_RING], raw[:, m % RAW_RING], ACT.Copy).then_inc(high_done, 1)

                def silu(j):
                    act.wait_ge(clipped, it * 2 + (j + 1))
                    act.activation(sil[:], g1[:], ACT.Silu, scale=ALPHA).then_inc(silu_done, 1)

                def turned_high(j):
                    act.wait_ge(act_turned, it * 2 + (j + 1))
                    act.activation(at_h[:, 4 * j:4 * j + 4, :].rearrange("p c s -> p (c s)"), ps[:, 6 + j, :], ACT.Copy).then_inc(at_high, 1)

                for m in range(3):
                    high(m)
                if x == 0:
                    for k in range(2):
                        act.wait_ge(gathered, p_ * 4 + (k + 1))
                        act.activation(xt_h[:, 4 * k:4 * k + 4].rearrange("p c x s -> p (c x s)"),
                                       ps[:, 2 * k:2 * k + 2, :].rearrange("p a b -> p (a b)"), ACT.Copy).then_inc(xt_ready, 1)
                    high(3)
                out_high_part(it, 1 - x)
                for m in range(4 - x, 7):
                    high(m)
                silu(0)
                high(7)
                high(8)
                turned_high(0)
                high(9)
                high(10)
                silu(1)
                high(11)
                turned_high(1)
                act.wait_ge(pick_used, it + 2)
                act.activation(gslot[:], ps[:, 3, 0:1], ACT.Copy, scale=1.0 / ALPHA).then_inc(gslot_ready, 1)

            with act.Fori(0, NE // 2) as g:
                for x in range(2):
                    expert(g, x)
            rounds = act.value_load(cnt_i[0:1, 0:1], min_val=1, max_val=TT)
            with act.Fori(1, TT) as r:
                with act.If(r < rounds):
                    with act.Fori(0, NE // 2) as g:
                        for x in range(2):
                            expert(r * (NE // 2) + g, x)
                act.nop()
            out_high_part(rounds * NE, 1)
            for i, (t, _) in enumerate(COMBINE_BANKS):
                act.wait_ge(y_added, rounds * (NE // 2 * TT) + (i + 1))
                if i:
                    act.wait_ge(sq3, i)
                act.activation(squares3[:], y[:, t, :], ACT.Square, accum_out=rt[:, 32 + t:33 + t]).then_inc(sq3, 1)
            act.wait_ge(r3_in, 1)
            act.activation(rt[:, 40:40 + TT], rt[:, 36:36 + TT], ACT.Sqrt).then_inc(r3_out, 1)

        @block.vector
        def _(dve):
            step = [0]

            def link(ins):
                step[0] += 1
                ins.then_inc(dve_step, 1)
                dve.wait_ge(dve_step, step[0])

            def low(n):
                dve.wait_ge(high_done, n + 1)
                dve.tensor_tensor(split_l[:, n % MIX_SPLIT], raw[:, n % MIX_RING],
                                  split_h[:, n % MIX_SPLIT].bitcast(F32), ALU.subtract).then_inc(low_done, 1)

            dve.wait_ge(squared, TT)
            link(dve.tensor_scalar(st8[:, 4:4 + TT], st8[:, 0:TT], 1.0 / D, RMS_EPS, ALU.mult, ALU.add))
            dve.reciprocal(st8[:, 4:4 + TT], st8[:, 4:4 + TT]).then_inc(rstd_in, 1)
            dve.wait_ge(rstd_out, 1)
            for t in range(TT):
                dve.tensor_scalar(xs[:, t, :], x_in[:, t, :], st8[:, 8 + t:9 + t], None, ALU.mult).then_inc(xs_ready, 1)
            dve.wait_ge(rows_turned, 1)
            link(dve.tensor_copy(cols[:], ps[:, 0, 0:ROWS]))
            turned = ps[:, 1, 0:CB * 32].rearrange("p (c r) -> p c r", r=32)
            dve.tensor_copy(samp_pad[:, :, :, 0:CW - 1], turned[:, :, 0:24].rearrange("p c (b k) -> p c b k", k=CW - 1))
            dve.tensor_copy(h0, turned[:, :, 24:32]).then_inc(rows_copied, 1)
            lam, neg, pos_, one, dif = cols[:, LAM_R:LAM_R + CB], st8[:, 16:24], lam8[:, 0:8], st8[:, 32:40], lam8[:, 8:16]
            link(dve.tensor_scalar(neg, lam, -1.0, None, ALU.mult))
            link(dve.tensor_scalar(pos_, neg, 0.0, None, ALU.max))
            dve.tensor_tensor(neg, neg, lam, ALU.min).then_inc(lam_in, 1)
            dve.wait_ge(lam_exp, 1)
            dve.tensor_scalar(one, st8[:, 24:32], 1.0, None, ALU.add).then_inc(lam_ln_in, 1)
            dve.wait_ge(lam_ln_in, 1)
            link(dve.tensor_scalar(dif, one, -1.0, None, ALU.add))
            link(dve.scalar_tensor_tensor(out=lam8[:, 16:24], in0=dif, scalar=0.0, in1=st8[:, 24:32], op0=ALU.is_equal, op1=ALU.mult))
            link(dve.tensor_scalar(dif, dif, 1e-30, None, ALU.max))
            link(dve.reciprocal(dif, dif))
            link(dve.tensor_tensor(dif, dif, st8[:, 24:32], ALU.mult))
            dve.wait_ge(lam_ln, 1)
            link(dve.tensor_tensor(dif, dif, st8[:, 40:48], ALU.mult))
            link(dve.tensor_tensor(dif, dif, lam8[:, 16:24], ALU.add))
            link(dve.tensor_tensor(dif, dif, pos_, ALU.add))
            dve.tensor_scalar(st8[:, 48:56], dif, -8.0, None, ALU.mult)
            dve.tensor_scalar(st8[:, 56:64], dif, 8.0, None, ALU.mult).then_inc(lam_ready, 1)
            for k in range(2):
                dve.wait_ge(ws_turned, k + 1)
                dve.tensor_copy(wst[:, k].rearrange("p g t -> p (g t)"), ps[:, 2 + k, :]).then_inc(ws_ready, 1)
            low(0)
            low(1)
            for c in range(CB):
                dve.wait_ge(xn_high, c + 1)
                i_ = dve.scalar_tensor_tensor(out=act_l[:, c, :], in0=ps[:, c, 0:T], scalar=cols[:, G1_R + c:G1_R + c + 1],
                                              in1=act_h[:, c, :].bitcast(F32), op0=ALU.mult, op1=ALU.subtract)
                i_.then_inc(xn_ready, 1)
            dve.wait_ge(xn_ready, CB)
            dve.nop().then_inc(z_evac, 4)
            low(2)

            def conv(k):
                for c in range(CB):
                    wk = cols[:, CONVW_R + CB * k + c:CONVW_R + CB * k + c + 1]
                    for src, dst in ((xpad[:, c, k:k + SEQ], xc[:, c, 0:SEQ]),
                                     (samp_pad[:, c, :, k:k + SF], xc[:, c, SEQ:T].rearrange("p (b s) -> p b s", s=SF))):
                        if k == 0:
                            i_ = dve.tensor_scalar(dst, src, wk, cols[:, CBIAS_R + c:CBIAS_R + c + 1], ALU.mult, ALU.add)
                        else:
                            i_ = dve.scalar_tensor_tensor(out=dst, in0=src, scalar=wk, in1=dst, op0=ALU.mult, op1=ALU.add)
                link(i_)

            for c in range(NZ):
                low(2 * c + 3)
                if c == 2:
                    dve.wait_ge(z_evac, 4 + 8)
                    dve.wait_ge(const_ready, 2)
                    conv(0)
                if c in (3, 4, 5):
                    conv(c - 2)
                if c == 5:
                    dve.nop().then_inc(conv_done, 1)
                    dve.tensor_copy(pack[:, :, 0:3], xpad[:, :, SEQ:PADP])
                    dve.tensor_copy(pack[:, :, 3:27].rearrange("p c (b k) -> p c b k", k=CW - 1), samp_pad[:, :, :, SF:])
                low(2 * c + 4)

            def lru(hf):
                cs = slice(4 * hf, 4 * hf + 4)
                dve.wait_ge(gates_read, 2 * hf + 2)
                link(dve.tensor_tensor(lru_i[:], lru_i[:], xc[:, cs], ALU.mult))
                dve.wait_ge(decay_ready, hf + 1)
                link(dve.tensor_tensor(tmp[:], lru_a[:], lru_a[:], ALU.mult))
                link(dve.scalar_tensor_tensor(out=lru_r[:], in0=tmp[:], scalar=1.0, in1=lru_r[:], op0=ALU.add, op1=ALU.mult))
                dve.tensor_scalar(lru_r[:], lru_r[:], 0.0, None, ALU.max).then_inc(mult_in, 1)
                dve.wait_ge(mult_ready, hf + 1)
                link(dve.memset(lru_r[:, :, 0:1], 1.0))
                link(dve.tensor_tensor(lru_i[:], lru_i[:], lru_r[:], ALU.mult))
                first_a = lru_a[:, :, SEQ:T].rearrange("p c (b s) -> p c b s", s=SF)[:, :, :, 0]
                first_i = lru_i[:, :, SEQ:T].rearrange("p c (b s) -> p c b s", s=SF)[:, :, :, 0]
                link(dve.tensor_tensor(tmp[:, :, 0:ST], first_a, h0[:, cs, :], ALU.mult))
                link(dve.tensor_tensor(first_i, first_i, tmp[:, :, 0:ST], ALU.add))
                dve.memset(first_a, 0.0)
                link(dve.memset(lru_a[:, :, 0:1], 0.0))
                link(dve.tensor_tensor_scan(xc[:, cs].rearrange("p c t -> p (c t)"), lru_a[:].rearrange("p c t -> p (c t)"),
                                            lru_i[:].rearrange("p c t -> p (c t)"), 0.0, ALU.mult, ALU.add))
                dve.tensor_copy(pack[:, cs, 27:28], xc[:, cs, SEQ - 1:SEQ])
                dve.tensor_copy(pack[:, cs, 28:36], xc[:, cs, SEQ:T].rearrange("p c (b s) -> p c b s", s=SF)[:, :, :, SF - 1]).then_inc(st_packed, 1)
                link(dve.tensor_tensor(tmp[:], xc[:, cs], ga[:, cs], ALU.mult))

            def lru_split(hf):
                cs = slice(4 * hf, 4 * hf + 4)
                dve.wait_ge(unit_used, PB_U)
                link(dve.tensor_copy(act_h[:, cs], tmp[:]))
                dve.tensor_tensor(act_l[:, cs], tmp[:], act_h[:, cs].bitcast(F32), ALU.subtract).then_inc(lru_ready, 1)
                dve.wait_ge(lru_ready, hf + 1)

            lru(0)
            low(V_U + 3)
            for t in range(TT):
                dve.wait_ge(v_read, t + 1)
                i_ = dve.bn_stats(bn[:, t, :], v[:, t, :])
            link(i_)
            for t in range(TT):
                i_ = dve.bn_aggr(bnm[:, t, :], bn[:, t, :])
            link(i_)
            link(dve.tensor_scalar(st8[:, 8:8 + TT], bnm[:, :, 1], LN_EPS, None, ALU.add))
            dve.reciprocal(st8[:, 8:8 + TT], st8[:, 8:8 + TT]).then_inc(ln_in, 1)
            dve.wait_ge(ln_out, 1)
            for t in range(TT):
                i_ = dve.tensor_scalar(v[:, t, :], v[:, t, :], bnm[:, t, 0:1], st8[:, 12 + t:13 + t], ALU.subtract, ALU.mult)
            link(i_)
            dve.wait_ge(ln_loaded, 48)
            link(dve.tensor_tensor(v[:], v[:], lng[:].unsqueeze(1).broadcast_to([P, TT, DM]), ALU.mult))
            dve.tensor_tensor(v[:], v[:], lnb[:].unsqueeze(1).broadcast_to([P, TT, DM]), ALU.add).then_inc(v_ready, 1)
            lru_split(0)
            low(V_U + 4)
            for g in range(MG):
                dve.wait_ge(vmix_mm, g + 1)
                s_p = tmp[:, g % 2, :]
                dve.tensor_tensor(s_p[:, 0:SEQ].rearrange("p (n t) -> p n t", t=P), ps[:, g, 0:SEQ].rearrange("p (n t) -> p n t", t=P),
                                  bsb[:, g, :].unsqueeze(1).broadcast_to([P, 2, P]), ALU.add)
                link(dve.tensor_tensor(s_p[:, SEQ:T].rearrange("p (b s) -> p b s", s=SF), ps[:, g, SEQ:T].rearrange("p (b s) -> p b s", s=SF),
                                       bsb[:, g, 0:SF].unsqueeze(1).broadcast_to([P, ST, SF]), ALU.add))
                link(dve.tensor_tensor(s_p, s_p, u[:, g, :], ALU.mult))
                link(dve.tensor_copy(yb_h[:, g, :], s_p))
                dve.tensor_tensor(yb_l[:, g, :], s_p, yb_h[:, g, :].bitcast(F32), ALU.subtract).then_inc(yb_ready, 1)
            lru(1)
            lru_split(1)
            low(V_U + 5)
            for k in range(2):
                for b in range(4):
                    wait_part(dve, pb_mm, 4, k, b, PB_U + k)
                    i_ = dve.tensor_tensor(gate_b[:, 4 * k + b, :], gate_b[:, 4 * k + b, :], ps[:, 4 * (1 - k) + b, 0:T], ALU.mult)
                    i_.then_inc(pb_read, 1)
                low(V_U + 6 + k)
            for k in range(2):
                for b in range(4):
                    c = 4 * k + b
                    wait_part(dve, pa_mm, 4, k, b, PA_U + 2 * k + 1)
                    link(dve.tensor_tensor(gate_a[:, c, :], gate_a[:, c, :], ps[:, 4 * (1 - k) + b, 0:T], ALU.mult))
                    if c == 0:
                        dve.wait_ge(pb_read, CB)
                    link(dve.tensor_tensor(gate_a[:, c, :], gate_a[:, c, :], gate_b[:, c, :], ALU.add))
                    link(dve.tensor_copy(mrg_h[:, c, :], gate_a[:, c, :]))
                    dve.tensor_tensor(mrg_l[:, c, :], gate_a[:, c, :], mrg_h[:, c, :].bitcast(F32), ALU.subtract).then_inc(mrg_ready, 1)
                low(V_U + 8 + 2 * k)
                low(V_U + 9 + 2 * k)
            for k in range(2):
                dve.wait_ge(st_turned, k + 1)
                i_ = dve.tensor_copy(state_out[:, 512 * k:512 * k + 512], ps[0:36, 4 * k + 3, :])
            i_.then_inc(st_ready, 1)
            dve.wait_ge(y_loaded, 32)
            for k in range(2):
                for t in range(TT):
                    wait_part(dve, wo_mm, TT, k, t, WO_U + 2 * k + 1)
                    dve.tensor_tensor(y[:, t, UC * k:UC * k + UC], y[:, t, UC * k:UC * k + UC], ps[:, 4 * (1 - k) + t, :],
                                      ALU.add).then_inc(y_ready, 1)
            dve.wait_ge(bias_loaded, 32)
            link(dve.tensor_copy(bias_hl[:], bias_raw[:]))
            dve.tensor_tensor(bias_hl[NE:2 * NE, :], bias_raw[NE:2 * NE, :], bias_hl[NE:2 * NE, :].bitcast(F32), ALU.subtract)
            dve.wait_ge(sq2, TT)
            link(dve.tensor_scalar(rt[:, 4:4 + TT], rt[:, 0:TT], 1.0 / D, RMS_EPS, ALU.mult, ALU.add))
            dve.reciprocal(rt[:, 4:4 + TT], rt[:, 4:4 + TT]).then_inc(r2_in, 1)
            dve.wait_ge(r2_out, 1)
            dve.wait_ge(late_loaded, 4 * 16)
            for t in range(TT):
                dve.scalar_tensor_tensor(out=xn2[:, t, :], in0=y[:, t, :], scalar=rt[:, 8 + t:9 + t], in1=n2b[:],
                                         op0=ALU.mult, op1=ALU.mult).then_inc(xn2_ready, 1)
            for t in range(TT):
                dve.wait_ge(xn2_high, t + 1)
                i_ = dve.tensor_tensor(xn_l[:, t, :], xn2[:, t, :], xn_h[:, t, :].bitcast(F32), ALU.subtract)
            i_.then_inc(xn2_low, 1)
            dve.wait_ge(logits_mm, 1)
            link(dve.tensor_tensor(lg[:], ps[:, 6, 0:TT * NE].rearrange("p (t e) -> p t e", e=NE),
                                   brb[:].unsqueeze(1).broadcast_to([P, TT, NE]), ALU.add))
            for t in range(TT):
                i_ = dve.max(mx[:, t, :], lg[:, t, :])
            link(i_)
            dve.tensor_scalar(rt[:, 16:16 + TT], mx[:, :, 0], -1.0, None, ALU.mult).then_inc(top_ready, 1)
            for t in range(TT):
                i_ = dve.max_index(ix[:, t, :], mx[:, t, :], lg[:, t, :])
            link(i_)
            link(dve.tensor_copy(ixf[:], ix[:]))
            dve.wait_ge(top_exp, 1)
            link(dve.reciprocal(rt[:, 24:24 + TT], rt[:, 20:20 + TT]))
            for t in range(TT):
                i_ = dve.tensor_scalar(ex[:, t, 0:TOPK], ex[:, t, 0:TOPK], rt[:, 24 + t:25 + t], None, ALU.mult)
            link(i_)
            for t in range(TT):
                for k in range(TOPK):
                    i_ = dve.tensor_scalar(oh[:, t, k, :], iota_s[:, 0:NE], ixf[:, t, k:k + 1], ex[:, t, k:k + 1], ALU.is_equal, ALU.mult)
            link(i_)
            link(dve.tensor_reduce(gat[:], oh[:].rearrange("p t k e -> p t e k"), AX_X, ALU.add))
            link(dve.tensor_scalar(maskf[:], gat[:], 0.0, None, ALU.is_gt))
            dve.tensor_copy(mask[:], maskf[:]).then_inc(mask_ready, 1)
            link(dve.tensor_scalar(maskf[:], maskf[:], FAR, P - FAR, ALU.mult, ALU.add))
            dve.wait_ge(pos_mm, 1)
            link(dve.tensor_tensor(pos[:], maskf[:], ps[:, 7, 0:TT * NE].rearrange("p (t e) -> p t e", e=NE), ALU.add))
            link(dve.tensor_reduce(cnt[0:1, 0:1], ps[0:1, 7, TT * NE:(TT + 1) * NE], AX_X, ALU.max))
            link(dve.tensor_scalar(cnt[0:1, 1:2], cnt[0:1, 0:1], float(P), 1.0, ALU.is_gt, ALU.add))
            link(dve.tensor_scalar(cnt[0:1, 2:3], cnt[0:1, 0:1], 2.0 * P, None, ALU.is_gt))
            link(dve.tensor_tensor(cnt[0:1, 3:4], cnt[0:1, 1:2], cnt[0:1, 2:3], ALU.add))
            dve.tensor_copy(cnt_i[0:1, 0:1], cnt[0:1, 3:4]).then_inc(pos_ready, 1)
            dve.wait_ge(post_mm, 1)
            dve.tensor_copy(post[:], ps[0:NE, 5, 0:T])
            dve.tensor_copy(gat_t[:], ps[0:NE, 4, 0:T]).then_inc(gat_ready, 1)
            dve.memset(pick_t[:, 1].bitcast(F32), 0.0).then_inc(pick_t_ready, 1)
            dve.wait_ge(gat_ready, 1)
            dve.wait_ge(pos_ready, 1)
            for t in range(TT):
                dve.wait_ge(bd_mm, t + 1)
                i_ = dve.tensor_tensor(y[:, t, :], y[:, t, :], ps[:, 2 * t:2 * t + 2, :].rearrange("p a b -> p (a b)"), ALU.add)
            i_.then_inc(route_ready, 1)
            dve.wait_ge(route_ready, 1)

            def out_low_part(it, x):
                dve.wait_ge(out_high, it + 1)
                dve.scalar_tensor_tensor(out=out_l[x][:], in0=ps[:, 4:6, :].rearrange("p a b -> p (a b)"), scalar=gslot[:, 0:1],
                                         in1=out_h[x][:].bitcast(F32), op0=ALU.mult, op1=ALU.subtract).then_inc(out_ready, 1)

            def add_to_tokens(p_, i):
                t, bank = COMBINE_BANKS[i]
                dve.wait_ge(combined, p_ * TT + (i + 1))
                dve.tensor_tensor(y[:, t, :], y[:, t, :], ps[:, bank:bank + 2, :].rearrange("p a b -> p (a b)"),
                                  ALU.add).then_inc(y_added, 1)

            def expert(p_, x):
                it = p_ * 2 + x

                def low(m):
                    dve.wait_ge(high_done, it * EXP_U + (MIX_U + m + 1))
                    dve.tensor_tensor(split_l[:, m % SPLIT_RING], raw[:, m % RAW_RING],
                                      split_h[:, m % SPLIT_RING].bitcast(F32), ALU.subtract).then_inc(low_done, 1)

                def clip(j):
                    gate_bank = (2, 0)[j]
                    dve.wait_ge(unit_used, it * EXP_U + (MIX_U + 4 * (j + 1)))
                    dve.tensor_scalar(g1[:], ps[:, gate_bank, :], LIMIT, None, ALU.min).then_inc(clipped, 1)
                    dve.tensor_scalar(u1[:], ps[:, gate_bank + 1, :], LIMIT, -LIMIT, ALU.min, ALU.max).then_inc(up_clipped, 1)

                def product(j):
                    dve.wait_ge(up_clipped, it * 2 + (j + 1))
                    dve.wait_ge(silu_done, it * 2 + (j + 1))
                    dve.scalar_tensor_tensor(out=actv[:, UC * j:UC * j + UC], in0=u1[:], scalar=1.0, in1=sil[:],
                                             op0=ALU.add, op1=ALU.mult).then_inc(act_ready, 1)

                def turned_low(j):
                    dve.wait_ge(at_high, it * 2 + (j + 1))
                    dve.tensor_tensor(at_l[:, 4 * j:4 * j + 4, :].rearrange("p c s -> p (c s)"), ps[:, 6 + j, :],
                                      at_h[:, 4 * j:4 * j + 4, :].rearrange("p c s -> p (c s)").bitcast(F32),
                                      ALU.subtract).then_inc(at_ready, 1)

                low(0)
                low(1)
                if x == 0:
                    low(2)
                    for k in range(2):
                        dve.wait_ge(gathered, p_ * 4 + (k + 3))
                        dve.tensor_copy(xt_l[:, 4 * k:4 * k + 4].rearrange("p c x s -> p (c x s)"),
                                        ps[:, 2 * k:2 * k + 2, :].rearrange("p a b -> p (a b)")).then_inc(xt_low_ready, 1)
                    low(3)
                    out_low_part(it, 1 - x)
                else:
                    out_low_part(it, 1 - x)
                    add_to_tokens(p_, 0)
                    low(2)
                    add_to_tokens(p_, 1)
                    low(3)
                    add_to_tokens(p_, 2)
                for m in range(4, 7):
                    low(m)
                clip(0)
                product(0)
                low(7)
                low(8)
                turned_low(0)
                low(9)
                clip(1)
                product(1)
                low(10)
                turned_low(1)
                low(11)
                dve.wait_ge(sel_used, it + 2)
                dve.tensor_scalar(pick_t[:, x], ps[:, 2, 0:T], slot_p[:, 0:1], None, ALU.is_equal).then_inc(pick_t_ready, 1)

            with dve.Fori(0, NE // 2) as g:
                for x in range(2):
                    expert(g, x)
            rounds = dve.value_load(cnt_i[0:1, 0:1], min_val=1, max_val=TT)
            with dve.Fori(1, TT) as r:
                with dve.If(r < rounds):
                    with dve.Fori(0, NE // 2) as g:
                        for x in range(2):
                            expert(r * (NE // 2) + g, x)
                dve.nop()
            out_low_part(rounds * NE, 1)
            for i in range(TT):
                add_to_tokens(rounds * (NE // 2), i)
            dve.wait_ge(sq3, TT)
            dve.tensor_scalar(rt[:, 36:36 + TT], rt[:, 32:32 + TT], 1.0 / D, RMS_EPS, ALU.mult, ALU.add).then_inc(r3_mean, 1)
            dve.wait_ge(r3_mean, 1)
            dve.reciprocal(rt[:, 36:36 + TT], rt[:, 36:36 + TT]).then_inc(r3_in, 1)
            dve.wait_ge(r3_out, 1)
            dve.wait_ge(fnb_loaded, 16)
            for t in range(TT):
                dve.scalar_tensor_tensor(out=y[:, t, :], in0=y[:, t, :], scalar=rt[:, 40 + t:41 + t], in1=fnb[:],
                                         op0=ALU.mult, op1=ALU.mult).then_inc(out_final, 1)

        @block.tensor
        def _(pe):
            def three(out, a_h, a_l, b_h, b_l, start, stop):
                pe.matmul(out, a_h, b_h, start=start, stop=False)
                pe.matmul(out, a_h, b_l, start=False, stop=False)
                return pe.matmul(out, a_l, b_h, start=False, stop=stop)

            pe.wait_ge(const_ready, 1)
            pe.wait_ge(rows_loaded, 8 * 16)
            pe.transpose(ps[:, 0, 0:ROWS], rows[:], ident[0:ROWS, 0:ROWS])
            for c in range(CB):
                i_ = pe.transpose(ps[:, 1, 32 * c:32 * c + 32], state_in[:, c * P:(c + 1) * P], ident[0:32, 0:32])
            i_.then_inc(rows_turned, 1)
            pe.wait_ge(ws_loaded, 16 * (1 + ST))
            for k in range(2):
                for g in range(MG):
                    i_ = pe.transpose(ps[:, 2 + k, g * P:(g + 1) * P], ws_raw[:, k, g, :], ident[:])
                i_.then_inc(ws_turned, 1)
            for c in range(CB):
                if c == 0:
                    pe.wait_ge(rows_copied, 1)
                    pe.wait_ge(xs_ready, TT)
                if c == 2:
                    pe.wait_ge(ws_ready, 2)
                for t in range(TT):
                    i_ = pe.transpose(ps[:, c, t * P:(t + 1) * P], xs[:, t, c * P:(c + 1) * P], ident[:])
                i_.then_inc(xs_turned, 1)
            pe.wait_ge(xn_ready, CB)

            def channel_unit(slot, k_blocks, bank, act_hl, start, stop, ready=None, before=None):
                x_h, x_l = act_hl
                for b in range(4):
                    if before:
                        before(b)
                    for j in range(KB):
                        cols_ = slice(b * P, (b + 1) * P)
                        i_ = three(ps[:, bank + b, 0:T], split_h[:, slot, j, cols_], split_l[:, slot, j, cols_],
                                   x_h[:, k_blocks + j, :], x_l[:, k_blocks + j, :], start and j == 0, stop and j == KB - 1)
                    if b == 3:
                        i_.then_inc(unit_used, 1)
                    elif ready:
                        i_.then_inc(ready, 1)

            with pe.Fori(0, NZ // 3) as g:
                for c in range(3):
                    for h in range(2):
                        pe.wait_ge(low_done, g * 6 + (2 * c + h + 1))

                        def bank_free(b):
                            if h == 0 and c != 1:
                                pe.wait_ge(z_evac, g * 12 + (b + 1 + (4 if c == 2 else 0)))
                        channel_unit((2 * c + h) % MIX_SPLIT, KB * h, 4 * (c % 2), (act_h, act_l), h == 0, h == 1,
                                     z_ready if h else None, bank_free)

            def lru_gates(hf):
                for k in range(2):
                    bank = 4 * (k if hf == 0 else 1 - k)
                    if hf == 0:
                        pe.wait_ge(z_evac, 4 * (NZ + 1))
                    else:
                        pe.wait_ge(gates_read, 2)
                        pe.wait_ge(v_read, TT)
                    for b in range(4):
                        i_ = pe.matmul(ps[:, bank + b, 0:T], lruw[:, k, 4 * hf + b, :], xc_view[:, 4 * hf + b, :], start=True, stop=True)
                    i_.then_inc(gates_mm, 1)

            xc_view = xc
            pe.wait_ge(conv_done, 1)
            pe.wait_ge(lruw_loaded, 64)
            lru_gates(0)
            pe.wait_ge(gates_read, 1)
            for h in range(2):
                n = V_U + h
                pe.wait_ge(low_done, n + 1)
                for t in range(TT):
                    for j in range(KB):
                        ts_ = slice(t * P, (t + 1) * P)
                        i_ = three(ps[:, t, :], act_h[:, KB * h + j, ts_], act_l[:, KB * h + j, ts_],
                                   split_h[:, n % MIX_SPLIT, j, :], split_l[:, n % MIX_SPLIT, j, :],
                                   h == 0 and j == 0, h == 1 and j == KB - 1)
                    if t == TT - 1:
                        i_.then_inc(unit_used, 1)
                    elif h:
                        i_.then_inc(v_mm, 1)
            lru_gates(1)
            pe.wait_ge(v_ready, 1)
            pe.wait_ge(const_ready, 4)
            pe.wait_ge(gates_read, 4)
            for g in range(MG):
                for t in range(TT):
                    i_ = pe.matmul(ps[:, g, t * P:(t + 1) * P], v[:, t, g * P:(g + 1) * P], wst[:, t // 2, g, :], start=True, stop=True)
                i_.then_inc(vmix_mm, 1)
            pe.wait_ge(yb_ready, MG)
            for k in range(2):
                pe.wait_ge(low_done, PB_U + k + 1)
                channel_unit((PB_U + k) % MIX_SPLIT, 0, 4 * (1 - k), (yb_h, yb_l), True, True, pb_mm)
            pe.wait_ge(lru_ready, 2)
            for k in range(2):
                for h in range(2):
                    n = PA_U + 2 * k + h
                    pe.wait_ge(low_done, n + 1)
                    channel_unit(n % MIX_SPLIT, KB * h, 4 * (1 - k), (act_h, act_l), h == 0, h == 1, pa_mm if h else None,
                                 (lambda b: pe.wait_ge(pb_read, 4 * k + b + 1)) if h == 0 else None)
            pe.wait_ge(mrg_ready, CB)
            pe.wait_ge(st_packed, 2)
            for c in range(CB):
                i_ = pe.transpose(ps[0:36, 4 * (c // 4) + 3, (c % 4) * P:(c % 4 + 1) * P], pack[:, c, :], ident[:])
                if c % 4 == 3:
                    i_.then_inc(st_turned, 1)
            for k in range(2):
                for h in range(2):
                    n = WO_U + 2 * k + h
                    pe.wait_ge(low_done, n + 1)
                    for t in range(TT):
                        for j in range(KB):
                            ts_ = slice(t * P, (t + 1) * P)
                            i_ = three(ps[:, 4 * (1 - k) + t, :], mrg_h[:, KB * h + j, ts_], mrg_l[:, KB * h + j, ts_],
                                       split_h[:, n % MIX_SPLIT, j, :], split_l[:, n % MIX_SPLIT, j, :],
                                       h == 0 and j == 0, h == 1 and j == KB - 1)
                        if t == TT - 1:
                            i_.then_inc(unit_used, 1)
                        elif h:
                            i_.then_inc(wo_mm, 1)
            pe.wait_ge(y_ready, 2 * TT)
            for t in range(TT):
                pe.wait_ge(xn2_ready, t + 1)
                for c in range(CB):
                    i_ = pe.transpose(ps[:, 2 * t + c // 4, (c % 4) * P:(c % 4 + 1) * P], xn2[:, t, c * P:(c + 1) * P], ident[:])
                    if c % 4 == 3:
                        i_.then_inc(xn2_turned, 1)
            for t in range(TT):
                pe.wait_ge(xnt_ready, 2 * (t + 1))
                for c in range(CB):
                    i_ = pe.matmul(ps[:, 6, t * NE:(t + 1) * NE], xnt[:, c, t * P:(t + 1) * P], wr[:, c, :], start=c == 0, stop=c == CB - 1)
            i_.then_inc(logits_mm, 1)
            pe.wait_ge(mask_ready, 1)
            pe.wait_ge(st_ready, 1)
            for t in range(TT):
                for s_ in range(t + 1):
                    pe.matmul(ps[:, 7, t * NE:(t + 1) * NE], tri[:] if s_ == t else ones_b[:], mask[:, s_, :], start=s_ == 0, stop=s_ == t)
            for t in range(TT):
                i_ = pe.matmul(ps[:, 7, TT * NE:(TT + 1) * NE], ones_b[:], mask[:, t, :], start=t == 0, stop=t == TT - 1)
            i_.then_inc(pos_mm, 1)
            pe.wait_ge(pos_ready, 1)
            for t in range(TT):
                pe.transpose(ps[0:NE, 5, t * P:(t + 1) * P], pos[:, t, :], ident[:])
                i_ = pe.transpose(ps[0:NE, 4, t * P:(t + 1) * P], gat[:, t, :], ident[:])
            i_.then_inc(post_mm, 1)
            pe.wait_ge(gat_ready, 1)
            for t in range(TT):
                for k in range(2):
                    i_ = pe.matmul(ps[:, 2 * t + k, :], gat_t[:, t * P:(t + 1) * P], bdn[:, UC * k:UC * k + UC], start=True, stop=True)
                i_.then_inc(bd_mm, 1)
            pe.wait_ge(route_ready, 1)
            pe.wait_ge(pick_t_ready, 1)
            pe.wait_ge(xn2_high, TT)
            pe.wait_ge(xn2_low, 1)
            pe.matmul(ps[:, 4, :], pick_t[:, 1, 0:P], xn_h[:, 0, 0:UC], start=True, stop=True).then_inc(pick_used, 1)
            pe.matmul(ps[:, 5, :], pick_t[:, 1, 0:P], xn_h[:, 0, 0:UC], start=True, stop=True).then_inc(sel_used, 1)

            def combine(t, bank, x, start, stop):
                for k in range(2):
                    pe.matmul(ps[:, bank + k, :], pick_t[:, x, t * P:(t + 1) * P], out_h[x][:, UC * k:UC * k + UC], start=start, stop=False)
                    i_ = pe.matmul(ps[:, bank + k, :], pick_t[:, x, t * P:(t + 1) * P], out_l[x][:, UC * k:UC * k + UC], start=False, stop=stop)
                return i_

            def gather(p_):
                pe.wait_ge(pick_ready, p_ + 1)
                for k in range(4):
                    if k == 1:
                        pe.wait_ge(pick_t_ready, p_ * 2 + 1)
                        pe.wait_ge(gslot_ready, p_ * 2 + 1)
                    if k >= 2:
                        pe.wait_ge(xt_ready, p_ * 2 + (k - 1))
                    for c in range(4):
                        for t in range(TT):
                            c_ = 4 * (k % 2) + c
                            i_ = pe.matmul(ps[:, 2 * (k % 2) + c // 2, c % 2 * 2 * P:(c % 2 + 1) * 2 * P],
                                           (xn_h, xn_l)[k // 2][:, t, c_ * P:(c_ + 1) * P],
                                           pick[:, t].rearrange("p x s -> p (x s)"), start=t == 0, stop=t == TT - 1)
                    i_.then_inc(gathered, 1)

            def expert(p_, x, e):
                it = p_ * 2 + x

                def unit(m, bank, x_h, x_l, first, last, midway=None):
                    pe.wait_ge(low_done, it * EXP_U + (MIX_U + m + 1))
                    k0 = KB * (m % 2 if m < 8 else (m - 8) // 2)
                    for j in range(KB):
                        if midway and j == KB // 2:
                            midway()
                        i_ = three(ps[:, bank, :], x_h[:, k0 + j, :], x_l[:, k0 + j, :], split_h[:, m % SPLIT_RING, j, :],
                                   split_l[:, m % SPLIT_RING, j, :], first and j == 0, last and j == KB - 1)
                    i_.then_inc(unit_used, 1)

                def linear(m, bank, bias_col):
                    if x == 0 and m == 0:
                        pe.wait_ge(xt_low_ready, p_ * 2 + 2)
                    pe.matmul(ps[:, bank, :], sel[:], bias_hl[:, bias_col:bias_col + UC], start=True, stop=False)
                    unit(m, bank, xt_h[:, :, x], xt_l[:, :, x], False, False)
                    unit(m + 1, bank, xt_h[:, :, x], xt_l[:, :, x], False, True)

                def turn(j):
                    pe.wait_ge(act_ready, it * 2 + (j + 1))
                    for c in range(4):
                        i_ = pe.transpose(ps[:, 6 + j, c * P:(c + 1) * P], actv[:, UC * j + c * P:UC * j + (c + 1) * P], ident[:])
                    i_.then_inc(act_turned, 1)

                if x == 0:
                    gather(p_)
                else:
                    pe.wait_ge(out_ready, p_ * 2 + 1)
                    pe.wait_ge(pick_t_ready, p_ * 2 + 2)
                    pe.wait_ge(gslot_ready, p_ * 2 + 2)
                    for t, bank in COMBINE_BANKS[::-1]:
                        combine(t, bank, 1, True, False)
                    pe.wait_ge(out_ready, p_ * 2 + 2)
                    for t, bank in COMBINE_BANKS:
                        combine(t, bank, 0, False, True).then_inc(combined, 1)
                    pe.wait_ge(y_added, p_ * TT + 1)
                pe.wait_ge(sel_ready, it + 1)
                linear(0, 2, 0)
                linear(2, 3, D)
                if x == 1:
                    pe.wait_ge(y_added, p_ * TT + 2)
                linear(4, 0, UC)
                if x == 1:
                    pe.wait_ge(y_added, p_ * TT + 3)
                turn(0)
                linear(6, 1, D + UC)
                pe.matmul(ps[:, 2, 0:T], sel[0:NE, :], post[:], start=True, stop=True).then_inc(sel_used, 1)
                for t in range(TT):
                    i_ = pe.matmul(ps[:, 3, 0:1], pick[:, t, x, :].bitcast(F32), gat[:, t, bass.ds(e, 1)], start=t == 0, stop=t == TT - 1)
                i_.then_inc(pick_used, 1)
                pe.wait_ge(at_ready, it * 2 + 1)
                unit(8, 4, at_h, at_l, True, False)
                unit(9, 5, at_h, at_l, True, False, lambda: turn(1))
                pe.wait_ge(at_ready, it * 2 + 2)
                unit(10, 4, at_h, at_l, False, True)
                unit(11, 5, at_h, at_l, False, True)

            with pe.Fori(0, NE // 2) as g:
                for x in range(2):
                    expert(g, x, g * 2 + x)
            rounds = pe.value_load(cnt_i[0:1, 0:1], min_val=1, max_val=TT)
            with pe.Fori(1, TT) as r:
                with pe.If(r < rounds):
                    with pe.Fori(0, NE // 2) as g:
                        for x in range(2):
                            expert(r * (NE // 2) + g, x, g * 2 + x)
                pe.nop()
            pe.wait_ge(out_ready, rounds * NE + 1)
            pe.wait_ge(pick_t_ready, rounds * NE + 1)
            pe.wait_ge(gslot_ready, rounds * NE + 1)
            for t, bank in COMBINE_BANKS:
                combine(t, bank, 1, True, True).then_inc(combined, 1)


_INS = ['x_prompt', 'x_sample', 'state_conv', 'state_h', 'norm1_g', 'w_in', 'conv_w', 'conv_b', 'w_rg', 'b_rg',
        'w_ig', 'b_ig', 'lru_lambda', 'ln_v_g', 'ln_v_b', 'w_s', 'b_s', 'w_proj_a', 'w_proj_b', 'w_out', 'norm2_g',
        'w_router', 'b_router', 'w_gate_up', 'b_gate_up', 'w_down', 'b_down', 'final_norm_g']
_OUTS = [((1, SEQ, D), 'float32'), ((ST, SF, D), 'float32'), ((1, 1, CW - 1, D), 'float32'), ((1, 1, D), 'float32'),
         ((1, ST, CW - 1, D), 'float32'), ((1, ST, D), 'float32'), ((1, ST, SF, DM), 'float32')]


def kernel(**inputs):
    import numpy as _np
    import concourse.bacc as _bacc
    from concourse import mybir as _mybir
    from concourse.bass_utils import run_bass_kernel_spmd as _run

    nc = _bacc.Bacc("TRN2", target_bir_lowering=False, num_devices=1)
    arrays, args = {}, []
    for name in _INS:
        a = _np.ascontiguousarray(inputs[name])
        arrays[f"in_{name}_dram"] = a
        args.append(nc.dram_tensor(f"in_{name}_dram", a.shape, _mybir.dt.from_np(a.dtype), kind="ExternalInput").ap())
    for i, (shape, dtype) in enumerate(_OUTS):
        dt = _mybir.dt.from_np(_np.dtype(dtype))
        args.append(nc.dram_tensor(f"out_{i}_dram", shape, dt, kind="ExternalOutput").ap())
    hawk_gmlp_moe_streaming_step(nc, *args)
    r = _run(nc, [arrays], core_ids=[0])
    return tuple(r.results[0][f"out_{i}_dram"] for i in range(len(_OUTS)))
```

```python
from contextlib import ExitStack

import concourse.bass as bass
from concourse import mybir

ALU = mybir.AluOpType
ACT = mybir.ActivationFunctionType
F32 = mybir.dt.float32
F32R = mybir.dt.float32r
BF16 = mybir.dt.bfloat16
I32 = mybir.dt.int32
U32 = mybir.dt.uint32
AX_X = mybir.AxisListType.X

P = 128
D = 1024
CB = D // P
SEQ = 256
ST, SF = 8, 16
T = SEQ + ST * SF
TT = T // P
CW = 4
PADP = CW - 1 + SEQ
PADS = CW - 1 + SF
DM = 512
MG = DM // P
NE = 32
TOPK = 4
LIMIT, ALPHA = 7.0, 1.702
RMS_EPS, LN_EPS = 1e-6, 1e-5

KB = 4
UC = 512
MIX_RING = 2
RAW_RING = 4
MIX_SPLIT = 3
SPLIT_RING = 4
IN_CHUNKS = [5, 0, 1, 2, 3, 4, 6, 7, 8, 9]
NZ = len(IN_CHUNKS) - 1
Z_U = 2
PB_U = Z_U + 2 * NZ
PA_U = PB_U + 2
WO_U = PA_U + 4
MIX_U = WO_U + 4
EXP_U = 12
COMBINE_BANKS = ((2, 2), (1, 0), (0, 6))
GATHER_BANKS = (0, 2, 6, 0)
FAR = 1000.0

G1_R, CBIAS_R, BRG_R, BIG_R, LAM_R, CONVW_R = 0, 8, 16, 24, 32, 40
ROWS = CONVW_R + CW * CB


def hawk_gmlp_moe_streaming_step(
    nc, x_prompt, x_sample, state_conv, state_h, norm1_g, w_in, conv_w, conv_b, w_rg, b_rg, w_ig, b_ig,
    lru_lambda, ln_v_g, ln_v_b, w_s, b_s, w_proj_a, w_proj_b, w_out, norm2_g, w_router, b_router,
    w_gate_up, b_gate_up, w_down, b_down, final_norm_g,
    y_prompt, y_sample, new_conv_prompt, new_h_prompt, new_conv_sample, new_h_sample, new_v_sample,
):
    base = (nc.sbuf_base + 31) // 32 * 32
    with ExitStack() as ctx:
        def at(name, offset, shape, dt=F32):
            return nc.alloc_sbuf_tensor_at(name, shape, dt, offset=base + offset)

        def sem(name):
            return ctx.enter_context(nc.semaphore(name))

        split_h = at("split_h", 0, [P, SPLIT_RING, KB, UC], F32R)
        split_l = at("split_l", 32768, [P, SPLIT_RING, KB, UC], F32R)
        raw = at("raw", 65536, [P, RAW_RING, KB, UC])
        x_in = at("x_in", 126976, [P, TT, D])
        lru_r = at("lru_r", 24576, [P, CB // 2, T])
        lru_i = at("lru_i", 57344, [P, CB // 2, T])
        lru_a = at("lru_a", 81920, [P, CB // 2, T])
        wst = at("wst", 88064, [P, 2, MG, P])
        lng = at("lng", 92160, [P, DM])
        lnb = at("lnb", 63488, [P, DM])
        bsb = at("bsb", 30720, [P, MG, P])
        tmp = at("tmp", 94208, [P, CB // 2, T])
        state_out = at("state_out", 94208, [36, D])
        act_h = at("act_h", 102400, [P, CB, T], F32R)
        act_l = at("act_l", 114688, [P, CB, T], F32R)
        xn_h = at("xn_h", 102400, [P, TT, D], F32R)
        xn_l = at("xn_l", 114688, [P, TT, D], F32R)
        ga = at("ga", 126976, [P, CB, T])
        mrg_h = at("mrg_h", 126976, [P, CB, T], F32R)
        xc = at("xc", 139264, [P, CB, T])
        mrg_l = at("mrg_l", 139264, [P, CB, T], F32R)
        at_h = at("at_h", 126976, [P, CB, P], F32R)
        at_l = at("at_l", 131072, [P, CB, P], F32R)
        out_h = [at("out_h0", 135168, [P, D], F32R), at("out_h1", 201728, [P, D], F32R)]
        out_l = [at("out_l0", 139264, [P, D], F32R), at("out_l1", 205824, [P, D], F32R)]
        xt_h = at("xt_h", 143360, [P, CB, 2, P], F32R)
        xt_l = at("xt_l", 176128, [P, CB, 2, P], F32R)
        gate_a = at("gate_a", 151552, [P, CB, T])
        xs = at("xs", 151552, [P, TT, D])
        bias_hl = at("bias_hl", 151552, [2 * NE, 2 * D], F32R)
        actv = at("actv", 159744, [P, D])
        bdn = at("bdn", 159744, [3 * NE, D])
        bdn_hl = at("bdn_hl", 163840, [3 * NE, D], F32R)
        gate_b = at("gate_b", 163840, [P, CB, T])
        ws_raw = at("ws_raw", 163840, [P, 2, MG, P])
        state_in = at("state_in", 172032, [32, D])
        g1 = at("g1", 163840, [P, UC])
        u1 = at("u1", 165888, [P, UC])
        sil = at("sil", 167936, [P, UC])
        pick = at("pick", 184320, [P, TT, 2, P], F32R)
        pick_t = at("pick_t", 169984, [P, 2, T], F32R)
        wr = at("wr", 173056, [P, CB, NE])
        sel = at("sel", 174080, [2 * NE, P], F32R)
        post = at("post", 174592, [NE, T], F32R)
        xpad = at("xpad", 176128, [P, CB, PADP + ST * PADS])
        yb_h = at("yb_h", 176128, [P, MG, T], F32R)
        yb_l = at("yb_l", 182272, [P, MG, T], F32R)
        bias_raw = at("bias_raw", 176128, [2 * NE, 2 * D])
        xnt = at("xnt", 176128, [P, CB, T])
        u = at("u", 189440, [P, MG, T])
        v = at("v", 195584, [P, TT, DM])
        y = at("y", 189440, [P, TT, D])
        lruw = at("lruw", 201728, [P, 2, CB, P])
        n2b = at("n2b", 201728, [P, D])
        fnb = at("fnb", 65536, [P, D])
        rows = at("rows", 209920, [ROWS, P])
        ident = at("ident", 210432, [P, P])
        iota_s = at("iota_s", 209920, [P, P])
        cols = at("cols", 210944, [P, ROWS])
        tri = at("tri", 211232, [P, P], BF16)
        small = at("small", 211488, [P, 320])
        pos = at("pos", 100352, [P, TT, NE])
        gat = at("gat", 100736, [P, TT, NE])
        h0 = small[:, 0:64].rearrange("p (c b) -> p c b", b=ST)
        st8 = small[:, 64:128]
        pack = at("pack", 100352, [P, CB, 36])
        ones_b = at("ones_b", 101504, [P, P], BF16)
        onehot = at("onehot", 101760, [2 * NE, NE])
        cnt_i = at("cnt_i", 101888, [1, 1], I32)
        slot_p = at("slot_p", 101920, [P, 1])
        pos_e = at("pos_e", 102112, [P, TT, 2])
        gslot = at("gslot", 101952, [P, 1])
        brb = at("brb", 101984, [P, NE])
        lg = at("lg", 126976, [P, TT, NE])
        mx = at("mx", 127360, [P, TT, 8])
        ix = at("ix", 127456, [P, TT, 8], U32)
        ixf = at("ixf", 127552, [P, TT, 8])
        ex = at("ex", 127648, [P, TT, 8])
        oh = at("oh", 127744, [P, TT, TOPK, NE])
        mask = at("mask", 129280, [P, TT, NE], BF16)
        maskf = at("maskf", 129472, [P, TT, NE])
        gat_t = at("gat_t", 129856, [3 * NE, T], F32R)
        gat3 = at("gat3", 131424, [P, TT, 3, NE])
        cnt = at("cnt", 131392, [1, 8])
        xn2 = at("xn2", 139264, [P, TT, D])
        squares = at("squares", 184320, [P, D])
        squares3 = at("squares3", 143360, [P, D])
        lam8 = small[:, 128:152]
        bn = small[:, 152:170].rearrange("p (t k) -> p t k", k=6)
        bnm = small[:, 170:176].rearrange("p (t k) -> p t k", k=2)
        rt = small[:, 192:256]
        ps = ctx.enter_context(nc.psum_tensor("ps", [P, 8, 512], F32))

        x_loaded, rows_loaded = [sem(f"x_loaded{t}") for t in range(TT)], sem("rows_loaded")
        lruw_loaded, ws_loaded, ln_loaded = sem("lruw_loaded"), sem("ws_loaded"), sem("ln_loaded")
        late_loaded, y_loaded, bias_loaded = sem("late_loaded"), sem("y_loaded"), sem("bias_loaded")
        fnb_loaded = sem("fnb_loaded")
        mix_landed = [sem(f"mix_landed{i}") for i in range(MIX_RING)]
        exp_landed = [sem(f"exp_landed{i}") for i in range(RAW_RING)]
        high_done, low_done, unit_used = sem("high_done"), sem("low_done"), sem("unit_used")
        const_ready, pool_step, dve_step = sem("const_ready"), sem("pool_step"), sem("dve_step")
        zeroed = sem("zeroed")
        squared, rstd_in, rstd_out, xs_ready = sem("squared"), sem("rstd_in"), sem("rstd_out"), sem("xs_ready")
        rows_turned, rows_copied, xs_turned, xn_high, xn_ready = (
            sem("rows_turned"), sem("rows_copied"), sem("xs_turned"), sem("xn_high"), sem("xn_ready"))
        lam_in, lam_exp, lam_ln_in, lam_ln, lam_ready = (
            sem("lam_in"), sem("lam_exp"), sem("lam_ln_in"), sem("lam_ln"), sem("lam_ready"))
        z_ready, z_evac, conv_done = sem("z_ready"), sem("z_evac"), sem("conv_done")
        gates_mm, gates_read, decay_ready, mult_in, mult_ready, lru_ready, scanned = (
            sem("gates_mm"), sem("gates_read"), sem("decay_ready"), sem("mult_in"), sem("mult_ready"),
            sem("lru_ready"), sem("scanned"))
        vmix_read = sem("vmix_read")
        v_mm, v_read, ln_in, ln_out, v_ready = sem("v_mm"), sem("v_read"), sem("ln_in"), sem("ln_out"), sem("v_ready")
        ws_turned, ws_ready, vmix_mm, yb_ready = sem("ws_turned"), sem("ws_ready"), sem("vmix_mm"), sem("yb_ready")
        pb_mm, pb_read, pa_mm, mrg_ready, wo_mm, y_ready = (
            sem("pb_mm"), sem("pb_read"), sem("pa_mm"), sem("mrg_ready"), sem("wo_mm"), sem("y_ready"))
        st_packed, st_turned, st_ready = sem("st_packed"), sem("st_turned"), sem("st_ready")
        sq2, r2_in, r2_out, xn2_ready, xn2_turned, xnt_ready, xn2_high = (
            sem("sq2"), sem("r2_in"), sem("r2_out"), sem("xn2_ready"), sem("xn2_turned"), sem("xnt_ready"),
            sem("xn2_high"))
        logits_mm, top_ready, top_exp, mask_ready, pos_mm, pos_ready, post_mm, route_ready = (
            sem("logits_mm"), sem("top_ready"), sem("top_exp"), sem("mask_ready"), sem("pos_mm"),
            sem("pos_ready"), sem("post_mm"), sem("route_ready"))
        zeros_ready = sem("zeros_ready")
        gat_ready, bd_mm = sem("gat_ready"), sem("bd_mm")
        ranks_ready, column_ready = sem("ranks_ready"), sem("column_ready")
        ranks_seen, column_seen = sem("ranks_seen"), sem("column_seen")
        pick_ready, pick_used, sel_ready, sel_used = (
            sem("pick_ready"), sem("pick_used"), sem("sel_ready"), sem("sel_used"))
        gathered, xt_ready, xt_low_ready, out_high, out_ready, pick_t_ready, combined, y_added = (
            sem("gathered"), sem("xt_ready"), sem("xt_low_ready"), sem("out_high"), sem("out_ready"), sem("pick_t_ready"),
            sem("combined"), sem("y_added"))
        clipped, up_clipped, silu_done, act_ready, act_turned, at_high, at_ready, gslot_ready = (
            sem("clipped"), sem("up_clipped"), sem("silu_done"), sem("act_ready"), sem("act_turned"), sem("at_high"),
            sem("at_ready"), sem("gslot_ready"))
        xn2_low, r3_mean = sem("xn2_low"), sem("r3_mean")
        sq3, r3_in, r3_out, out_final, stored = sem("sq3"), sem("r3_in"), sem("r3_out"), sem("out_final"), sem("stored")

        def halves(w):
            return w.rearrange("o (h j p) n -> (o h) p j n", j=KB, p=P)

        win, wpa, wpb, wout = halves(w_in), halves(w_proj_a), halves(w_proj_b), halves(w_out)
        wgu = w_gate_up.rearrange("o e (h j p) n -> (o e) h p j n", j=KB, p=P)
        wdn = w_down.rearrange("o e (h j p) n -> (o e) h p j n", j=KB, p=P)

        def mix_unit(n):
            if n < PB_U:
                c = IN_CHUNKS[n // 2]
                return win[n % 2][:, :, c * UC:(c + 1) * UC]
            if n < PA_U:
                c = n - PB_U
                return wpb[0][:, :, c * UC:(c + 1) * UC]
            w, m = (wpa, n - PA_U) if n < WO_U else (wout, n - WO_U)
            return w[m % 2][:, :, m // 2 * UC:(m // 2 + 1) * UC]

        def exp_unit(e, m):
            if m < 8:
                c = (0, 2, 1, 3)[m // 2]
                w, half = wgu, m % 2
            else:
                c, half, w = m % 2, (m - 8) // 2, wdn
            return w[bass.ds(e, 1), half, :, :, c * UC:(c + 1) * UC].rearrange("o p j n -> (o p) j n")

        def wait_part(eng, ready, parts, k, i, unit):
            if i < parts - 1:
                eng.wait_ge(ready, (parts - 1) * k + i + 1)
            else:
                eng.wait_ge(unit_used, unit + 1)

        samp_pad = xpad[:, :, PADP:].rearrange("p c (b j) -> p c b j", j=PADS)
        block = ctx.enter_context(nc.Block())

        @block.sync
        def _(sp):
            for t in range(2):
                sp.dma_start(x_in[:, t, :], x_prompt[:, t * P:(t + 1) * P, :].rearrange("o p d -> (o p) d")).then_inc(x_loaded[t], 16)
            sp.dma_start(x_in[:, 2, :], x_sample.rearrange("b s d -> (b s) d")).then_inc(x_loaded[2], 16)
            for r, a in ((G1_R, norm1_g), (CBIAS_R, conv_b), (BRG_R, b_rg), (BIG_R, b_ig), (LAM_R, lru_lambda)):
                sp.dma_start(rows[r:r + CB, :], a.rearrange("o (c p) -> (o c) p", p=P)).then_inc(rows_loaded, 16)
            sp.dma_start(rows[CONVW_R:ROWS, :], conv_w.rearrange("o k (c p) -> (o k c) p", p=P)).then_inc(rows_loaded, 16)
            sp.dma_start(state_in[0:24, :], state_conv.rearrange("o b k d -> (o b k) d")).then_inc(rows_loaded, 16)
            sp.dma_start(state_in[24:32, :], state_h.rearrange("o b d -> (o b) d")).then_inc(rows_loaded, 16)
            for n in range(MIX_U):
                if n >= MIX_RING:
                    sp.wait_ge(low_done, n - MIX_RING + 1)
                sp.dma_start(raw[:, n % MIX_RING], mix_unit(n)).then_inc(mix_landed[n % MIX_RING], 16)
                if n == PA_U:
                    sp.wait_ge(v_ready, 1)
                    sp.dma_start(new_v_sample.rearrange("o b s d -> (o b s) d"), v[:, 2, :]).then_inc(stored, 16)
            sp.wait_ge(yb_ready, 1)
            sp.wait_ge(stored, 16)
            for t in range(2):
                sp.dma_start(y[:, t, :], x_prompt[:, t * P:(t + 1) * P, :].rearrange("o p d -> (o p) d")).then_inc(y_loaded, 16)
            sp.dma_start(y[:, 2, :], x_sample.rearrange("b s d -> (b s) d")).then_inc(y_loaded, 16)
            sp.wait_ge(st_ready, 1)
            sp.dma_start(new_conv_prompt.rearrange("o b k d -> (o b k) d"), state_out[0:3, :]).then_inc(stored, 16)
            sp.dma_start(new_conv_sample.rearrange("o b k d -> (o b k) d"), state_out[3:27, :]).then_inc(stored, 16)
            sp.dma_start(new_h_prompt.rearrange("o b d -> (o b) d"), state_out[27:28, :]).then_inc(stored, 16)
            sp.dma_start(new_h_sample.rearrange("o b d -> (o b) d"), state_out[28:36, :]).then_inc(stored, 16)
            sp.wait_ge(stored, 5 * 16)
            sp.wait_ge(low_done, MIX_U)

            def expert(it, e):
                for m in range(EXP_U):
                    sp.wait_ge(low_done, it * EXP_U + (MIX_U + m - RAW_RING + 1))
                    sp.dma_start(raw[:, m % RAW_RING], exp_unit(e, m)).then_inc(exp_landed[m % RAW_RING], 16)

            with sp.Fori(0, NE // 2) as g:
                for x in range(2):
                    expert(g * 2 + x, g * 2 + x)
            sp.wait_ge(route_ready, 1)
            rounds = sp.value_load(cnt_i[0:1, 0:1], min_val=1, max_val=TT)
            with sp.Fori(1, TT) as r:
                with sp.If(r < rounds):
                    with sp.Fori(0, NE // 2) as g:
                        for x in range(2):
                            expert(r * NE + (g * 2 + x), g * 2 + x)
                sp.nop()
            sp.wait_ge(low_done, rounds * (NE * EXP_U) + MIX_U)
            sp.dma_start(fnb[:], final_norm_g.rearrange("(o d) -> o d", o=1).broadcast_to([P, D])).then_inc(fnb_loaded, 16)
            sp.wait_ge(out_final, TT)
            sp.dma_start(y_prompt.rearrange("o (t p) d -> p (o t) d", p=P), y[:, 0:2, :]).then_inc(stored, 16)
            sp.dma_start(y_sample.rearrange("b s d -> (b s) d"), y[:, 2, :]).then_inc(stored, 16)
            sp.wait_ge(stored, 7 * 16)

        @block.gpsimd
        def _(pool):
            step = [0]

            def link(ins):
                step[0] += 1
                ins.then_inc(pool_step, 1)
                pool.wait_ge(pool_step, step[0])

            link(pool.memset(ident[:], 0.0))
            pool.affine_select(out=ident[:], in_=ident[:], compare_op=ALU.not_equal, fill=1.0, base=0,
                               pattern=[[-1, P]], channel_multiplier=1).then_inc(const_ready, 1)
            pool.memset(lruw[:], 0.0).then_inc(zeroed, 1)
            pool.memset(ws_raw[:, 1], 0.0).then_inc(zeroed, 1)
            pool.memset(xpad[:, :, 0:CW - 1], 0.0).then_inc(const_ready, 1)
            pool.wait_ge(zeroed, 2)
            pool.dma_start(ws_raw[:, 0], w_s.rearrange("o g t s -> t (o g) s")).then_inc(ws_loaded, 16)
            for b in range(ST):
                pool.dma_start(ws_raw[b * SF:(b + 1) * SF, 1, :, b * SF:(b + 1) * SF],
                               w_s[:, :, 0:SF, 0:SF].rearrange("o g t s -> t (o g) s")).then_inc(ws_loaded, 16)
            for k, w in enumerate((w_rg, w_ig)):
                for q in range(2):
                    pool.dma_start(lruw[64 * q:64 * q + 64, k, :, 64 * q:64 * q + 64],
                                   w.rearrange("o (c q) i j -> q i (o c) j", q=2)[q]).then_inc(lruw_loaded, 16)
            pool.dma_start(lng[:], ln_v_g.broadcast_to([P, DM])).then_inc(ln_loaded, 16)
            pool.dma_start(lnb[:], ln_v_b.broadcast_to([P, DM])).then_inc(ln_loaded, 16)
            pool.dma_start(bsb[:], b_s.broadcast_to([P, MG, P])).then_inc(ln_loaded, 16)
            link(pool.memset(tri[:], 1.0))
            link(pool.affine_select(out=tri[:], in_=tri[:], compare_op=ALU.is_gt, fill=0.0, base=0,
                                    pattern=[[1, P]], channel_multiplier=-1))
            link(pool.memset(ones_b[:], 1.0))
            for k in range(2):
                pool.wait_ge(ws_ready, k + 1)
                pool.affine_select(out=wst[:, k], in_=wst[:, k], compare_op=ALU.is_ge, fill=0.0, base=0,
                                   pattern=[[0, MG], [1, P]], channel_multiplier=-1).then_inc(const_ready, 1)
            pool.wait_ge(rows_copied, 1)
            link(pool.iota(iota_s[:], pattern=[[1, P]], base=0, channel_multiplier=0, allow_small_or_imprecise_dtypes=True))
            link(pool.iota(slot_p[:], pattern=[[0, 1]], base=0, channel_multiplier=1, allow_small_or_imprecise_dtypes=True))
            link(pool.memset(onehot[:], 0.0))
            link(pool.affine_select(out=onehot[:], in_=onehot[:], compare_op=ALU.not_equal, fill=1.0, base=0,
                                    pattern=[[-1, NE]], channel_multiplier=1))
            pool.affine_select(out=onehot[:], in_=onehot[:], compare_op=ALU.not_equal, fill=1.0, base=-NE,
                               pattern=[[-1, NE]], channel_multiplier=1).then_inc(const_ready, 1)
            pool.dma_start(brb[:], b_router.broadcast_to([P, NE])).then_inc(late_loaded, 16)
            pool.wait_ge(gates_mm, 4)
            pool.dma_start(n2b[:], norm2_g.broadcast_to([P, D])).then_inc(late_loaded, 16)
            pool.wait_ge(unit_used, PA_U)
            for k in range(2):
                pool.dma_start(bias_raw[k * NE:(k + 1) * NE, :], b_gate_up.rearrange("o e n -> (o e) n")).then_inc(bias_loaded, 16)
            pool.wait_ge(mrg_ready, CB)
            pool.dma_start(wr[:], w_router.rearrange("o (c p) e -> p (o c) e", p=P)).then_inc(late_loaded, 16)
            for k in range(3):
                pool.dma_start(bdn[k * NE:(k + 1) * NE, :], b_down.rearrange("o e n -> (o e) n")).then_inc(late_loaded, 16)

            pool.wait_ge(gat_ready, 1)
            pool.wait_ge(const_ready, 5)

            def next_ranks(r):
                pool.wait_ge(sel_used, r * NE + 1)
                pool.sem_inc(ranks_seen, 1)
                pool.tensor_scalar(pos[:], pos[:], -float(P), None, ALU.add)
                pool.tensor_scalar(post[:], post[:].bitcast(F32), -float(P), None, ALU.add).then_inc(ranks_ready, 1)
                pool.wait_ge(ranks_ready, r)
                pool.sem_inc(ranks_seen, 1)

            def pair(p_, g):
                pool.wait_ge(pick_used, p_ * 2 + 1)
                pool.tensor_copy(pos_e[:], pos[:, :, bass.ds(g * 2, 2)]).then_inc(column_ready, 1)
                pool.wait_ge(column_ready, p_ + 1)
                pool.sem_inc(column_seen, 1)
                for t in range(TT):
                    for x in range(2):
                        i_ = pool.tensor_scalar(pick[:, t, x, :], iota_s[:], pos_e[:, t, x:x + 1], None, ALU.is_equal)
                i_.then_inc(pick_ready, 1)
                for x in range(2):
                    pool.wait_ge(sel_used, p_ * 2 + (x + 1))
                    pool.tensor_copy(sel[:], onehot[:, bass.ds(g * 2 + x, 1)].broadcast_to([2 * NE, P])).then_inc(sel_ready, 1)

            with pool.Fori(0, NE // 2) as g:
                pair(g, g)
            rounds = pool.value_load(cnt_i[0:1, 0:1], min_val=1, max_val=TT)
            with pool.Fori(1, TT) as r:
                with pool.If(r < rounds):
                    next_ranks(r)
                    with pool.Fori(0, NE // 2) as g:
                        pair(r * (NE // 2) + g, g)
                pool.nop()

        @block.scalar
        def _(act):
            def high(n):
                act.wait_ge(mix_landed[n % MIX_RING], 16 * (n // MIX_RING + 1))
                if n >= MIX_SPLIT:
                    act.wait_ge(unit_used, n - MIX_SPLIT + 1)
                act.activation(split_h[:, n % MIX_SPLIT], raw[:, n % MIX_RING], ACT.Copy).then_inc(high_done, 1)

            act.preload_act_table(ACT.Sqrt)
            for t in range(TT):
                act.wait_ge(x_loaded[t], 16)
                act.activation(xs[:, t, :], x_in[:, t, :], ACT.Square, accum_out=st8[:, t:t + 1]).then_inc(squared, 1)
            act.wait_ge(rstd_in, 1)
            act.activation(st8[:, 8:8 + TT], st8[:, 4:4 + TT], ACT.Sqrt).then_inc(rstd_out, 1)
            high(0)
            act.wait_ge(rows_copied, 1)
            for c in range(CB):
                act.wait_ge(xs_turned, c + 1)
                act.activation(act_h[:, c, :], ps[:, c, 0:T], ACT.Identity, scale=cols[:, G1_R + c:G1_R + c + 1]).then_inc(xn_high, 1)
            high(1)
            high(2)
            act.wait_ge(lam_in, 1)
            act.activation(st8[:, 24:32], st8[:, 16:24], ACT.Exp).then_inc(lam_exp, 1)
            act.wait_ge(lam_ln_in, 1)
            act.activation(st8[:, 40:48], st8[:, 32:40], ACT.Ln).then_inc(lam_ln, 1)

            def evacuate(c):
                for b in range(4):
                    wait_part(act, z_ready, 4, c, b, Z_U + 2 * c + 1)
                    src = ps[:, 4 * (c % 3 % 2) + b, 0:T]
                    if c < 2:
                        act.activation(xpad[:, 4 * c + b, CW - 1:PADP], src[:, 0:SEQ], ACT.Identity)
                        act.activation(samp_pad[:, 4 * c + b, :, CW - 1:],
                                       src[:, SEQ:T].rearrange("p (b s) -> p b s", s=SF), ACT.Identity).then_inc(z_evac, 1)
                        continue
                    dst, func = {2: (ga[:, b], 0), 3: (ga[:, 4 + b], 0), 4: (u[:, b], 0), 5: (gate_a[:, b], 1),
                                 6: (gate_a[:, 4 + b], 1), 7: (gate_b[:, b], 1), 8: (gate_b[:, 4 + b], 1)}[c]
                    act.activation(dst, src, ACT.Sigmoid if func else ACT.Gelu_apprx_tanh).then_inc(z_evac, 1)

            def sigmoids(hf):
                for k, (dst, r) in enumerate(((lru_r, BRG_R), (lru_i, BIG_R))):
                    act.wait_ge(gates_mm, 2 * hf + k + 1)
                    for b in range(4):
                        bank = 4 * (1 - k) + b
                        col = r + 4 * hf + b
                        if k == 0 and hf == 1 and b == 0:
                            act.wait_ge(st_packed, 1)
                        i_ = act.activation(dst[:, b], ps[:, bank, 0:T], ACT.Sigmoid, bias=cols[:, col:col + 1])
                    i_.then_inc(gates_read, 1)

            def decays(hf):
                act.wait_ge(lam_ready, 1)
                act.wait_ge(gates_read, 2 * hf + 1)
                for b in range(4):
                    act.activation(lru_a[:, b], lru_r[:, b], ACT.Exp, scale=st8[:, 48 + 4 * hf + b:49 + 4 * hf + b])
                for b in range(4):
                    i_ = act.activation(lru_r[:, b], lru_r[:, b], ACT.Tanh, scale=st8[:, 56 + 4 * hf + b:57 + 4 * hf + b])
                i_.then_inc(decay_ready, 1)

            def roots(hf):
                act.wait_ge(mult_in, hf + 1)
                act.activation(lru_r[:], lru_r[:], ACT.Sqrt).then_inc(mult_ready, 1)

            high(3)
            for t in range(TT):
                wait_part(act, v_mm, TT, 0, t, 1)
                act.activation(v[:, t, :], ps[:, t, :], ACT.Gelu_apprx_tanh).then_inc(v_read, 1)
            high(4)
            act.wait_ge(ln_in, 1)
            act.activation(st8[:, 12:15], st8[:, 8:11], ACT.Sqrt).then_inc(ln_out, 1)
            for c in range(NZ):
                if c in (6, 7):
                    roots(c - 6)
                high(Z_U + 2 * c + 3)
                evacuate(c)
                high(Z_U + 2 * c + 4)
                if c in (5, 6):
                    sigmoids(c - 5)
                    decays(c - 5)
            for n in range(PB_U + 3, MIX_U):
                high(n)

            act.preload_act_table(ACT.Sqrt)
            for k in range(2):
                for t in range(TT):
                    n = TT * k + t
                    act.wait_ge(y_ready, n + 1)
                    if n >= 2:
                        act.wait_ge(sq2, n - 1)
                    act.activation(squares[:, UC * (n % 2):UC * (n % 2) + UC], y[:, t, UC * k:UC * k + UC], ACT.Square,
                                   accum_out=rt[:, 48 + n:49 + n]).then_inc(sq2, 1)
            act.wait_ge(r2_in, 1)
            act.activation(rt[:, 8:8 + TT], rt[:, 4:4 + TT], ACT.Sqrt).then_inc(r2_out, 1)
            act.preload_act_table(ACT.Exp)
            for t in range(TT):
                act.wait_ge(xn2_ready, t + 1)
                act.activation(xn_h[:, t, :], xn2[:, t, :], ACT.Copy).then_inc(xn2_high, 1)
            for t in range(TT):
                for half in range(2):
                    act.wait_ge(xn2_turned, 2 * t + half + 1)
                    act.activation(xnt[:, 4 * half:4 * half + 4, t * P:(t + 1) * P],
                                   ps[:, 2 * t + half, :].rearrange("p (c t) -> p c t", t=P), ACT.Copy).then_inc(xnt_ready, 1)
            act.wait_ge(top_ready, 1)
            for t in range(TT):
                i_ = act.activation(ex[:, t, 0:TOPK], mx[:, t, 0:TOPK], ACT.Exp, bias=rt[:, 16 + t:17 + t], accum_out=rt[:, 20 + t:21 + t])
            i_.then_inc(top_exp, 1)
            act.preload_act_table(ACT.Silu)
            act.activation(gslot[:], slot_p[:], ACT.Copy, scale=0.0).then_inc(gslot_ready, 1)

            def out_high_part(it, x):
                act.wait_ge(zeros_ready, 1)
                act.wait_ge(unit_used, it * EXP_U + MIX_U)
                act.wait_ge(gslot_ready, it + 1)
                act.activation(out_h[x][:], ps[:, 4:6, :].rearrange("p a b -> p (a b)"), ACT.Copy, scale=gslot[:, 0:1]).then_inc(out_high, 1)

            def expert(p_, x):
                it = p_ * 2 + x

                def high(m):
                    act.wait_ge(exp_landed[m % RAW_RING], it * (16 * EXP_U // RAW_RING) + 16 * (m // RAW_RING + 1))
                    act.wait_ge(unit_used, it * EXP_U + (MIX_U + m - SPLIT_RING + 1))
                    act.activation(split_h[:, m % SPLIT_RING], raw[:, m % RAW_RING], ACT.Copy).then_inc(high_done, 1)

                def silu(j):
                    act.wait_ge(clipped, it * 2 + (j + 1))
                    act.activation(sil[:], g1[:], ACT.Silu, scale=ALPHA).then_inc(silu_done, 1)

                def turned_high(j):
                    act.wait_ge(act_turned, it * 2 + (j + 1))
                    act.activation(at_h[:, 4 * j:4 * j + 4, :].rearrange("p c s -> p (c s)"), ps[:, 6 + j, :], ACT.Copy).then_inc(at_high, 1)

                for m in range(3):
                    high(m)
                if x == 0:
                    for k in range(2):
                        act.wait_ge(gathered, p_ * 4 + (k + 1))
                        act.activation(xt_h[:, 4 * k:4 * k + 4].rearrange("p c x s -> p (c x s)"),
                                       ps[:, 2 * k:2 * k + 2, :].rearrange("p a b -> p (a b)"), ACT.Copy).then_inc(xt_ready, 1)
                    high(3)
                out_high_part(it, 1 - x)
                for m in range(4 - x, 7):
                    high(m)
                silu(0)
                high(7)
                high(8)
                turned_high(0)
                high(9)
                high(10)
                silu(1)
                high(11)
                turned_high(1)
                act.wait_ge(pick_used, it + 2)
                act.activation(gslot[:], ps[:, 3, 0:1], ACT.Copy, scale=1.0 / ALPHA).then_inc(gslot_ready, 1)

            with act.Fori(0, NE // 2) as g:
                for x in range(2):
                    expert(g, x)
            act.wait_ge(route_ready, 1)
            rounds = act.value_load(cnt_i[0:1, 0:1], min_val=1, max_val=TT)
            with act.Fori(1, TT) as r:
                with act.If(r < rounds):
                    with act.Fori(0, NE // 2) as g:
                        for x in range(2):
                            expert(r * (NE // 2) + g, x)
                act.nop()
            out_high_part(rounds * NE, 1)
            for i, (t, _) in enumerate(COMBINE_BANKS):
                act.wait_ge(y_added, rounds * (NE // 2 * TT) + (i + 1))
                if i:
                    act.wait_ge(sq3, i)
                act.activation(squares3[:], y[:, t, :], ACT.Square, accum_out=rt[:, 32 + t:33 + t]).then_inc(sq3, 1)
            act.wait_ge(r3_in, 1)
            act.activation(rt[:, 40:40 + TT], rt[:, 36:36 + TT], ACT.Sqrt).then_inc(r3_out, 1)

        @block.vector
        def _(dve):
            step = [0]

            def link(ins):
                step[0] += 1
                ins.then_inc(dve_step, 1)
                dve.wait_ge(dve_step, step[0])

            def low(n):
                dve.wait_ge(high_done, n + 1)
                dve.tensor_tensor(split_l[:, n % MIX_SPLIT], raw[:, n % MIX_RING],
                                  split_h[:, n % MIX_SPLIT].bitcast(F32), ALU.subtract).then_inc(low_done, 1)

            dve.wait_ge(squared, TT)
            link(dve.tensor_scalar(st8[:, 4:4 + TT], st8[:, 0:TT], 1.0 / D, RMS_EPS, ALU.mult, ALU.add))
            dve.reciprocal(st8[:, 4:4 + TT], st8[:, 4:4 + TT]).then_inc(rstd_in, 1)
            dve.wait_ge(rstd_out, 1)
            for t in range(TT):
                dve.tensor_scalar(xs[:, t, :], x_in[:, t, :], st8[:, 8 + t:9 + t], None, ALU.mult).then_inc(xs_ready, 1)
            dve.wait_ge(rows_turned, 1)
            link(dve.tensor_copy(cols[:], ps[:, 0, 0:ROWS]))
            turned = ps[:, 1, 0:CB * 32].rearrange("p (c r) -> p c r", r=32)
            dve.tensor_copy(samp_pad[:, :, :, 0:CW - 1], turned[:, :, 0:24].rearrange("p c (b k) -> p c b k", k=CW - 1))
            dve.tensor_copy(h0, turned[:, :, 24:32]).then_inc(rows_copied, 1)
            low(0)
            for k in range(2):
                dve.wait_ge(ws_turned, k + 1)
                dve.tensor_copy(wst[:, k].rearrange("p g t -> p (g t)"), ps[:, 6 + k, :]).then_inc(ws_ready, 1)
            for c in range(CB):
                dve.wait_ge(xn_high, c + 1)
                i_ = dve.scalar_tensor_tensor(out=act_l[:, c, :], in0=ps[:, c, 0:T], scalar=cols[:, G1_R + c:G1_R + c + 1],
                                              in1=act_h[:, c, :].bitcast(F32), op0=ALU.mult, op1=ALU.subtract)
                i_.then_inc(xn_ready, 1)
                if c == 3:
                    dve.wait_ge(xn_ready, 4)
                    dve.nop().then_inc(z_evac, 4)
            low(1)
            low(2)
            lam, neg, pos_, one, dif = cols[:, LAM_R:LAM_R + CB], st8[:, 16:24], lam8[:, 0:8], st8[:, 32:40], lam8[:, 8:16]
            link(dve.tensor_scalar(neg, lam, -1.0, None, ALU.mult))
            link(dve.tensor_scalar(pos_, neg, 0.0, None, ALU.max))
            dve.tensor_tensor(neg, neg, lam, ALU.min).then_inc(lam_in, 1)
            dve.wait_ge(lam_exp, 1)
            dve.tensor_scalar(one, st8[:, 24:32], 1.0, None, ALU.add).then_inc(lam_ln_in, 1)
            dve.wait_ge(lam_ln_in, 1)
            link(dve.tensor_scalar(dif, one, -1.0, None, ALU.add))
            link(dve.scalar_tensor_tensor(out=lam8[:, 16:24], in0=dif, scalar=0.0, in1=st8[:, 24:32], op0=ALU.is_equal, op1=ALU.mult))
            link(dve.tensor_scalar(dif, dif, 1e-30, None, ALU.max))
            link(dve.reciprocal(dif, dif))
            link(dve.tensor_tensor(dif, dif, st8[:, 24:32], ALU.mult))
            dve.wait_ge(lam_ln, 1)
            link(dve.tensor_tensor(dif, dif, st8[:, 40:48], ALU.mult))
            link(dve.tensor_tensor(dif, dif, lam8[:, 16:24], ALU.add))
            link(dve.tensor_tensor(dif, dif, pos_, ALU.add))
            dve.tensor_scalar(st8[:, 48:56], dif, -8.0, None, ALU.mult)
            dve.tensor_scalar(st8[:, 56:64], dif, 8.0, None, ALU.mult).then_inc(lam_ready, 1)

            def conv(k):
                for c in range(CB):
                    wk = cols[:, CONVW_R + CB * k + c:CONVW_R + CB * k + c + 1]
                    for src, dst in ((xpad[:, c, k:k + SEQ], xc[:, c, 0:SEQ]),
                                     (samp_pad[:, c, :, k:k + SF], xc[:, c, SEQ:T].rearrange("p (b s) -> p b s", s=SF))):
                        if k == 0:
                            i_ = dve.tensor_scalar(dst, src, wk, cols[:, CBIAS_R + c:CBIAS_R + c + 1], ALU.mult, ALU.add)
                        else:
                            i_ = dve.scalar_tensor_tensor(out=dst, in0=src, scalar=wk, in1=dst, op0=ALU.mult, op1=ALU.add)
                link(i_)

            def lru(hf):
                cs = slice(4 * hf, 4 * hf + 4)
                dve.wait_ge(gates_read, 2 * hf + 2)
                link(dve.tensor_tensor(lru_i[:], lru_i[:], xc[:, cs], ALU.mult))
                dve.wait_ge(decay_ready, hf + 1)
                link(dve.tensor_tensor(tmp[:], lru_a[:], lru_a[:], ALU.mult))
                link(dve.scalar_tensor_tensor(out=lru_r[:], in0=tmp[:], scalar=1.0, in1=lru_r[:], op0=ALU.add, op1=ALU.mult))
                dve.tensor_scalar(lru_r[:], lru_r[:], 0.0, None, ALU.max).then_inc(mult_in, 1)
                dve.wait_ge(mult_ready, hf + 1)
                link(dve.memset(lru_r[:, :, 0:1], 1.0))
                link(dve.tensor_tensor(lru_i[:], lru_i[:], lru_r[:], ALU.mult))
                first_a = lru_a[:, :, SEQ:T].rearrange("p c (b s) -> p c b s", s=SF)[:, :, :, 0]
                first_i = lru_i[:, :, SEQ:T].rearrange("p c (b s) -> p c b s", s=SF)[:, :, :, 0]
                link(dve.tensor_tensor(tmp[:, :, 0:ST], first_a, h0[:, cs, :], ALU.mult))
                link(dve.tensor_tensor(first_i, first_i, tmp[:, :, 0:ST], ALU.add))
                dve.memset(first_a, 0.0)
                link(dve.memset(lru_a[:, :, 0:1], 0.0))
                link(dve.tensor_tensor_scan(xc[:, cs].rearrange("p c t -> p (c t)"), lru_a[:].rearrange("p c t -> p (c t)"),
                                            lru_i[:].rearrange("p c t -> p (c t)"), 0.0, ALU.mult, ALU.add))
                dve.tensor_copy(pack[:, cs, 27:28], xc[:, cs, SEQ - 1:SEQ])
                dve.tensor_copy(pack[:, cs, 28:36], xc[:, cs, SEQ:T].rearrange("p c (b s) -> p c b s", s=SF)[:, :, :, SF - 1]).then_inc(st_packed, 1)
                link(dve.tensor_tensor(ga[:, cs], xc[:, cs], ga[:, cs], ALU.mult))

            def lru_split(hf):
                cs = slice(4 * hf, 4 * hf + 4)
                dve.wait_ge(unit_used, PB_U)
                link(dve.tensor_copy(act_h[:, cs], ga[:, cs]))
                dve.tensor_tensor(act_l[:, cs], ga[:, cs], act_h[:, cs].bitcast(F32), ALU.subtract).then_inc(lru_ready, 1)
                dve.wait_ge(lru_ready, hf + 1)

            low(3)
            for t in range(TT):
                dve.wait_ge(v_read, t + 1)
                i_ = dve.bn_stats(bn[:, t, :], v[:, t, :])
            link(i_)
            for t in range(TT):
                i_ = dve.bn_aggr(bnm[:, t, :], bn[:, t, :])
            link(i_)
            link(dve.tensor_scalar(st8[:, 8:8 + TT], bnm[:, :, 1], LN_EPS, None, ALU.add))
            dve.reciprocal(st8[:, 8:8 + TT], st8[:, 8:8 + TT]).then_inc(ln_in, 1)
            low(4)
            dve.wait_ge(ln_out, 1)
            for t in range(TT):
                i_ = dve.tensor_scalar(v[:, t, :], v[:, t, :], bnm[:, t, 0:1], st8[:, 12 + t:13 + t], ALU.subtract, ALU.mult)
            link(i_)
            dve.wait_ge(ln_loaded, 48)
            link(dve.tensor_tensor(v[:], v[:], lng[:].unsqueeze(1).broadcast_to([P, TT, DM]), ALU.mult))
            dve.tensor_tensor(v[:], v[:], lnb[:].unsqueeze(1).broadcast_to([P, TT, DM]), ALU.add).then_inc(v_ready, 1)

            def gate_mix():
                for g in range(MG):
                    dve.wait_ge(vmix_mm, g + 1)
                    s_p = tmp[:, g, :]
                    dve.tensor_tensor(s_p[:, 0:SEQ].rearrange("p (n t) -> p n t", t=P), ps[:, 4 + g, 0:SEQ].rearrange("p (n t) -> p n t", t=P),
                                      bsb[:, g, :].unsqueeze(1).broadcast_to([P, 2, P]), ALU.add)
                    i_ = dve.tensor_tensor(s_p[:, SEQ:T].rearrange("p (b s) -> p b s", s=SF), ps[:, 4 + g, SEQ:T].rearrange("p (b s) -> p b s", s=SF),
                                           bsb[:, g, 0:SF].unsqueeze(1).broadcast_to([P, ST, SF]), ALU.add)
                i_.then_inc(vmix_read, 1)
                dve.wait_ge(vmix_read, 1)
                link(dve.tensor_tensor(u[:], tmp[:], u[:], ALU.mult))

            for c in range(NZ):
                if c == 6:
                    gate_mix()
                    lru(0)
                if c == 7:
                    link(dve.tensor_copy(yb_h[:], u[:]))
                    dve.tensor_tensor(yb_l[:], u[:], yb_h[:].bitcast(F32), ALU.subtract).then_inc(yb_ready, 1)
                    lru(1)
                low(Z_U + 2 * c + 3)
                if c == 2:
                    dve.wait_ge(z_evac, 4 + 8)
                    dve.wait_ge(const_ready, 2)
                    conv(0)
                if c == 3:
                    conv(1)
                    conv(2)
                if c == 4:
                    conv(3)
                    dve.nop().then_inc(conv_done, 1)
                    dve.tensor_copy(pack[:, :, 0:3], xpad[:, :, SEQ:PADP])
                    link(dve.tensor_copy(pack[:, :, 3:27].rearrange("p c (b k) -> p c b k", k=CW - 1), samp_pad[:, :, :, SF:]))
                low(Z_U + 2 * c + 4)
            lru_split(0)
            lru_split(1)
            low(PB_U + 3)
            for k in range(2):
                for b in range(4):
                    wait_part(dve, pb_mm, 4, k, b, PB_U + k)
                    i_ = dve.tensor_tensor(gate_b[:, 4 * k + b, :], gate_b[:, 4 * k + b, :], ps[:, 4 * (1 - k) + b, 0:T], ALU.mult)
                    i_.then_inc(pb_read, 1)
                low(PB_U + 4 + k)
            for k in range(2):
                for b in range(4):
                    c = 4 * k + b
                    wait_part(dve, pa_mm, 4, k, b, PA_U + 2 * k + 1)
                    link(dve.tensor_tensor(gate_a[:, c, :], gate_a[:, c, :], ps[:, 4 * (1 - k) + b, 0:T], ALU.mult))
                    if c == 0:
                        dve.wait_ge(pb_read, CB)
                    link(dve.tensor_tensor(gate_a[:, c, :], gate_a[:, c, :], gate_b[:, c, :], ALU.add))
                    link(dve.tensor_copy(mrg_h[:, c, :], gate_a[:, c, :]))
                    dve.tensor_tensor(mrg_l[:, c, :], gate_a[:, c, :], mrg_h[:, c, :].bitcast(F32), ALU.subtract).then_inc(mrg_ready, 1)
                low(PB_U + 6 + 2 * k)
                low(PB_U + 7 + 2 * k)
            dve.wait_ge(bias_loaded, 32)
            link(dve.tensor_copy(bias_hl[:], bias_raw[:]))
            dve.tensor_tensor(bias_hl[NE:2 * NE, :], bias_raw[NE:2 * NE, :], bias_hl[NE:2 * NE, :].bitcast(F32), ALU.subtract)
            dve.wait_ge(y_loaded, 48)
            for k in range(2):
                for t in range(TT):
                    wait_part(dve, wo_mm, TT, k, t, WO_U + 2 * k + 1)
                    dve.tensor_tensor(y[:, t, UC * k:UC * k + UC], y[:, t, UC * k:UC * k + UC], ps[:, 4 * (1 - k) + t, :],
                                      ALU.add).then_inc(y_ready, 1)
                if k == 0:
                    for q in range(2):
                        dve.wait_ge(st_turned, q + 1)
                        i_ = dve.tensor_copy(state_out[:, 512 * q:512 * q + 512], ps[0:36, 4 * q + 3, :])
                    i_.then_inc(st_ready, 1)
                    dve.wait_ge(late_loaded, 6 * 16)
                    link(dve.tensor_copy(bdn_hl[:], bdn[:]))
                    link(dve.tensor_tensor(bdn_hl[NE:2 * NE, :], bdn[NE:2 * NE, :], bdn_hl[NE:2 * NE, :].bitcast(F32), ALU.subtract))
            dve.wait_ge(sq2, 2 * TT)
            link(dve.tensor_tensor(rt[:, 0:TT], rt[:, 48:48 + TT], rt[:, 48 + TT:48 + 2 * TT], ALU.add))
            link(dve.tensor_scalar(rt[:, 4:4 + TT], rt[:, 0:TT], 1.0 / D, RMS_EPS, ALU.mult, ALU.add))
            dve.reciprocal(rt[:, 4:4 + TT], rt[:, 4:4 + TT]).then_inc(r2_in, 1)
            dve.wait_ge(r2_out, 1)
            for t in range(TT):
                dve.scalar_tensor_tensor(out=xn2[:, t, :], in0=y[:, t, :], scalar=rt[:, 8 + t:9 + t], in1=n2b[:],
                                         op0=ALU.mult, op1=ALU.mult).then_inc(xn2_ready, 1)
            for t in range(TT):
                dve.wait_ge(xn2_high, t + 1)
                i_ = dve.tensor_tensor(xn_l[:, t, :], xn2[:, t, :], xn_h[:, t, :].bitcast(F32), ALU.subtract)
            i_.then_inc(xn2_low, 1)
            dve.wait_ge(logits_mm, 1)
            link(dve.tensor_tensor(lg[:], ps[:, 6, 0:TT * NE].rearrange("p (t e) -> p t e", e=NE),
                                   brb[:].unsqueeze(1).broadcast_to([P, TT, NE]), ALU.add))
            for t in range(TT):
                i_ = dve.max(mx[:, t, :], lg[:, t, :])
            link(i_)
            dve.tensor_scalar(rt[:, 16:16 + TT], mx[:, :, 0], -1.0, None, ALU.mult).then_inc(top_ready, 1)
            for t in range(TT):
                i_ = dve.max_index(ix[:, t, :], mx[:, t, :], lg[:, t, :])
            link(i_)
            link(dve.tensor_copy(ixf[:], ix[:]))
            for t in range(TT):
                i_ = dve.tensor_tensor(oh[:, t], iota_s[:, 0:NE].unsqueeze(1).broadcast_to([P, TOPK, NE]),
                                       ixf[:, t, 0:TOPK].unsqueeze(2).broadcast_to([P, TOPK, NE]), ALU.is_equal)
            link(i_)
            link(dve.tensor_reduce(maskf[:], oh[:].rearrange("p t k e -> p t e k"), AX_X, ALU.add))
            dve.tensor_copy(mask[:], maskf[:]).then_inc(mask_ready, 1)
            dve.wait_ge(top_exp, 1)
            link(dve.reciprocal(rt[:, 24:24 + TT], rt[:, 20:20 + TT]))
            link(dve.tensor_tensor(ex[:, :, 0:TOPK], ex[:, :, 0:TOPK], rt[:, 24:24 + TT].unsqueeze(2).broadcast_to([P, TT, TOPK]), ALU.mult))
            link(dve.tensor_tensor(oh[:], oh[:], ex[:, :, 0:TOPK].unsqueeze(3).broadcast_to([P, TT, TOPK, NE]), ALU.mult))
            link(dve.tensor_reduce(gat[:], oh[:].rearrange("p t k e -> p t e k"), AX_X, ALU.add))
            link(dve.tensor_copy(gat3[:], gat[:].unsqueeze(2).broadcast_to([P, TT, 3, NE])))
            link(dve.tensor_scalar(maskf[:], maskf[:], FAR, -FAR, ALU.mult, ALU.add))
            dve.wait_ge(pos_mm, 1)
            dve.tensor_tensor(pos[:], maskf[:], ps[:, 7, 0:TT * NE].rearrange("p (t e) -> p t e", e=NE), ALU.add).then_inc(pos_ready, 1)
            dve.wait_ge(post_mm, 1)
            dve.tensor_copy(post[:], ps[0:NE, 5, 0:T])
            link(dve.tensor_copy(gat_t[:], ps[0:3 * NE, 4, 0:T]))
            dve.tensor_tensor(gat_t[2 * NE:3 * NE, :], ps[2 * NE:3 * NE, 4, 0:T], gat_t[2 * NE:3 * NE, :].bitcast(F32),
                              ALU.subtract).then_inc(gat_ready, 1)
            dve.memset(pick_t[:, 1].bitcast(F32), 0.0).then_inc(pick_t_ready, 1)
            link(dve.tensor_reduce(cnt[0:1, 0:1], ps[0:1, 7, TT * NE:(TT + 1) * NE], AX_X, ALU.max))
            link(dve.tensor_scalar(cnt[0:1, 1:2], cnt[0:1, 0:1], float(P), 1.0, ALU.is_gt, ALU.add))
            link(dve.tensor_scalar(cnt[0:1, 2:3], cnt[0:1, 0:1], 2.0 * P, None, ALU.is_gt))
            link(dve.tensor_tensor(cnt[0:1, 3:4], cnt[0:1, 1:2], cnt[0:1, 2:3], ALU.add))
            link(dve.tensor_copy(cnt_i[0:1, 0:1], cnt[0:1, 3:4]))
            dve.wait_ge(gat_ready, 1)
            dve.wait_ge(pos_ready, 1)
            for t in range(TT):
                dve.wait_ge(bd_mm, t + 1)
                i_ = dve.tensor_tensor(y[:, t, :], y[:, t, :], ps[:, 2 * t:2 * t + 2, :].rearrange("p a b -> p (a b)"), ALU.add)
            i_.then_inc(route_ready, 1)
            dve.wait_ge(route_ready, 1)

            def out_low_part(it, x):
                dve.wait_ge(out_high, it + 1)
                dve.scalar_tensor_tensor(out=out_l[x][:], in0=ps[:, 4:6, :].rearrange("p a b -> p (a b)"), scalar=gslot[:, 0:1],
                                         in1=out_h[x][:].bitcast(F32), op0=ALU.mult, op1=ALU.subtract).then_inc(out_ready, 1)

            def add_to_tokens(p_, i):
                t, bank = COMBINE_BANKS[i]
                dve.wait_ge(combined, p_ * TT + (i + 1))
                dve.tensor_tensor(y[:, t, :], y[:, t, :], ps[:, bank:bank + 2, :].rearrange("p a b -> p (a b)"),
                                  ALU.add).then_inc(y_added, 1)

            def expert(p_, x):
                it = p_ * 2 + x

                def low(m):
                    dve.wait_ge(high_done, it * EXP_U + (MIX_U + m + 1))
                    dve.tensor_tensor(split_l[:, m % SPLIT_RING], raw[:, m % RAW_RING],
                                      split_h[:, m % SPLIT_RING].bitcast(F32), ALU.subtract).then_inc(low_done, 1)

                def clip(j):
                    gate_bank = (2, 0)[j]
                    dve.wait_ge(unit_used, it * EXP_U + (MIX_U + 4 * (j + 1)))
                    dve.tensor_scalar(g1[:], ps[:, gate_bank, :], LIMIT, None, ALU.min).then_inc(clipped, 1)
                    dve.tensor_scalar(u1[:], ps[:, gate_bank + 1, :], LIMIT, -LIMIT, ALU.min, ALU.max).then_inc(up_clipped, 1)

                def product(j):
                    dve.wait_ge(up_clipped, it * 2 + (j + 1))
                    dve.wait_ge(silu_done, it * 2 + (j + 1))
                    dve.scalar_tensor_tensor(out=actv[:, UC * j:UC * j + UC], in0=u1[:], scalar=1.0, in1=sil[:],
                                             op0=ALU.add, op1=ALU.mult).then_inc(act_ready, 1)

                def turned_low(j):
                    dve.wait_ge(at_high, it * 2 + (j + 1))
                    dve.tensor_tensor(at_l[:, 4 * j:4 * j + 4, :].rearrange("p c s -> p (c s)"), ps[:, 6 + j, :],
                                      at_h[:, 4 * j:4 * j + 4, :].rearrange("p c s -> p (c s)").bitcast(F32),
                                      ALU.subtract).then_inc(at_ready, 1)

                low(0)
                low(1)
                if x == 0:
                    low(2)
                    for k in range(2):
                        bank = GATHER_BANKS[2 + k]
                        dve.wait_ge(gathered, p_ * 4 + (k + 3))
                        dve.tensor_copy(xt_l[:, 4 * k:4 * k + 4].rearrange("p c x s -> p (c x s)"),
                                        ps[:, bank:bank + 2, :].rearrange("p a b -> p (a b)")).then_inc(xt_low_ready, 1)
                    low(3)
                    out_low_part(it, 1 - x)
                else:
                    out_low_part(it, 1 - x)
                    add_to_tokens(p_, 0)
                    low(2)
                    add_to_tokens(p_, 1)
                    low(3)
                    add_to_tokens(p_, 2)
                for m in range(4, 7):
                    low(m)
                clip(0)
                product(0)
                low(7)
                low(8)
                turned_low(0)
                low(9)
                clip(1)
                product(1)
                low(10)
                turned_low(1)
                low(11)
                dve.wait_ge(sel_used, it + 2)
                dve.tensor_scalar(pick_t[:, x], ps[:, 2, 0:T], slot_p[:, 0:1], None, ALU.is_equal).then_inc(pick_t_ready, 1)

            with dve.Fori(0, NE // 2) as g:
                for x in range(2):
                    expert(g, x)
            rounds = dve.value_load(cnt_i[0:1, 0:1], min_val=1, max_val=TT)
            with dve.Fori(1, TT) as r:
                with dve.If(r < rounds):
                    with dve.Fori(0, NE // 2) as g:
                        for x in range(2):
                            expert(r * (NE // 2) + g, x)
                dve.nop()
            out_low_part(rounds * NE, 1)
            for i in range(TT):
                add_to_tokens(rounds * (NE // 2), i)
            dve.wait_ge(sq3, TT)
            dve.tensor_scalar(rt[:, 36:36 + TT], rt[:, 32:32 + TT], 1.0 / D, RMS_EPS, ALU.mult, ALU.add).then_inc(r3_mean, 1)
            dve.wait_ge(r3_mean, 1)
            dve.reciprocal(rt[:, 36:36 + TT], rt[:, 36:36 + TT]).then_inc(r3_in, 1)
            dve.wait_ge(r3_out, 1)
            dve.wait_ge(fnb_loaded, 16)
            for t in range(TT):
                dve.scalar_tensor_tensor(out=y[:, t, :], in0=y[:, t, :], scalar=rt[:, 40 + t:41 + t], in1=fnb[:],
                                         op0=ALU.mult, op1=ALU.mult).then_inc(out_final, 1)

        @block.tensor
        def _(pe):
            def three(out, a_h, a_l, b_h, b_l, start, stop):
                pe.matmul(out, a_h, b_h, start=start, stop=False)
                pe.matmul(out, a_h, b_l, start=False, stop=False)
                return pe.matmul(out, a_l, b_h, start=False, stop=stop)

            pe.wait_ge(const_ready, 1)
            pe.wait_ge(rows_loaded, 8 * 16)
            pe.transpose(ps[:, 0, 0:ROWS], rows[:], ident[0:ROWS, 0:ROWS])
            for c in range(CB):
                i_ = pe.transpose(ps[:, 1, 32 * c:32 * c + 32], state_in[:, c * P:(c + 1) * P], ident[0:32, 0:32])
            i_.then_inc(rows_turned, 1)
            for c in range(CB):
                if c == 0:
                    pe.wait_ge(rows_copied, 1)
                    pe.wait_ge(xs_ready, TT)
                if c == 4:
                    pe.wait_ge(ws_loaded, 16 * (1 + ST))
                    for k in range(2):
                        for g in range(MG):
                            i_ = pe.transpose(ps[:, 6 + k, g * P:(g + 1) * P], ws_raw[:, k, g, :], ident[:])
                        i_.then_inc(ws_turned, 1)
                if c == 6:
                    pe.wait_ge(ws_ready, 2)
                for t in range(TT):
                    i_ = pe.transpose(ps[:, c, t * P:(t + 1) * P], xs[:, t, c * P:(c + 1) * P], ident[:])
                i_.then_inc(xs_turned, 1)
            def channel_unit(slot, k_blocks, bank, act_hl, start, stop, ready=None, before=None):
                x_h, x_l = act_hl
                for b in range(4):
                    if before:
                        before(b)
                    for j in range(KB):
                        cols_ = slice(b * P, (b + 1) * P)
                        i_ = three(ps[:, bank + b, 0:T], split_h[:, slot, j, cols_], split_l[:, slot, j, cols_],
                                   x_h[:, k_blocks + j, :], x_l[:, k_blocks + j, :], start and j == 0, stop and j == KB - 1)
                    if b == 3:
                        i_.then_inc(unit_used, 1)
                    elif ready:
                        i_.then_inc(ready, 1)

            for h in range(2):
                pe.wait_ge(xn_ready, 4 * (h + 1))
                pe.wait_ge(low_done, h + 1)
                for t in range(TT):
                    for j in range(KB):
                        ts_ = slice(t * P, (t + 1) * P)
                        i_ = three(ps[:, t, :], act_h[:, KB * h + j, ts_], act_l[:, KB * h + j, ts_],
                                   split_h[:, h, j, :], split_l[:, h, j, :], h == 0 and j == 0, h == 1 and j == KB - 1)
                    if t == TT - 1:
                        i_.then_inc(unit_used, 1)
                    elif h:
                        i_.then_inc(v_mm, 1)

            def z_chunk(c, c_in_group, low_needed, bank_wait):
                for h in range(2):
                    pe.wait_ge(low_done, low_needed + (h + 1))
                    channel_unit((Z_U + 2 * c_in_group + h) % MIX_SPLIT, KB * h, 4 * (c_in_group % 2), (act_h, act_l), h == 0, h == 1,
                                 z_ready if h else None, bank_wait if h == 0 else None)

            with pe.Fori(0, 2) as g:
                def first_free(b):
                    pe.wait_ge(v_read, min(b + 1, TT))
                    pe.wait_ge(z_evac, g * 12 + (b + 1))

                z_chunk(0, 0, g * 6 + Z_U, first_free)
                z_chunk(1, 1, g * 6 + (Z_U + 2), None)
                z_chunk(2, 2, g * 6 + (Z_U + 4), lambda b: pe.wait_ge(z_evac, g * 12 + (b + 5)))

            def lru_gates(hf):
                for k in range(2):
                    if hf == 0:
                        pe.wait_ge(z_evac, 4 * (6 + k))
                    elif k == 0:
                        pe.wait_ge(vmix_read, 1)
                    else:
                        pe.wait_ge(z_evac, 4 * 8)
                    for b in range(4):
                        i_ = pe.matmul(ps[:, 4 * (1 - k) + b, 0:T], lruw[:, k, 4 * hf + b, :], xc[:, 4 * hf + b, :], start=True, stop=True)
                    i_.then_inc(gates_mm, 1)

            pe.wait_ge(conv_done, 1)
            pe.wait_ge(lruw_loaded, 64)
            lru_gates(0)
            pe.wait_ge(v_ready, 1)
            pe.wait_ge(const_ready, 4)
            pe.wait_ge(gates_read, 1)
            for g in range(MG):
                for t in range(TT):
                    i_ = pe.matmul(ps[:, 4 + g, t * P:(t + 1) * P], v[:, t, g * P:(g + 1) * P], wst[:, t // 2, g, :], start=True, stop=True)
                i_.then_inc(vmix_mm, 1)
            z_chunk(6, 0, 12 + Z_U, lambda b: pe.wait_ge(gates_read, 2))
            lru_gates(1)
            z_chunk(7, 1, 14 + Z_U, lambda b: pe.wait_ge(gates_read, 3))
            z_chunk(8, 2, 16 + Z_U, lambda b: pe.wait_ge(gates_read, 4))
            pe.wait_ge(yb_ready, 1)
            for k in range(2):
                pe.wait_ge(low_done, PB_U + k + 1)
                pe.wait_ge(z_evac, 4 * (9 + k))
                channel_unit((PB_U + k) % MIX_SPLIT, 0, 4 * (1 - k), (yb_h, yb_l), True, True, pb_mm)
            for k in range(2):
                for h in range(2):
                    n = PA_U + 2 * k + h
                    pe.wait_ge(lru_ready, h + 1)
                    pe.wait_ge(low_done, n + 1)
                    channel_unit(n % MIX_SPLIT, KB * h, 4 * (1 - k), (act_h, act_l), h == 0, h == 1, pa_mm if h else None,
                                 (lambda b: pe.wait_ge(pb_read, 4 * k + b + 1)) if h == 0 else None)
            for k in range(2):
                for h in range(2):
                    n = WO_U + 2 * k + h
                    pe.wait_ge(low_done, n + 1)
                    pe.wait_ge(mrg_ready, 4 * (h + 1))
                    for t in range(TT):
                        for j in range(KB):
                            ts_ = slice(t * P, (t + 1) * P)
                            i_ = three(ps[:, 4 * (1 - k) + t, :], mrg_h[:, KB * h + j, ts_], mrg_l[:, KB * h + j, ts_],
                                       split_h[:, n % MIX_SPLIT, j, :], split_l[:, n % MIX_SPLIT, j, :],
                                       h == 0 and j == 0, h == 1 and j == KB - 1)
                        if t == TT - 1:
                            i_.then_inc(unit_used, 1)
                        elif h:
                            i_.then_inc(wo_mm, 1)
                if k == 0:
                    pe.wait_ge(st_packed, 2)
                    for c in range(CB):
                        i_ = pe.transpose(ps[0:36, 4 * (c // 4) + 3, (c % 4) * P:(c % 4 + 1) * P], pack[:, c, :], ident[:])
                        if c % 4 == 3:
                            i_.then_inc(st_turned, 1)
            pe.wait_ge(y_ready, 2 * TT)
            for t in range(TT):
                pe.wait_ge(xn2_ready, t + 1)
                for c in range(CB):
                    i_ = pe.transpose(ps[:, 2 * t + c // 4, (c % 4) * P:(c % 4 + 1) * P], xn2[:, t, c * P:(c + 1) * P], ident[:])
                    if c % 4 == 3:
                        i_.then_inc(xn2_turned, 1)
            for t in range(TT):
                pe.wait_ge(xnt_ready, 2 * (t + 1))
                for c in range(CB):
                    i_ = pe.matmul(ps[:, 6, t * NE:(t + 1) * NE], xnt[:, c, t * P:(t + 1) * P], wr[:, c, :], start=c == 0, stop=c == CB - 1)
            i_.then_inc(logits_mm, 1)
            pe.wait_ge(mask_ready, 1)
            pe.wait_ge(st_ready, 1)
            for t in range(TT):
                for s_ in range(t + 1):
                    pe.matmul(ps[:, 7, t * NE:(t + 1) * NE], tri[:] if s_ == t else ones_b[:], mask[:, s_, :], start=s_ == 0, stop=s_ == t)
            for t in range(TT):
                i_ = pe.matmul(ps[:, 7, TT * NE:(TT + 1) * NE], ones_b[:], mask[:, t, :], start=t == 0, stop=t == TT - 1)
            i_.then_inc(pos_mm, 1)
            pe.wait_ge(pos_ready, 1)
            for t in range(TT):
                j_ = pe.transpose(ps[0:NE, 5, t * P:(t + 1) * P], pos[:, t, :], ident[:])
                if t < 2:
                    j_.then_inc((pick_used, sel_used)[t], 1)
                i_ = pe.transpose(ps[0:3 * NE, 4, t * P:(t + 1) * P], gat3[:, t].rearrange("p k e -> p (k e)"), ident[:])
            i_.then_inc(post_mm, 1)
            pe.wait_ge(gat_ready, 1)
            for t in range(TT):
                for k in range(2):
                    i_ = pe.matmul(ps[:, 2 * t + k, :], gat_t[:, t * P:(t + 1) * P], bdn_hl[:, UC * k:UC * k + UC], start=True, stop=True)
                i_.then_inc(bd_mm, 1)
            pe.wait_ge(route_ready, 1)
            pe.wait_ge(pick_t_ready, 1)
            pe.wait_ge(xn2_high, TT)
            pe.wait_ge(xn2_low, 1)
            pe.matmul(ps[:, 4, :], pick_t[:, 1, 0:P], xn_h[:, 0, 0:UC], start=True, stop=True)
            pe.matmul(ps[:, 5, :], pick_t[:, 1, 0:P], xn_h[:, 0, 0:UC], start=True, stop=True).then_inc(zeros_ready, 1)

            def combine(t, bank, x, start, stop):
                for k in range(2):
                    pe.matmul(ps[:, bank + k, :], pick_t[:, x, t * P:(t + 1) * P], out_h[x][:, UC * k:UC * k + UC], start=start, stop=False)
                    i_ = pe.matmul(ps[:, bank + k, :], pick_t[:, x, t * P:(t + 1) * P], out_l[x][:, UC * k:UC * k + UC], start=False, stop=stop)
                return i_

            def gather(p_):
                pe.wait_ge(pick_ready, p_ + 1)
                for k in range(4):
                    if k == 1:
                        pe.wait_ge(pick_t_ready, p_ * 2 + 1)
                        pe.wait_ge(gslot_ready, p_ * 2 + 1)
                    if k == 3:
                        pe.wait_ge(xt_ready, p_ * 2 + 1)
                    for c in range(4):
                        for t in range(TT):
                            c_ = 4 * (k % 2) + c
                            i_ = pe.matmul(ps[:, GATHER_BANKS[k] + c // 2, c % 2 * 2 * P:(c % 2 + 1) * 2 * P],
                                           (xn_h, xn_l)[k // 2][:, t, c_ * P:(c_ + 1) * P],
                                           pick[:, t].rearrange("p x s -> p (x s)"), start=t == 0, stop=t == TT - 1)
                    i_.then_inc(gathered, 1)

            def expert(p_, x, e):
                it = p_ * 2 + x

                def unit(m, bank, x_h, x_l, first, last, midway=None):
                    pe.wait_ge(low_done, it * EXP_U + (MIX_U + m + 1))
                    k0 = KB * (m % 2 if m < 8 else (m - 8) // 2)
                    for j in range(KB):
                        if midway and j == KB // 2:
                            midway()
                        i_ = three(ps[:, bank, :], x_h[:, k0 + j, :], x_l[:, k0 + j, :], split_h[:, m % SPLIT_RING, j, :],
                                   split_l[:, m % SPLIT_RING, j, :], first and j == 0, last and j == KB - 1)
                    i_.then_inc(unit_used, 1)

                def linear(m, bank, bias_col):
                    if x == 0 and m == 0:
                        pe.wait_ge(xt_ready, p_ * 2 + 2)
                    pe.matmul(ps[:, bank, :], sel[:], bias_hl[:, bias_col:bias_col + UC], start=True, stop=False)
                    if x == 0 and m == 0:
                        pe.wait_ge(xt_low_ready, p_ * 2 + 1)
                    unit(m, bank, xt_h[:, :, x], xt_l[:, :, x], False, False)
                    if x == 0 and m == 0:
                        pe.wait_ge(xt_low_ready, p_ * 2 + 2)
                    unit(m + 1, bank, xt_h[:, :, x], xt_l[:, :, x], False, True)

                def turn(j):
                    pe.wait_ge(act_ready, it * 2 + (j + 1))
                    for c in range(4):
                        i_ = pe.transpose(ps[:, 6 + j, c * P:(c + 1) * P], actv[:, UC * j + c * P:UC * j + (c + 1) * P], ident[:])
                    i_.then_inc(act_turned, 1)

                if x == 0:
                    gather(p_)
                else:
                    pe.wait_ge(out_ready, p_ * 2 + 1)
                    pe.wait_ge(pick_t_ready, p_ * 2 + 2)
                    pe.wait_ge(gslot_ready, p_ * 2 + 2)
                    for t, bank in COMBINE_BANKS[::-1]:
                        combine(t, bank, 1, True, False)
                    pe.wait_ge(out_ready, p_ * 2 + 2)
                    for t, bank in COMBINE_BANKS:
                        combine(t, bank, 0, False, True).then_inc(combined, 1)
                    pe.wait_ge(y_added, p_ * TT + 1)
                pe.wait_ge(sel_ready, it + 1)
                linear(0, 2, 0)
                linear(2, 3, D)
                if x == 1:
                    pe.wait_ge(y_added, p_ * TT + 2)
                linear(4, 0, UC)
                if x == 1:
                    pe.wait_ge(y_added, p_ * TT + 3)
                turn(0)
                linear(6, 1, D + UC)
                pe.matmul(ps[:, 2, 0:T], sel[0:NE, :], post[:], start=True, stop=True).then_inc(sel_used, 1)
                for t in range(TT):
                    i_ = pe.matmul(ps[:, 3, 0:1], pick[:, t, x, :].bitcast(F32), gat[:, t, bass.ds(e, 1)], start=t == 0, stop=t == TT - 1)
                i_.then_inc(pick_used, 1)
                pe.wait_ge(at_ready, it * 2 + 1)
                unit(8, 4, at_h, at_l, True, False)
                unit(9, 5, at_h, at_l, True, False, lambda: turn(1))
                pe.wait_ge(at_ready, it * 2 + 2)
                unit(10, 4, at_h, at_l, False, True)
                unit(11, 5, at_h, at_l, False, True)

            with pe.Fori(0, NE // 2) as g:
                for x in range(2):
                    expert(g, x, g * 2 + x)
            rounds = pe.value_load(cnt_i[0:1, 0:1], min_val=1, max_val=TT)
            with pe.Fori(1, TT) as r:
                with pe.If(r < rounds):
                    with pe.Fori(0, NE // 2) as g:
                        for x in range(2):
                            expert(r * (NE // 2) + g, x, g * 2 + x)
                pe.nop()
            pe.wait_ge(out_ready, rounds * NE + 1)
            pe.wait_ge(pick_t_ready, rounds * NE + 1)
            pe.wait_ge(gslot_ready, rounds * NE + 1)
            for t, bank in COMBINE_BANKS:
                combine(t, bank, 1, True, True).then_inc(combined, 1)


_INS = ['x_prompt', 'x_sample', 'state_conv', 'state_h', 'norm1_g', 'w_in', 'conv_w', 'conv_b', 'w_rg', 'b_rg',
        'w_ig', 'b_ig', 'lru_lambda', 'ln_v_g', 'ln_v_b', 'w_s', 'b_s', 'w_proj_a', 'w_proj_b', 'w_out', 'norm2_g',
        'w_router', 'b_router', 'w_gate_up', 'b_gate_up', 'w_down', 'b_down', 'final_norm_g']
_OUTS = [((1, SEQ, D), 'float32'), ((ST, SF, D), 'float32'), ((1, 1, CW - 1, D), 'float32'), ((1, 1, D), 'float32'),
         ((1, ST, CW - 1, D), 'float32'), ((1, ST, D), 'float32'), ((1, ST, SF, DM), 'float32')]


def kernel(**inputs):
    import numpy as _np
    import concourse.bacc as _bacc
    from concourse import mybir as _mybir
    from concourse.bass_utils import run_bass_kernel_spmd as _run

    nc = _bacc.Bacc("TRN2", target_bir_lowering=False, num_devices=1)
    arrays, args = {}, []
    for name in _INS:
        a = _np.ascontiguousarray(inputs[name])
        arrays[f"in_{name}_dram"] = a
        args.append(nc.dram_tensor(f"in_{name}_dram", a.shape, _mybir.dt.from_np(a.dtype), kind="ExternalInput").ap())
    for i, (shape, dtype) in enumerate(_OUTS):
        dt = _mybir.dt.from_np(_np.dtype(dtype))
        args.append(nc.dram_tensor(f"out_{i}_dram", shape, dt, kind="ExternalOutput").ap())
    hawk_gmlp_moe_streaming_step(nc, *args)
    r = _run(nc, [arrays], core_ids=[0])
    return tuple(r.results[0][f"out_{i}_dram"] for i in range(len(_OUTS)))
```
